# Optimizing a Trainium2 kernel written in Bass

```python
import jax, jax.numpy as jnp
from jax import lax
import numpy as np

D_MODEL = 1024
BATCH = 1
SEQ = 1024
DEPTH = 2
DEC_BATCH = 8
DEC_SEQ = 1
PAST_LEN = 256
PAGE_SIZE = 128

N_LAYERS_A = DEPTH // 2
N_LAYERS_B = DEPTH - N_LAYERS_A
HEADS_A = 8
DK_A = 128
DV_A = 128
KEY_W_A = HEADS_A * DK_A
VAL_W_A = HEADS_A * DV_A
QKV_W_A = 2 * KEY_W_A + VAL_W_A
PROJ_W_A = QKV_W_A + VAL_W_A + 2 * HEADS_A
CONV_W = 4
GDN_CHUNK = 64
BRANCH_WINDOWS = (128, 512, 2048)
BRANCH_DILATIONS = (1, 4, 16)
N_BRANCH = 3
HEADS_B = 8
KV_HEADS_B = 2
GQA_B = HEADS_B // KV_HEADS_B
HEAD_DIM_B = 64
Q_W_B = N_BRANCH * HEADS_B * HEAD_DIM_B
KV_W_B = N_BRANCH * 2 * KV_HEADS_B * HEAD_DIM_B
OUT_W_B = HEADS_B * HEAD_DIM_B
Q_BLOCK = 128
D_FF = 4 * D_MODEL
EPS = 1e-6

kernel_name = 'yoco_gdn_dilated_alibi_decoder_step'

def rmsnorm(x, gain):
    xf = x.astype(jnp.float32)
    y = xf * lax.rsqrt(jnp.mean(xf * xf, axis=-1, keepdims=True) + EPS)
    return (y * gain.astype(jnp.float32)).astype(x.dtype)

def l2norm(x):
    return x * lax.rsqrt(jnp.sum(x * x, axis=-1, keepdims=True) + EPS)

def sq_relu_mlp(h, w_up, w_down):
    u = jax.nn.relu(h @ w_up)
    return (u * u) @ w_down

def alibi_slopes():
    return jnp.exp2(-8.0 * jnp.arange(1, HEADS_B + 1, dtype=jnp.float32) / HEADS_B)

def gated_delta_rule(q, k, v, g, beta, s0):
    N, L, H, _ = q.shape
    C = GDN_CHUNK
    n_chunks = -(-L // C)
    pad = n_chunks * C - L

    def to_chunks(t):
        t = jnp.pad(t.astype(jnp.float32), [(0, 0), (0, pad)] + [(0, 0)] * (t.ndim - 2))
        t = t.reshape((N, n_chunks, C) + t.shape[2:])
        return t.transpose((1, 0, 3, 2) + tuple(range(4, t.ndim)))

    qc, kc, vc, gc, bc = (to_chunks(t) for t in (q, k, v, g, beta))
    G = jnp.cumsum(gc, axis=-1)
    causal = jnp.tril(jnp.ones((C, C), dtype=bool))
    strict = jnp.tril(jnp.ones((C, C), dtype=bool), -1)
    diff = G[..., :, None] - G[..., None, :]
    decay = jnp.where(causal, jnp.exp(jnp.where(causal, diff, 0.0)), 0.0)
    kb = kc * bc[..., None]
    lower = jnp.where(strict, jnp.einsum('...ik,...jk->...ij', kb, kc) * decay, 0.0)
    eye = jnp.broadcast_to(jnp.eye(C, dtype=jnp.float32), lower.shape)
    T = lax.linalg.triangular_solve(eye + lower, eye, left_side=True, lower=True, unit_diagonal=True)
    u = jnp.einsum('...ij,...jv->...iv', T, vc * bc[..., None])
    w = jnp.einsum('...ij,...jk->...ik', T, kb * jnp.exp(G)[..., None])
    attn = jnp.einsum('...ik,...jk->...ij', qc, kc) * decay
    q_dec = qc * jnp.exp(G)[..., None]
    G_last = G[..., -1]
    k_dec = kc * jnp.exp(G_last[..., None] - G)[..., None]
    decay_last = jnp.exp(G_last)

    def step(S, inp):
        u_c, w_c, qd_c, kd_c, a_c, dl_c = inp
        v_new = u_c - jnp.einsum('nhck,nhkv->nhcv', w_c, S)
        o_c = jnp.einsum('nhck,nhkv->nhcv', qd_c, S) + jnp.einsum('nhcj,nhjv->nhcv', a_c, v_new)
        S = S * dl_c[..., None, None] + jnp.einsum('nhck,nhcv->nhkv', kd_c, v_new)
        return S, o_c

    S_fin, o = lax.scan(step, s0.astype(jnp.float32), (u, w, q_dec, k_dec, attn, decay_last))
    o = o.transpose(1, 0, 3, 2, 4).reshape(N, n_chunks * C, H, DV_A)[:, :L]
    return o, S_fin

def gdn_mixer(h, s0, conv_buf, w_in, w_conv, a_log, dt_bias, g_norm, w_out):
    N, L, _ = h.shape
    proj = h @ w_in
    qkv = proj[..., :QKV_W_A]
    z = proj[..., QKV_W_A:QKV_W_A + VAL_W_A]
    b_raw = proj[..., QKV_W_A + VAL_W_A:QKV_W_A + VAL_W_A + HEADS_A]
    a_raw = proj[..., QKV_W_A + VAL_W_A + HEADS_A:]
    ext = jnp.concatenate([conv_buf.astype(qkv.dtype), qkv], axis=1)
    new_conv = ext[:, ext.shape[1] - (CONV_W - 1):]
    conv = sum(ext[:, j:j + L] * w_conv[j] for j in range(CONV_W))
    qkv_c = jax.nn.silu(conv.astype(jnp.float32))
    q = l2norm(qkv_c[..., :KEY_W_A].reshape(N, L, HEADS_A, DK_A)) * (DK_A ** -0.5)
    k = l2norm(qkv_c[..., KEY_W_A:2 * KEY_W_A].reshape(N, L, HEADS_A, DK_A))
    v = qkv_c[..., 2 * KEY_W_A:].reshape(N, L, HEADS_A, DV_A)
    beta = jax.nn.sigmoid(b_raw.astype(jnp.float32))
    g = -jnp.exp(a_log.astype(jnp.float32)) * jax.nn.softplus(a_raw.astype(jnp.float32) + dt_bias.astype(jnp.float32))
    o, s_new = gated_delta_rule(q, k, v, g, beta, s0)
    o = o * lax.rsqrt(jnp.mean(o * o, axis=-1, keepdims=True) + EPS) * g_norm.astype(jnp.float32)
    o = o * jax.nn.silu(z.astype(jnp.float32).reshape(N, L, HEADS_A, DV_A))
    out = o.reshape(N, L, VAL_W_A).astype(h.dtype) @ w_out
    return out, s_new.astype(s0.dtype), new_conv.astype(conv_buf.dtype)

def dilated_branch(q, k_ext, v_ext, q_start, window, dilation, slopes):
    N, Lq = q.shape[0], q.shape[1]
    qb = Q_BLOCK if Lq % Q_BLOCK == 0 else Lq
    nb = Lq // qb
    dist = jnp.arange(window // dilation + 1, dtype=jnp.int32) * dilation
    bias = -slopes[:, :, None] * dist.astype(jnp.float32)
    scale = HEAD_DIM_B ** -0.5

    def block(args):
        q_blk, start = args
        kidx = (start + jnp.arange(qb, dtype=jnp.int32))[:, None] - dist[None, :]
        valid = kidx >= 0
        kidx = jnp.maximum(kidx, 0)
        kg = jnp.take(k_ext, kidx, axis=1).astype(jnp.float32)
        vg = jnp.take(v_ext, kidx, axis=1).astype(jnp.float32)
        s = jnp.einsum('nqhgd,nqkhd->nqhgk', q_blk.astype(jnp.float32), kg) * scale + bias
        s = jnp.where(valid[None, :, None, None, :], s, -jnp.inf)
        m = jnp.max(s, axis=-1, keepdims=True)
        lse = m + jnp.log(jnp.sum(jnp.exp(s - m), axis=-1, keepdims=True))
        p = jnp.exp(s - lse)
        o = jnp.einsum('nqhgk,nqkhd->nqhgd', p, vg)
        return o, lse[..., 0]

    q_blocks = q.reshape((N, nb, qb) + q.shape[2:]).swapaxes(0, 1)
    starts = q_start + jnp.arange(nb, dtype=jnp.int32) * qb
    o, lse = lax.map(block, (q_blocks, starts))
    o = o.swapaxes(0, 1).reshape((N, Lq) + o.shape[3:])
    lse = lse.swapaxes(0, 1).reshape((N, Lq) + lse.shape[3:])
    return o, lse

def dilated_mixer(h, kv_exts, buf_lens, w_q, w_o):
    N, L, _ = h.shape
    q = (h @ w_q).reshape(N, L, N_BRANCH, KV_HEADS_B, GQA_B, HEAD_DIM_B)
    slopes = alibi_slopes().reshape(KV_HEADS_B, GQA_B)
    outs, lses = [], []
    for bi in range(N_BRANCH):
        o, lse = dilated_branch(q[:, :, bi], kv_exts[bi][:, :, 0], kv_exts[bi][:, :, 1], buf_lens[bi],
                                BRANCH_WINDOWS[bi], BRANCH_DILATIONS[bi], slopes)
        outs.append(o)
        lses.append(lse)
    wts = jax.nn.softmax(jnp.stack(lses), axis=0)
    out = jnp.sum(wts[..., None] * jnp.stack(outs), axis=0)
    return out.reshape(N, L, OUT_W_B).astype(h.dtype) @ w_o

def trunk(x, rec0, conv0, kv_bufs, w):
    N, L, _ = x.shape
    rec_new, conv_new, bufs_new, kv_exts = [], [], [], []
    buf_lens = [b.shape[1] for b in kv_bufs]
    for l in range(DEPTH):
        if l < N_LAYERS_A:
            mix, s_l, c_l = gdn_mixer(rmsnorm(x, w['norm_mix'][l]), rec0[l], conv0[l], w['w_in_a'][l],
                                      w['conv_a'][l], w['a_log'][l], w['dt_bias'][l], w['norm_o_a'][l],
                                      w['w_out_a'][l])
            rec_new.append(s_l)
            conv_new.append(c_l)
        else:
            if l == N_LAYERS_A:
                kv = (rmsnorm(x, w['norm_kv']) @ w['w_kv']).reshape(N, L, N_BRANCH, 2, KV_HEADS_B, HEAD_DIM_B)
                for bi in range(N_BRANCH):
                    e = jnp.concatenate([kv_bufs[bi].astype(kv.dtype), kv[:, :, bi]], axis=1)
                    kv_exts.append(e)
                    keep = min(BRANCH_WINDOWS[bi], e.shape[1])
                    bufs_new.append(e[:, e.shape[1] - keep:].astype(kv_bufs[bi].dtype))
            mix = dilated_mixer(rmsnorm(x, w['norm_mix'][l]), kv_exts, buf_lens,
                                w['w_q_b'][l - N_LAYERS_A], w['w_o_b'][l - N_LAYERS_A])
        x = x + mix
        x = x + sq_relu_mlp(rmsnorm(x, w['norm_mlp'][l]), w['w_up'][l], w['w_down'][l])
    y = rmsnorm(x, w['norm_final'])
    return y, jnp.stack(rec_new), jnp.stack(conv_new), bufs_new[0], bufs_new[1], bufs_new[2]

def setup_inputs(seed: int = 0) -> dict:
    key = jax.random.key(seed)
    ks = jax.random.split(key, 24)
    f32 = jnp.float32
    nrm = lambda k, shape, s: jax.random.normal(k, shape, f32) * s
    gain = lambda k, shape: 1.0 + 0.02 * jax.random.normal(k, shape, f32)
    dt = jnp.exp(jax.random.uniform(ks[5], (N_LAYERS_A, HEADS_A), f32, np.log(1e-3), np.log(1e-1)))
    return {
        'x_prompt': nrm(ks[0], (BATCH, SEQ, D_MODEL), 1.0),
        'x_sample': nrm(ks[1], (DEC_BATCH, DEC_SEQ, D_MODEL), 1.0),
        'state_a_rec': nrm(ks[2], (N_LAYERS_A, DEC_BATCH, HEADS_A, DK_A, DV_A), 0.1),
        'state_a_conv': nrm(ks[3], (N_LAYERS_A, DEC_BATCH, CONV_W - 1, QKV_W_A), 1.0),
        'cache_b0_kv': nrm(ks[4], (DEC_BATCH, min(BRANCH_WINDOWS[0], PAST_LEN), 2, KV_HEADS_B, HEAD_DIM_B), 1.0),
        'cache_b1_kv': nrm(ks[6], (DEC_BATCH, min(BRANCH_WINDOWS[1], PAST_LEN), 2, KV_HEADS_B, HEAD_DIM_B), 1.0),
        'cache_b2_kv': nrm(ks[7], (DEC_BATCH, min(BRANCH_WINDOWS[2], PAST_LEN), 2, KV_HEADS_B, HEAD_DIM_B), 1.0),
        'norm_mix': gain(ks[8], (DEPTH, D_MODEL)),
        'norm_mlp': gain(ks[9], (DEPTH, D_MODEL)),
        'w_in_a': nrm(ks[10], (N_LAYERS_A, D_MODEL, PROJ_W_A), D_MODEL ** -0.5),
        'conv_a': nrm(ks[11], (N_LAYERS_A, CONV_W, QKV_W_A), CONV_W ** -0.5),
        'a_log': jnp.log(jax.random.uniform(ks[12], (N_LAYERS_A, HEADS_A), f32, 1.0, 16.0)),
        'dt_bias': dt + jnp.log(-jnp.expm1(-dt)),
        'norm_o_a': gain(ks[13], (N_LAYERS_A, DV_A)),
        'w_out_a': nrm(ks[14], (N_LAYERS_A, VAL_W_A, D_MODEL), VAL_W_A ** -0.5),
        'norm_kv': gain(ks[15], (D_MODEL,)),
        'w_kv': nrm(ks[16], (D_MODEL, KV_W_B), D_MODEL ** -0.5),
        'w_q_b': nrm(ks[17], (N_LAYERS_B, D_MODEL, Q_W_B), D_MODEL ** -0.5),
        'w_o_b': nrm(ks[18], (N_LAYERS_B, OUT_W_B, D_MODEL), OUT_W_B ** -0.5),
        'w_up': nrm(ks[19], (DEPTH, D_MODEL, D_FF), D_MODEL ** -0.5),
        'w_down': nrm(ks[20], (DEPTH, D_FF, D_MODEL), D_FF ** -0.5),
        'norm_final': gain(ks[21], (D_MODEL,)),
    }

def reference(x_prompt, x_sample, state_a_rec, state_a_conv, cache_b0_kv, cache_b1_kv, cache_b2_kv,
              norm_mix, norm_mlp, w_in_a, conv_a, a_log, dt_bias, norm_o_a, w_out_a, norm_kv, w_kv,
              w_q_b, w_o_b, w_up, w_down, norm_final):
    w = {'norm_mix': norm_mix, 'norm_mlp': norm_mlp, 'w_in_a': w_in_a, 'conv_a': conv_a, 'a_log': a_log,
         'dt_bias': dt_bias, 'norm_o_a': norm_o_a, 'w_out_a': w_out_a, 'norm_kv': norm_kv, 'w_kv': w_kv,
         'w_q_b': w_q_b, 'w_o_b': w_o_b, 'w_up': w_up, 'w_down': w_down, 'norm_final': norm_final}
    p_rec0 = jnp.zeros((N_LAYERS_A, BATCH, HEADS_A, DK_A, DV_A), state_a_rec.dtype)
    p_conv0 = jnp.zeros((N_LAYERS_A, BATCH, CONV_W - 1, QKV_W_A), state_a_conv.dtype)
    p_bufs0 = [jnp.zeros((BATCH, 0, 2, KV_HEADS_B, HEAD_DIM_B), c.dtype) for c in (cache_b0_kv, cache_b1_kv, cache_b2_kv)]
    y_prompt, p_rec, p_conv, p_kv0, p_kv1, p_kv2 = trunk(x_prompt, p_rec0, p_conv0, p_bufs0, w)
    y_sample, s_rec, s_conv, s_kv0, s_kv1, s_kv2 = trunk(
        x_sample, state_a_rec, state_a_conv, [cache_b0_kv, cache_b1_kv, cache_b2_kv], w)
    return (y_prompt, y_sample, p_rec, p_conv, p_kv0, p_kv1, p_kv2, s_rec, s_conv, s_kv0, s_kv1, s_kv2)


_drawn_inputs = setup_inputs


def setup_inputs(seed=0):
    import zlib

    import numpy as np

    out = dict(_drawn_inputs(seed))
    spreads = {}
    factors = {'norm_o_a': 4.694, 'norm_kv': 22.384, 'norm_final': 20.314, 'norm_mlp': 3.748}
    for name, (base, spread) in spreads.items():
        noise = np.random.default_rng([zlib.crc32(name.encode()), seed]).standard_normal(out[name].shape)
        drawn = base * np.exp(spread * noise) if base else spread * noise
        out[name] = __import__('jax').numpy.asarray(drawn.astype(out[name].dtype))
    for name, factor in factors.items():
        out[name] = (out[name] * factor).astype(out[name].dtype)
    return out
```

```python
from contextlib import ExitStack, contextmanager

import numpy as np

import concourse.bass as bass
from concourse import mybir

F32 = mybir.dt.float32
F32R = mybir.dt.float32r
BF16 = mybir.dt.bfloat16
ALU = mybir.AluOpType
ACT = mybir.ActivationFunctionType
AXX = mybir.AxisListType.X

P = 128
D_MODEL = 1024
SEQ = 1024
NS = 8
HEADS = 8
D_FF = 4096
EPS = 1e-6
KT = D_MODEL // P
CH = SEQ // P
HALF = 512
HD = 64
OW = 8 * HD + 16
SA = 128
SB = 64 + 1 + 16 + 1 + 1
SK = SA + SB
BRANCH = 3
DIL = (1, 4, 16)
CACHE = (128, 64, 16)
NEG = -1.0e30
UW = 4
RING = 4
LEVELS = 6

U_IN, U_OUT = 0, 16
U_MLP0, U_KVQ = 20, 52
U_WO, U_MLP1 = 62, 64
UNITS = 96
CREDIT = {"raw_free": 2, "product_free": 2, "sample_free": 1, "square_free": 2,
          "head_squares_free": 1, "o_raw_free": 2, "q_tile_free": 2, "merge_free": 2,
          "out0_stored": 32, "out1_stored": 32, "out_taken": 1,
          **{f"bank{b}_free": 1 for b in range(8)}}


PER = {
    "weights": {"raw_free": 2, "raw0_landed": 16, "raw1_landed": 16},
    "act heads": {"bank3_full": 54, "bank3_free": 54, "bank4_full": 38, "bank4_free": 38, "bank5_full": 36,
        "bank5_free": 36, "raw0_landed": 64, "weight_half_hi": 8, "raw1_landed": 64, "act_order": 6,
        "bank6_full": 32, "bank6_free": 32, "bank7_full": 34, "bank7_free": 34, "sample_full": 2, "sample_free": 2,
        "product_free": 16, "tap0_ready": 6, "taps_ready": 6, "qkv_ready": 6, "z_ready": 2, "conv_stored": 32,
        "head_squares_free": 4, "norms_ready": 2, "decay_args_ready": 4, "decay_ready": 4, "rms_arg_ready": 2,
        "rms_ready": 2, "s_state_landed": 32, "s_conv_ready": 2, "s_silu_ready": 2, "s_state_ready": 2,
        "s_state_stored": 32, "head_output_stored": 32, "state_stored": 32},
    "dve heads": {"dve_order": 72, "bank3_free": 54, "bank3_full": 54, "bank4_free": 38, "bank4_full": 38,
        "bank5_free": 36, "bank5_full": 36, "weight_half_hi": 8, "raw_free": 8, "bank6_full": 32, "bank6_free": 32,
        "bank7_full": 34, "bank7_free": 34, "product_full": 16, "product_free": 16, "s_conv_ready": 2,
        "tap0_ready": 6, "taps_ready": 6, "decay_terms_ready": 2, "head_squares_free": 4, "decay_args_ready": 4,
        "norms_ready": 2, "decay_ready": 4, "blocks_ready": 14, "inverse_t_ready": 2, "state_ready": 2,
        "v_for_state_ready": 16, "rms_arg_ready": 2, "rms_ready": 2, "o_tok_ready": 2, "z_ready": 2,
        "s_silu_ready": 2, "s_squares_ready": 2, "s_qk_ready": 2, "s_v_ready": 2, "s_out_squares_ready": 2,
        "s_v_wide_ready": 2, "s_state_ready": 2, "head_output_stored": 32, "state_stored": 32, "conv_stored": 32,
        "s_state_stored": 32},
    "pe heads": {"bank5_free": 36, "bank5_full": 36, "bank3_free": 54, "bank3_full": 54, "bank4_free": 38,
        "bank4_full": 38, "bank6_free": 32, "bank6_full": 32, "bank7_free": 34, "bank7_full": 34, "raw_free": 8,
        "product_free": 16, "product_full": 16, "sample_free": 2, "sample_full": 2, "qkv_ready": 6,
        "decay_terms_ready": 2, "blocks_ready": 14, "inverse_t_ready": 2, "state_ready": 2,
        "v_for_state_ready": 16, "o_tok_ready": 2, "s_squares_ready": 2, "s_qk_ready": 2, "s_state_landed": 32,
        "s_v_ready": 2, "s_v_wide_ready": 2, "s_out_squares_ready": 2},
    "act mlp0": {"bank3_full": 1, "bank3_free": 1, "bank4_full": 1, "bank4_free": 1, "bank5_full": 1,
        "bank5_free": 1, "raw0_landed": 64, "weight_half_hi": 8, "raw1_landed": 64, "sample_full": 1,
        "sample_free": 1, "product_free": 24, "relu_square_ready": 8, "u_hi_ready": 8},
    "dve mlp0": {"dve_order": 2, "bank3_free": 1, "bank3_full": 1, "bank4_free": 1, "bank4_full": 1,
        "bank5_free": 1, "bank5_full": 1, "weight_half_hi": 8, "raw_free": 8, "product_full": 24,
        "product_free": 24, "relu_square_ready": 8, "u_hi_ready": 8, "u_ready": 8, "u_samples_ready": 1},
    "pe mlp0": {"bank5_free": 1, "bank5_full": 1, "bank3_free": 1, "bank3_full": 1, "bank4_free": 1,
        "bank4_full": 1, "raw_free": 8, "product_free": 24, "product_full": 24, "sample_free": 1, "sample_full": 1,
        "u_ready": 8, "u_samples_ready": 1},
    "sp branch 0": {"q_tile_free": 2, "q_tile0_landed": 16, "q_tile1_landed": 16},
    "sp branch 1": {"q_tile_free": 2, "q_tile0_landed": 16, "q_tile1_landed": 16},
    "sp branch 2": {"q_tile_free": 2, "q_tile0_landed": 16, "q_tile1_landed": 16},
    "sp merge": {"merge_free": 2, "merge0_landed": 16, "merge1_landed": 16},
    "act branch 0": {"bank3_full": 2, "bank3_free": 2, "bank4_full": 4, "bank4_free": 4, "bank5_full": 4,
        "bank5_free": 4, "bank6_full": 2, "bank6_free": 2, "bank7_full": 2, "bank0_full": 2, "bank0_free": 2,
        "bank1_full": 2, "bank1_free": 2, "bank2_full": 2, "bank2_free": 2, "max_ready": 4, "probs_ready": 16,
        "out_taken": 2, "out0_stored": 32, "out1_stored": 32},
    "act branch 1": {"bank3_full": 2, "bank3_free": 2, "bank4_full": 2, "bank4_free": 2, "bank5_full": 4,
        "bank5_free": 4, "bank6_full": 2, "bank6_free": 2, "bank7_full": 2, "bank0_full": 2, "bank0_free": 2,
        "bank1_full": 2, "bank1_free": 2, "bank2_full": 2, "bank2_free": 2, "max_ready": 4, "probs_ready": 16,
        "out_taken": 2, "out0_stored": 32, "out1_stored": 32},
    "act branch 2": {"bank3_full": 2, "bank3_free": 2, "bank5_full": 4, "bank5_free": 4, "bank6_full": 2,
        "bank6_free": 2, "bank7_full": 2, "bank0_full": 2, "bank0_free": 2, "bank1_full": 2, "bank1_free": 2,
        "bank2_full": 2, "bank2_free": 2, "max_ready": 4, "probs_ready": 16, "out_taken": 2, "out0_stored": 32,
        "out1_stored": 32},
    "act merge": {"bank4_full": 1, "bank4_free": 1, "bank5_full": 1, "bank5_free": 1, "u_hi_ready": 2,
        "share_args_ready": 2, "shares_ready": 2},
    "act mlp1": {"bank3_full": 1, "bank3_free": 1, "bank4_full": 1, "bank4_free": 1, "bank5_full": 1,
        "bank5_free": 1, "raw0_landed": 64, "weight_half_hi": 8, "raw1_landed": 64, "sample_full": 1,
        "sample_free": 1, "product_free": 24, "relu_square_ready": 8, "u_hi_ready": 8},
    "dve branch 0": {"dve_order": 8, "bank3_free": 2, "bank3_full": 2, "bank4_free": 4, "bank4_full": 4,
        "bank5_free": 4, "bank5_full": 4, "bank6_full": 2, "bank6_free": 2, "bank7_full": 2, "bank0_full": 2,
        "bank0_free": 2, "bank1_full": 2, "bank1_free": 2, "bank2_full": 2, "bank2_free": 2, "out0_stored": 32,
        "max_ready": 4, "out_taken": 2, "out1_stored": 32},
    "dve branch 1": {"dve_order": 8, "bank3_free": 2, "bank3_full": 2, "bank4_free": 2, "bank4_full": 2,
        "bank5_free": 4, "bank5_full": 4, "bank6_full": 2, "bank6_free": 2, "bank7_full": 2, "bank0_full": 2,
        "bank0_free": 2, "bank1_full": 2, "bank1_free": 2, "bank2_full": 2, "bank2_free": 2, "out0_stored": 32,
        "max_ready": 4, "out_taken": 2, "out1_stored": 32},
    "dve branch 2": {"dve_order": 8, "bank3_free": 2, "bank3_full": 2, "bank5_free": 4, "bank5_full": 4,
        "bank6_full": 2, "bank6_free": 2, "bank7_full": 2, "bank0_full": 2, "bank0_free": 2, "bank1_full": 2,
        "bank1_free": 2, "bank2_full": 2, "bank2_free": 2, "out0_stored": 32, "max_ready": 4, "out_taken": 2,
        "out1_stored": 32},
    "dve merge": {"dve_order": 20, "bank4_free": 1, "bank4_full": 1, "bank5_free": 1, "bank5_full": 1,
        "u_hi_ready": 2, "merge0_landed": 16, "share_args_ready": 2, "shares_ready": 2, "merge_free": 2,
        "merged_ready": 2, "merge1_landed": 16},
    "dve mlp1": {"dve_order": 2, "bank3_free": 1, "bank3_full": 1, "bank4_free": 1, "bank4_full": 1,
        "bank5_free": 1, "bank5_full": 1, "weight_half_hi": 8, "raw_free": 8, "product_full": 24,
        "product_free": 24, "relu_square_ready": 8, "u_hi_ready": 8, "u_ready": 8, "u_samples_ready": 1},
    "pe branch 0": {"bank5_free": 4, "bank5_full": 4, "bank3_free": 2, "bank3_full": 2, "bank4_free": 4,
        "bank4_full": 4, "bank6_free": 2, "bank6_full": 2, "bank7_full": 2, "bank0_free": 2, "bank0_full": 2,
        "bank1_free": 2, "bank1_full": 2, "bank2_free": 2, "bank2_full": 2, "q_tile0_landed": 16,
        "probs_ready": 16, "q_tile_free": 2, "out_taken": 2, "q_tile1_landed": 16},
    "pe branch 1": {"bank5_free": 4, "bank5_full": 4, "bank3_free": 2, "bank3_full": 2, "bank4_free": 2,
        "bank4_full": 2, "bank6_free": 2, "bank6_full": 2, "bank7_full": 2, "bank0_free": 2, "bank0_full": 2,
        "bank1_free": 2, "bank1_full": 2, "bank2_free": 2, "bank2_full": 2, "q_tile0_landed": 16,
        "probs_ready": 16, "q_tile_free": 2, "out_taken": 2, "q_tile1_landed": 16},
    "pe branch 2": {"bank5_free": 4, "bank5_full": 4, "bank3_free": 2, "bank3_full": 2, "bank6_free": 2,
        "bank6_full": 2, "bank7_full": 2, "bank0_free": 2, "bank0_full": 2, "bank1_free": 2, "bank1_full": 2,
        "bank2_free": 2, "bank2_full": 2, "q_tile0_landed": 16, "probs_ready": 16, "q_tile_free": 2,
        "out_taken": 2, "q_tile1_landed": 16},
    "pe merge": {"bank5_free": 1, "bank5_full": 1, "bank4_free": 1, "bank4_full": 1, "merged_ready": 2},
    "pe mlp1": {"bank5_free": 1, "bank5_full": 1, "bank3_free": 1, "bank3_full": 1, "bank4_free": 1,
        "bank4_full": 1, "raw_free": 8, "product_free": 24, "product_full": 24, "sample_free": 1, "sample_full": 1,
        "u_ready": 8, "u_samples_ready": 1},
}


class Lane:

    def __init__(self, eng, sem, room=()):
        self.eng, self.sem = eng, sem
        self.room = set(room)
        self.n, self.turn, self.per, self.last = {}, None, {}, None

    def first(self, name):
        return 0 if name in self.room else CREDIT.get(name, 0)

    def value(self, name):
        n = self.n.get(name, self.first(name))
        assert n > 0, name
        return n if self.turn is None else n + self.turn * self.per.get(name, 0)

    def skip(self, name, n=1):
        self.n[name] = self.n.get(name, self.first(name)) + n

    def next(self, name, n=1):
        self.skip(name, n)
        return self.value(name)

    def add(self, name, n=1):
        self.skip(name, n)
        self.last = name
        return n

    @contextmanager
    def loop(self, trips, name):
        per = PER.get(name, {})
        first = dict(self.n)
        with self.eng.Fori(0, trips) as i:
            self.turn, self.per = i, per
            yield i
            if self.last in self.per and not self.last.endswith(("landed", "stored")):
                self.eng.wait_ge(self.sem(self.last), self.value(self.last))
            self.turn, self.per = None, {}
        moved = {c: self.n[c] - first.get(c, self.first(c)) for c in self.n}
        moved = {c: m for c, m in moved.items() if m}
        if moved != per:
            raise ValueError(f"PER[{name!r}] = {moved}")
        for c, m in moved.items():
            self.n[c] += m * (trips - 1)


def build(nc, t):
    ctx = ExitStack()
    made = {}

    def sem(name):
        if name not in made:
            made[name] = ctx.enter_context(nc.semaphore(name))
        return made[name]

    offset = [1152]

    def at(name, shape, dt, where=None, word=4):
        size = int(np.prod(shape[1:])) * word
        if where is None:
            place = offset[0]
            offset[0] += -(-size // 32) * 32
        else:
            place = where[0]
            where[0] += -(-size // 32) * 32
            assert where[0] <= where[1], (name, where)
        return nc.alloc_sbuf_tensor_at(name, list(shape), dt, offset=place)

    w_hi = at("w_hi", [P, RING, UW, HALF], F32R)
    w_lo = at("w_lo", [P, RING, UW, HALF], F32R)
    w_raw = at("w_raw", [P, 2, 2, HALF], F32)
    gains = at("gains", [P, UNITS * UW], F32)
    ident = at("ident", [P, P], F32)
    ones = at("ones", [P, P], F32)
    fold = at("fold", [2 * NS, NS], F32)
    rs = at("rs", [P, SEQ], F32)
    s_x = at("s_x", [P, KT, NS], F32)
    s_rs = at("s_rs", [P, NS], F32)
    s_tok = at("s_tok", [2 * NS, HALF], F32)
    s_lhs = at("s_lhs", [P, KT, P], F32R)
    s_tmp = at("s_tmp", [P, 4, KT * NS], F32)
    eps = at("eps", [P, 1], F32)
    g_fin = at("g_fin", [P, KT], F32)
    x_start = offset[0]
    x_hi = at("x_hi", [P, KT, SEQ], F32R)
    x_lo = at("x_lo", [P, KT, SEQ], F32R)
    region = offset[0]
    END = 229368
    assert region < END

    def area(start=region):
        return [start, END]

    a = area()
    x = at("x", [P, KT, SEQ], F32, a)
    sq = at("sq", [P, 2, SEQ], F32, a)
    sq_sum = at("sq_sum", [P, SEQ], F32, a)
    w_ab = at("w_ab", [P, KT, 2 * HEADS], F32, a)
    g_ab = at("g_ab", [P, KT], F32, a)
    ab_feat = at("ab_feat", [2 * HEADS, SEQ], F32, a)
    ab = at("ab", [P, 6, 2 * HEADS * CH], F32, a)
    dtb = at("dtb", [P, 2, HEADS], F32, a)
    s_wide = at("s_wide", [2 * HEADS, 2 * HEADS, NS], F32, a)
    s_ab = at("s_ab", [2 * HEADS, NS], F32, a)
    lvl_in = at("lvl_in", [P, LEVELS + 1, P], F32, a)
    start_end = a[0]

    a = area()
    pre = at("pre", [P, 3, SEQ + 8], F32, a)
    z_g = at("z_g", [P, SEQ], F32, a)
    qkv = at("qkv", [P, 3, SEQ], F32, a)
    k_tok = at("k_tok", [P, CH, P], F32, a)
    v_tok = at("v_tok", [P, CH, P], F32, a)
    dec = at("dec", [P, CH, P], F32, a)
    low = at("low", [P, CH, P], F32, a)
    att = at("att", [P, CH, P], F32, a)
    blk = at("blk", [P, CH, P], F32, a)
    inv = at("inv", [P, CH, P], F32, a)
    inv_t = at("inv_t", [P, CH, P], F32, a)
    prod, head_out = dec, dec
    o_tok = low
    a = [max(start_end, a[0]), END]
    lvl = at("lvl", [P, LEVELS + 1, P], BF16, a, 2)
    tri = at("tri", [P, P], F32, a)
    msk = at("msk", [P, P], F32, a)
    state = at("state", [P, P], F32, a)
    gt = at("gt", [P, 6, HEADS * CH], F32, a)
    beta, g_sum, e_pos, e_neg, e_rest, e_last = (gt[:, n] for n in range(6))
    cw = at("cw", [P, HEADS * 12], F32, a)
    col = at("col", [P, 14, CH], F32, a)
    tmp_o = at("tmp_o", [P, P], F32, a)
    g_keep = at("g_keep", [P, HEADS * CH], F32, a)
    vz = at("vz", [P, 3, P], F32, a)
    s_gate = at("s_gate", [P, 2, HEADS, NS], F32, a)
    s_ext = at("s_ext", [P, HEADS, 3, 4, NS], F32, a)
    s_z = at("s_z", [P, NS], F32, a)
    s_taps = at("s_taps", [P, 3, 4, NS], F32, a)
    s_qkv = at("s_qkv", [P, 3, NS], F32, a)
    s_u = at("s_u", [P, 8, NS], F32, a)
    s_og = at("s_og", [P, HEADS, NS], F32, a)
    s_state = blk
    s_v_wide = inv
    s_rows = vz
    a = area()
    a[0] += KT * SEQ * 4
    o_raw = at("o_raw", [P, 2, SEQ], F32, a)
    a = area()
    a[0] += KT * SEQ * 4
    u_hi = at("u_hi", [P, UW, SEQ], F32R, a)
    u_lo = at("u_lo", [P, UW, SEQ], F32R, a)
    relu = at("relu", [P, HALF], F32, a)
    u_lhs = at("u_lhs", [P, UW, P], F32R, a)
    s_acc = at("s_acc", [2 * NS, SEQ], F32, a)

    a = area()
    a[0] += KT * SEQ * 4
    k_mask = at("k_mask", [P, BRANCH, 2, SEQ], F32, a)
    v_feat = at("v_feat", [P, BRANCH, SEQ], F32, a)
    q_stage = at("q_stage", [P, 2, HALF], F32, a)
    s_kv = at("s_kv", [P, 2 * BRANCH, NS], F32, a)
    s_q = at("s_q", [P, 4 * BRANCH, NS], F32, a)

    a = [x_start, region]
    v_keys = at("v_keys", [P, BRANCH, CH, P], F32, a)
    q_tile = at("q_tile", [P, 2, 4, P], F32, a)
    prob = at("prob", [P, 8, 2 * P], F32, a)
    prob_t = at("prob_t", [P, 2, 8, P], F32, a)
    bias = at("bias", [P, 8, 2 * P], F32, a)
    o_out = at("o_out", [P, 2, OW], F32, a)
    dist = at("dist", [P, 3, P], F32, a)
    slopes = at("slopes", [P, BRANCH, 8], F32, a)
    neg_max = at("neg_max", [P, 8], F32, a)
    merge = at("merge", [P, 2, BRANCH, OW], F32, a)
    merged = at("merged", [P, 2, 8 * HD], F32, a)
    share = at("share", [P, 5, BRANCH, 8], F32, a)
    a = [x_start, region]
    a[0] += 4 * (BRANCH * CH * P + 2 * 4 * P)
    s_keys = at("s_keys", [P, NS, SK], F32, a)
    s_va = at("s_va", [P, NS, P], F32, a)
    s_vb = at("s_vb", [SB, NS, P], F32, a)
    s_bias = at("s_bias", [8, SK], F32, a)
    s_qz = at("s_qz", [P, BRANCH, NS, 8], F32, a)
    s_p = at("s_p", [8, NS, SK], F32, a)
    s_pm = at("s_pm", [8, 2, NS], F32, a)
    s_pt = at("s_pt", [P, 2, NS * 8], F32, a)
    s_vrow = at("s_vrow", [NS, BRANCH, P], F32, a)
    s_of = at("s_of", [P, 4, NS], F32, a)

    psum = ctx.enter_context(nc.psum_tensor("psum", [P, 8, HALF], F32))
    for name in CREDIT:
        sem(name)
    block = ctx.enter_context(nc.Block())
    halves = [slice(0, HALF), slice(HALF, SEQ)]

    def f(ap):
        return ap.bitcast(F32)

    def b3(ap, n, m=P):
        return ap.unsqueeze(2).to_broadcast([ap.shape[0], n, m])

    def o3(ap, n):
        return ap.unsqueeze(1).to_broadcast([ap.shape[0], n, ap.shape[-1]])

    def hc(h):
        return slice(4 * h, 4 * h + 4)

    def tiles_of(L, lane, one, before=lambda b: None):
        before(0)
        one(0, 0, 0, 1, 0)
        with L.loop(3, f"{lane} branch 0") as i:
            one(0, 2 * i + 1, 1, 2, 2 * i + 1)
            one(0, 2 * i + 2, 0, 2, 2 * i + 2)
        one(0, 7, 1, 2, 7)
        before(1)
        with L.loop(4, f"{lane} branch 1") as i:
            one(1, 2 * i, 0, 1, (i, 0))
            one(1, 2 * i + 1, 1, 2, (i, 1))
        before(2)
        with L.loop(4, f"{lane} branch 2") as i:
            one(2, 2 * i, 0, 1, 2 * i)
            one(2, 2 * i + 1, 1, 1, 2 * i + 1)

    @block.sync
    def _(sp):
        L = Lane(sp, sem, room=["raw_free", "o_raw_free", "q_tile_free", "merge_free"])
        for dst, name in CONSTS:
            dst_tiles = {"ident": ident, "w_ab": w_ab, "g_ab": g_ab, "dtb": dtb, "lvl": lvl_in, "tri": tri, "msk": msk,
                               "cw": cw, "fold": fold, "s_ext": s_ext, "g_fin": g_fin, "s_x": s_x, "gains": gains}
            sp.dma_start(dst_tiles[dst][:], t[name]).then_inc(sem("constants_landed"), L.add("constants_landed", 16))
        for k in range(KT):
            sp.dma_start(x[:, k, :], t["x"][:, k, :]).then_inc(sem("x_landed"), L.add("x_landed", 16))

        def stream(first, last):
            with L.loop(last - first, "weights") as i:
                for part in range(2):
                    sp.wait_ge(sem("raw_free"), L.next("raw_free"))
                    sp.dma_start(w_raw[:, part:part + 1], t["w"][:, bass.ds((i + first) * 2 + part, 1)]
                    ).then_inc(sem(f"raw{part}_landed"), L.add(f"raw{part}_landed", 16))

        def attention_traffic():
            sp.wait_ge(sem("kvq_done"), L.next("kvq_done"))
            for dst, name in ((dist, "dist"), (slopes, "slopes"), (s_keys, "s_keys"), (s_va, "s_va"), (s_vb, "s_vb"),
                              (s_bias, "s_bias")):
                sp.dma_start(dst[:], t[name]
                ).then_inc(sem("attention_constants_landed"), L.add("attention_constants_landed", 16))
            for g in range(2):
                rows = slice(g * HD, (g + 1) * HD)
                sp.dma_start(t["p_k"][rows], k_mask[rows, :, g]
                ).then_inc(sem("outputs_stored"), L.add("outputs_stored", 16))
            sp.dma_start(t["p_v"], v_feat[:]).then_inc(sem("outputs_stored"), L.add("outputs_stored", 16))
            sp.dma_start(t["s_kv_new"], s_kv[:]).then_inc(sem("outputs_stored"), L.add("outputs_stored", 16))
            sp.wait_ge(sem("s_vrow_ready"), L.next("s_vrow_ready"))
            sp.dma_start(t["s_vnew"], s_vrow[:]).then_inc(sem("s_vnew_stored"), L.add("s_vnew_stored", 16))
            sp.wait_ge(sem("s_vnew_stored"), L.value("s_vnew_stored"))
            sp.wait_ge(sem("attention_constants_landed"), L.value("attention_constants_landed"))
            for b, row in ((1, 64), (2, 81), (0, 82)):
                sp.dma_start(s_vb[row:row + 1], t["s_vnew"][:, b].unsqueeze(0)
                ).then_inc(sem("s_vown_landed"), L.add("s_vown_landed", 16))
            sp.wait_ge(sem("q0_stored"), L.next("q0_stored", 16 * 12))
            sp.wait_ge(sem("q1_stored"), L.next("q1_stored", 16 * 12))

            def load(b, tile, par, nk, place):
                sp.wait_ge(sem("q_tile_free"), L.next("q_tile_free"))
                sp.dma_start(q_tile[:, par], t["q"][:, 4 * b:4 * b + 4, bass.ds(tile * P, P)]
                ).then_inc(sem(f"q_tile{par}_landed"), L.add(f"q_tile{par}_landed", 16))
            tiles_of(L, "sp", load)
            sp.wait_ge(sem("out0_stored"), L.next("out0_stored", 32 * 12))
            sp.wait_ge(sem("out1_stored"), L.next("out1_stored", 32 * 12))
            with L.loop(CH // 2, "sp merge") as i:
                for par in range(2):
                    sp.wait_ge(sem("merge_free"), L.next("merge_free"))
                    sp.dma_start(merge[:, par], t["att"][bass.ds((2 * i + par) * P, P)]
                    ).then_inc(sem(f"merge{par}_landed"), L.add(f"merge{par}_landed", 16))

        stream(0, U_OUT + 2)
        for b in range(BRANCH):
            sp.dma_start(t[f"s_kv{b}_old"], t[f"cache{b}"]).then_inc(sem("outputs_stored"), L.add("outputs_stored", 16))
        sp.wait_ge(sem("head_output_stored"), L.next("head_output_stored", 16 * HEADS))
        sp.wait_ge(sem("x_back"), L.next("x_back", KT))
        sp.dma_start(t["s_conv"], s_ext[:].rearrange("p h k j n -> p (h k) j n")[:, :, 1:4]
        ).then_inc(sem("outputs_stored"), L.add("outputs_stored", 16))
        for k in range(KT):
            sp.wait_ge(sem("o_raw_free"), L.next("o_raw_free"))
            sp.dma_start(o_raw[:, k % 2], t["o_heads"][:, k]
            ).then_inc(sem(f"o_raw{k % 2}_landed"), L.add(f"o_raw{k % 2}_landed", 16))
        stream(U_OUT + 2, U_KVQ + 2)
        stream(U_KVQ + 2, U_WO + 2)
        attention_traffic()
        stream(U_WO + 2, UNITS)
        sp.wait_ge(sem("y_ready"), L.next("y_ready", KT + 1))
        for k in range(KT):
            sp.dma_start(t["y"][:, k], x[:, k]).then_inc(sem("outputs_stored"), L.add("outputs_stored", 16))
        sp.dma_start(t["s_y"], s_x[:]).then_inc(sem("outputs_stored"), L.add("outputs_stored", 16))
        sp.wait_ge(sem("outputs_stored"), L.value("outputs_stored"))
        sp.wait_ge(sem("state_stored"), L.next("state_stored", 16 * HEADS))
        sp.wait_ge(sem("conv_stored"), L.next("conv_stored", 16 * HEADS))
        sp.wait_ge(sem("s_state_stored"), L.next("s_state_stored", 16 * HEADS))

    @block.scalar
    def _(act):
        L = Lane(act, sem, room=["square_free", "head_squares_free"])

        def split_hi(unit, slot, parts=(0, 1)):
            for part in parts:
                act.wait_ge(sem(f"raw{part}_landed"), L.next(f"raw{part}_landed", 16))
                for k in range(2):
                    done = act.activation(w_hi[:, slot, 2 * part + k], w_raw[:, part, k], ACT.Copy,
                                          scale=gains[:, bass.ds(unit * UW + 2 * part + k, 1)])
                done.then_inc(sem("weight_half_hi"), L.add("weight_half_hi"))

        def norm(split=True):
            if split:
                for k in range(KT):
                    act.activation(x_hi[:, k], x[:, k], ACT.Copy).then_inc(sem("x_hi_ready"), L.add("x_hi_ready"))
            for k in range(KT):
                act.wait_ge(sem("square_free"), L.next("square_free"))
                act.activation(sq[:, k % 2], x[:, k], ACT.Square).then_inc(sem("square_ready"), L.add("square_ready"))
            for h in range(2):
                act.wait_ge(sem(f"bank{3 + h}_full"), L.next(f"bank{3 + h}_full"))
                act.activation(rs[:, halves[h]], psum[:, 3 + h], ACT.Sqrt, scale=1.0 / D_MODEL, bias=eps[:, 0:1]
                ).then_inc(sem(f"bank{3 + h}_free"), L.add(f"bank{3 + h}_free"))
            act.wait_ge(sem("bank5_full"), L.next("bank5_full"))
            act.activation(s_rs[:], psum[:, 5, 0:NS], ACT.Sqrt, scale=1.0 / D_MODEL, bias=eps[:, 0:1]
            ).then_inc(sem("bank5_free"), L.add("bank5_free"))

        def skip(*banks):
            for b in banks:
                L.skip(f"bank{b}_full"), L.skip(f"bank{b}_free")

        act.wait_ge(sem("constants_landed"), L.next("constants_landed", 16 * len(CONSTS)))
        act.wait_ge(sem("eps_set"), L.next("eps_set"))
        act.wait_ge(sem("x_landed"), L.next("x_landed", 16 * KT))
        norm()
        split_hi(0, 0)
        split_hi(1, 1)

        skip(3, 4, 5, 5, 5)
        act.wait_ge(sem("gate_args_ready"), L.next("gate_args_ready"))
        act.activation(ab[:, 0:1], ab[:, 0:1], ACT.Exp, scale=-1.0
        ).then_inc(sem("act_order"), L.add("act_order"))
        act.activation(dtb[:, 0], dtb[:, 0], ACT.Exp).then_inc(sem("act_order"), L.add("act_order"))
        act.activation(ab[:, 3], ab[:, 2], ACT.Exp, scale=-1.0
        ).then_inc(sem("gate_exps_ready"), L.add("gate_exps_ready"))
        act.wait_ge(sem("softplus_arg_ready"), L.next("softplus_arg_ready"))
        act.activation(ab[:, 5], ab[:, 4], ACT.Ln
        ).then_inc(sem("softplus_log_ready"), L.add("softplus_log_ready"))
        skip(6, 7)
        act.wait_ge(sem("decay_sums_ready"), L.next("decay_sums_ready"))
        act.activation(e_pos, g_sum, ACT.Exp).then_inc(sem("act_order"), L.add("act_order"))
        act.activation(e_last, e_last, ACT.Exp).then_inc(sem("act_order"), L.add("act_order"))
        act.activation(e_rest, e_rest, ACT.Exp).then_inc(sem("act_order"), L.add("act_order"))
        act.activation(s_gate[:, 1], ab[:, 3, 64:].rearrange("p (h n) -> p h n", n=NS), ACT.Exp
        ).then_inc(sem("decays_ready"), L.add("decays_ready"))

        def conv_silu(head):
            act.wait_ge(sem("product_free"), L.next("product_free", 8))
            act.dma_start(t["p_conv"][:, bass.ds(head * 3, 3)], pre[:, :, SEQ:SEQ + 3]
            ).then_inc(sem("conv_stored"), L.add("conv_stored", 16))
            for n in range(3):
                act.activation(qkv[:, n], pre[:, n, 0:SEQ], ACT.Copy, scale=cw[:, bass.ds(head * 12 + n * 4, 1)]
                ).then_inc(sem("tap0_ready"), L.add("tap0_ready"))
            for n in range(3):
                act.wait_ge(sem("taps_ready"), L.next("taps_ready"))
                act.activation(qkv[:, n], qkv[:, n], ACT.Silu).then_inc(sem("qkv_ready"), L.add("qkv_ready"))
            act.activation(z_g[:], z_g[:], ACT.Silu).then_inc(sem("z_ready"), L.add("z_ready"))

        def gdn(head, slots, more):
            act.wait_ge(sem("bank3_full"), L.next("bank3_full"))
            L.skip("bank3_free")
            for h in range(2):
                act.wait_ge(sem("bank3_full"), L.next("bank3_full"))
                act.wait_ge(sem("head_squares_free"), L.next("head_squares_free"))
                act.activation(k_tok[:, hc(h)], psum[:, 3].rearrange("p (c n) -> p c n", n=P), ACT.Copy
                ).then_inc(sem("act_order"), L.add("act_order"))
                act.activation(blk[:, 0:4], psum[:, 3].rearrange("p (c n) -> p c n", n=P), ACT.Square
                ).then_inc(sem("bank3_free"), L.add("bank3_free"))
                act.wait_ge(sem("bank4_full"), L.next("bank4_full"))
                act.activation(blk[:, 4:8], psum[:, 4].rearrange("p (c n) -> p c n", n=P), ACT.Square
                ).then_inc(sem("bank4_free"), L.add("bank4_free"))
                skip(5)
            act.wait_ge(sem("head_squares_free"), L.next("head_squares_free"))
            L.skip("head_squares_free", -1)
            act.activation(col[:, 2:4], col[:, 0:2], ACT.Sqrt, bias=eps[:, 0:1]
            ).then_inc(sem("norms_ready"), L.add("norms_ready"))
            for h in range(2):
                act.wait_ge(sem("decay_args_ready"), L.next("decay_args_ready"))
                act.activation(dec[:, hc(h)], dec[:, hc(h)], ACT.Exp).then_inc(sem("decay_ready"), L.add("decay_ready"))
            skip(6, 7, 3, 4, 5, 3, 6, 7)
            for level in range(1, LEVELS + 1):
                for h in range(2):
                    act.wait_ge(sem(f"bank{3 + h}_full"), L.next(f"bank{3 + h}_full"))
                    act.activation(prod[:, hc(h)], psum[:, 3 + h].rearrange("p (c n) -> p c n", n=P), ACT.Copy
                    ).then_inc(sem(f"bank{3 + h}_free"), L.add(f"bank{3 + h}_free"))
                    skip(*((5 + h,) if level < LEVELS else ()))
                skip(7, 3)
                if more and level <= 4:
                    which, part = divmod(level - 1, 2)
                    split_hi(2 * head + 4 + which, slots[which], (part,))
            for c in range(CH):
                act.wait_ge(sem("bank6_full"), L.next("bank6_full"))
                if c:
                    act.wait_ge(sem("bank7_free"), L.next("bank7_free"))
                act.activation(tmp_o[:], psum[:, 6, 0:P], ACT.Copy, scale=gt[:, 2, bass.ds(head * CH + c, 1)]
                ).then_inc(sem("bank6_free"), L.add("bank6_free"))
                skip(4, 5, 3)
                L.skip("bank7_full")
            act.wait_ge(sem("bank7_free"), L.next("bank7_free"))
            act.wait_ge(sem("rms_arg_ready"), L.next("rms_arg_ready"))
            act.activation(col[:, 10], col[:, 9], ACT.Sqrt, scale=1.0 / P, bias=eps[:, 0:1]
            ).then_inc(sem("rms_ready"), L.add("rms_ready"))
            for b in (4, 5):
                L.skip(f"bank{b}_full")
                act.wait_ge(sem(f"bank{b}_free"), L.next(f"bank{b}_free"))
            act.dma_start(s_state[:].unsqueeze(1), t["s_rec_in"][:, bass.ds(head, 1)]
            ).then_inc(sem("s_state_landed"), L.add("s_state_landed", 16))
            act.wait_ge(sem("s_conv_ready"), L.next("s_conv_ready"))
            act.activation(s_qkv[:], s_qkv[:], ACT.Silu).then_inc(sem("act_order"), L.add("act_order"))
            act.activation(s_z[:], s_z[:], ACT.Silu).then_inc(sem("s_silu_ready"), L.add("s_silu_ready"))
            act.wait_ge(sem("bank3_full"), L.next("bank3_full"))
            act.activation(s_u[:, 0:2], psum[:, 3, 0:2 * NS].rearrange("p (k n) -> p k n", n=NS), ACT.Sqrt,
                                bias=eps[:, 0:1]).then_inc(sem("bank3_free"), L.add("bank3_free"))
            skip(4)
            act.wait_ge(sem("bank5_full"), L.next("bank5_full"))
            act.activation(s_rows[0:NS, 0:2], psum[0:NS, 5, 0:2 * P].rearrange("p (k n) -> p k n", n=P), ACT.Copy
            ).then_inc(sem("bank5_free"), L.add("bank5_free"))
            skip(6, 7)
            act.wait_ge(sem("bank3_full"), L.next("bank3_full"))
            act.activation(s_u[:, 6], psum[:, 3, 0:NS], ACT.Sqrt, scale=1.0 / P / P, bias=eps[:, 0:1]
            ).then_inc(sem("bank3_free"), L.add("bank3_free"))
            act.wait_ge(sem("s_state_ready"), L.next("s_state_ready"))
            act.dma_start(t["s_rec"][:, bass.ds(head, 1)], s_state[:].unsqueeze(1)
            ).then_inc(sem("s_state_stored"), L.add("s_state_stored", 16))
            act.dma_start(t["o_heads"][:, bass.ds(head, 1)], head_out[:].rearrange("p c n -> p (c n)").unsqueeze(1)
            ).then_inc(sem("head_output_stored"), L.add("head_output_stored", 16))
            act.dma_start(t["p_rec"][:, bass.ds(head, 1)], state[:].unsqueeze(1)
            ).then_inc(sem("state_stored"), L.add("state_stored", 16))

        def samples_out():
            act.wait_ge(sem("sample_full"), L.next("sample_full"))
            act.activation(s_tok[:], psum[0:2 * NS, 2], ACT.Copy).then_inc(sem("sample_free"), L.add("sample_free"))

        def step(head, slots, more=True):
            samples_out()
            conv_silu(head)
            gdn(head, slots, more)

        split_hi(2, 2)
        split_hi(3, 3)
        with L.loop(HEADS // 2 - 1, "act heads") as i:
            step(2 * i, (0, 1))
            step(2 * i + 1, (2, 3))
        step(HEADS - 2, (0, 1))
        step(HEADS - 1, (2, 3), more=False)

        for k in range(KT):
            act.wait_ge(sem(f"o_raw{k % 2}_landed"), L.next(f"o_raw{k % 2}_landed", 16))
            act.wait_ge(sem("x_back"), L.next("x_back"))
            act.activation(x_hi[:, k], o_raw[:, k % 2], ACT.Copy).then_inc(sem("o_hi_ready"), L.add("o_hi_ready"))
        for g in range(2):
            split_hi(U_OUT + 2 * g + 2, (2 * g + 2) % RING)
            split_hi(U_OUT + 2 * g + 3, (2 * g + 3) % RING)
            samples_out()
            act.wait_ge(sem("bank3_full"), L.next("bank3_full"))
            L.skip("bank3_free")
        act.wait_ge(sem("product_free"), L.next("product_free", 16))

        def mlp(unit, name, more):
            def block(b, last=False):
                u = unit + 4 * b
                for n in range(8):
                    if n == 1:
                        split_hi(u + 2, 2)
                    if n == 4:
                        split_hi(u + 3, 3)
                    h, tile = divmod(n, 4)
                    act.wait_ge(sem("relu_square_ready"), L.next("relu_square_ready"))
                    act.activation(u_hi[:, tile, halves[h]], relu[:], ACT.Copy
                    ).then_inc(sem("u_hi_ready"), L.add("u_hi_ready"))
                samples_out()
                if not last:
                    split_hi(u + 4, 0)
                    split_hi(u + 5, 1)
                act.wait_ge(sem("bank3_full"), L.next("bank3_full"))
                L.skip("bank3_free")
                for bank in (4, 5):
                    act.wait_ge(sem(f"bank{bank}_full"), L.next(f"bank{bank}_full")), L.skip(f"bank{bank}_free")
                act.wait_ge(sem("product_free"), L.next("product_free", 24))
            with L.loop(8 if more else 7, name) as b:
                block(b)
            if not more:
                block(7, last=True)
            skip(3)

        def attention_layer():
            norm()
            for gi in range(5):
                split_hi(U_KVQ + 2 * gi + 2, (2 * gi + 2) % RING)
                split_hi(U_KVQ + 2 * gi + 3, (2 * gi + 3) % RING)
                if gi < 2:
                    act.wait_ge(sem("product_free"), L.next("product_free", 8 if gi == 0 else 4))
                else:
                    b = gi - 2
                    d = DIL[b]
                    I = HALF // d
                    for n in range(8):
                        h, tile = divmod(n, 4)
                        act.wait_ge(sem("product_free"), L.next("product_free"))
                        dst = t["q"][:, 4 * b + tile].rearrange("p (r i) -> p r i", r=d)[:, :, h * I:(h + 1) * I]
                        act.dma_start(dst, q_stage[:, n % 2].rearrange("p (r i) -> p r i", r=d)
                        ).then_inc(sem(f"q{n % 2}_stored"), L.add(f"q{n % 2}_stored", 16))
                samples_out()
                act.wait_ge(sem("bank3_full"), L.next("bank3_full")), L.skip("bank3_free")
            act.wait_ge(sem("kvq_done"), L.next("kvq_done"))
            for b in range(BRANCH):
                for h in range(2):
                    act.wait_ge(sem(f"bank{3 + h}_full"), L.next(f"bank{3 + h}_full"))
                    act.activation(v_keys[:, b, hc(h)], psum[:, 3 + h].rearrange("p (c n) -> p c n", n=P), ACT.Copy
                    ).then_inc(sem(f"bank{3 + h}_free"), L.add(f"bank{3 + h}_free"))
            act.wait_ge(sem("bank4_full"), L.next("bank4_full"))
            act.activation(s_vrow[:], psum[0:NS, 4, 0:BRANCH * P].rearrange("p (b n) -> p b n", n=P), ACT.Copy
            ).then_inc(sem("s_vrow_ready"), L.add("s_vrow_ready"))
            skip(0, 1, 2, 3)
            act.wait_ge(sem("s_scores_ready"), L.next("s_scores_ready"))
            act.activation(s_p[:], s_p[:], ACT.Exp).then_inc(sem("s_exp_ready"), L.add("s_exp_ready"))
            act.wait_ge(sem("bank4_full"), L.next("bank4_full"))
            act.activation(s_pt[:, 0], psum[:, 4, 0:8 * NS], ACT.Copy).then_inc(sem("bank4_free"), L.add("bank4_free"))
            act.wait_ge(sem("bank5_full"), L.next("bank5_full"))
            act.activation(s_pt[0:SB, 1], psum[0:SB, 5, 0:8 * NS], ACT.Copy
            ).then_inc(sem("bank5_free"), L.add("bank5_free"))
            skip(6)

            def tile_step(b, tile, par, nk, place):
                cols = slice((2 - nk) * P, 2 * P)
                for hs in range(2):
                    act.wait_ge(sem("max_ready"), L.next("max_ready"))
                    for s in range(4 * hs, 4 * hs + 4):
                        act.activation(prob[:, s, cols], prob[:, s, cols], ACT.Exp, bias=neg_max[:, s:s + 1],
                                            accum_out=o_out[:, par, 8 * HD + 8 + s:8 * HD + 9 + s]
                                            ).then_inc(sem("probs_ready"), L.add("probs_ready"))
                skip(0, 1, 2, 3)
                for hs in range(2):
                    if nk == 2:
                        act.wait_ge(sem("bank4_full"), L.next("bank4_full"))
                        act.activation(prob_t[:, 0, hc(hs)], psum[:, 4].rearrange("p (c n) -> p c n", n=P), ACT.Copy
                        ).then_inc(sem("bank4_free"), L.add("bank4_free"))
                    skip(5)
                skip(6)
                L.skip("bank7_full")
                act.wait_ge(sem("out_taken"), L.next("out_taken"))
                for g in range(2):
                    rows = slice(g * HD, (g + 1) * HD)
                    if b == 0:
                        dst = t["att"][bass.ds(place * P + g * HD, HD), 0]
                        act.dma_start(dst, o_out[rows, par]
                        ).then_inc(sem(f"out{par}_stored"), L.add(f"out{par}_stored", 16))
                        continue
                    if b == 1:
                        r, i = place
                        dst = t["att"][:, 1].rearrange("(n r) w -> n r w", r=4)[i * P + g * HD:i * P + (g + 1) * HD,
                                                                              bass.ds(r, 1)]
                    else:
                        dst = t["att"][:, 2].rearrange("(n r) w -> n r w", r=16)[:, bass.ds(2 * place + g, 1)]
                    act.dma_start(dst, o_out[rows, par].unsqueeze(1)
                    ).then_inc(sem(f"out{par}_stored"), L.add(f"out{par}_stored", 16))
            tiles_of(L, "act", tile_step)
            with L.loop(CH // 2, "act merge") as i:
                for par in range(2):
                    act.wait_ge(sem("share_args_ready"), L.next("share_args_ready"))
                    act.activation(share[:, 1], share[:, 0], ACT.Exp
                    ).then_inc(sem("shares_ready"), L.add("shares_ready"))
                    act.wait_ge(sem(f"bank{4 + par}_full"), L.next(f"bank{4 + par}_full")), L.skip(f"bank{4 + par}_free")
                    act.activation(u_hi[:, :, bass.ds((2 * i + par) * P, P)],
                                        psum[:, 4 + par].rearrange("p (c n) -> p c n", n=P), ACT.Copy
                                        ).then_inc(sem("u_hi_ready"), L.add("u_hi_ready"))
            split_hi(U_MLP1, 0)
            split_hi(U_MLP1 + 1, 1)
            for bank in (4, 5):
                act.wait_ge(sem(f"bank{bank}_full"), L.next(f"bank{bank}_full")), L.skip(f"bank{bank}_free")
            skip(3)

        norm()
        mlp(U_MLP0, "act mlp0", True)
        attention_layer()
        act.wait_ge(sem("product_free"), L.next("product_free", 16))
        norm()
        mlp(U_MLP1, "act mlp1", False)
        norm(split=False)

    @block.vector
    def _(dve):
        L = Lane(dve, sem, room=["out0_stored", "out1_stored"])
        v = dve
        for name, n in CREDIT.items():
            v.sem_inc(sem(name), n)

        def split_lo(unit, slot, parts=(0, 1)):
            for part in parts:
                v.wait_ge(sem("weight_half_hi"), L.next("weight_half_hi"))
                for k in range(2):
                    done = v.scalar_tensor_tensor(w_lo[:, slot, 2 * part + k], w_raw[:, part, k],
                                                  gains[:, bass.ds(unit * UW + 2 * part + k, 1)],
                                                  f(w_hi[:, slot, 2 * part + k]), ALU.mult, ALU.subtract)
                done.then_inc(sem("raw_free"), L.add("raw_free"))

        def norm(split=True):
            if split:
                for k in range(KT):
                    v.wait_ge(sem("x_hi_ready"), L.next("x_hi_ready"))
                    v.tensor_tensor(x_lo[:, k], x[:, k], f(x_hi[:, k]), ALU.subtract
                    ).then_inc(sem("x_ready"), L.add("x_ready"))
                v.tensor_copy(s_lhs[:, :, 0:NS], s_x[:]).then_inc(sem("dve_order"), L.add("dve_order"))
                v.wait_ge(sem(L.last), L.value(L.last))
                v.tensor_tensor(s_lhs[:, :, NS:2 * NS], s_x[:], f(s_lhs[:, :, 0:NS]), ALU.subtract
                ).then_inc(sem("samples_ready"), L.add("samples_ready"))
            flat = s_x[:].rearrange("p k n -> p (k n)")
            v.tensor_tensor(s_tmp[:, 0], flat, flat, ALU.mult).then_inc(sem("dve_order"), L.add("dve_order"))
            v.wait_ge(sem(L.last), L.value(L.last))
            v.tensor_reduce(s_tmp[:, 1, 0:NS], s_tmp[:, 0].rearrange("p (k n) -> p n k", n=NS), AXX, ALU.add
            ).then_inc(sem("sample_squares_ready"), L.add("sample_squares_ready"))
            for k in range(KT):
                v.wait_ge(sem("square_ready"), L.next("square_ready"))
                if k == 0:
                    v.tensor_copy(sq_sum[:], sq[:, 0]).then_inc(sem("square_free"), L.add("square_free"))
                else:
                    v.wait_ge(sem(L.last), L.value(L.last))
                    v.tensor_tensor(sq_sum[:], sq_sum[:], sq[:, k % 2], ALU.add
                    ).then_inc(sem("square_free"), L.add("square_free"))
            for h in range(2):
                v.wait_ge(sem(f"bank{3 + h}_free"), L.next(f"bank{3 + h}_free"))
                L.skip(f"bank{3 + h}_full")
                v.reciprocal(rs[:, halves[h]], rs[:, halves[h]]).then_inc(sem("rs_ready"), L.add("rs_ready"))
            v.wait_ge(sem("bank5_free"), L.next("bank5_free"))
            L.skip("bank5_full")
            v.reciprocal(s_rs[:], s_rs[:]).then_inc(sem("rs_ready"), L.add("rs_ready"))
            v.wait_ge(sem(L.last), L.value(L.last))

        def skip(*banks):
            for b in banks:
                L.skip(f"bank{b}_full"), L.skip(f"bank{b}_free")


        v.memset(eps[:], EPS).then_inc(sem("eps_set"), L.add("eps_set"))
        v.memset(ones[:], 1.0).then_inc(sem("ones_set"), L.add("ones_set"))
        v.memset(f(s_lhs[:]), 0.0).then_inc(sem("dve_order"), L.add("dve_order"))
        v.wait_ge(sem(L.last), L.value(L.last))
        v.wait_ge(sem("constants_landed"), L.next("constants_landed", 16 * len(CONSTS)))
        v.tensor_copy(lvl[:], lvl_in[:]).then_inc(sem("dve_order"), L.add("dve_order"))
        v.wait_ge(sem("x_landed"), L.next("x_landed", 16 * KT))
        v.tensor_tensor(w_ab[:], w_ab[:], b3(g_ab[:], KT, 2 * HEADS), ALU.mult
        ).then_inc(sem("w_ab_ready"), L.add("w_ab_ready"))
        norm()
        split_lo(0, 0)
        split_lo(1, 1)

        for h in range(2):
            v.wait_ge(sem(f"bank{3 + h}_full"), L.next(f"bank{3 + h}_full"))
            v.tensor_tensor(ab_feat[:, halves[h]], psum[0:2 * HEADS, 3 + h], rs[0:2 * HEADS, halves[h]], ALU.mult
            ).then_inc(sem(f"bank{3 + h}_free"), L.add(f"bank{3 + h}_free"))
        v.wait_ge(sem("bank5_full"), L.next("bank5_full"))
        v.tensor_tensor(s_ab[:], psum[0:2 * HEADS, 5, 0:NS], s_rs[0:2 * HEADS], ALU.mult
        ).then_inc(sem("bank5_free"), L.add("bank5_free"))
        v.wait_ge(sem(L.last), L.value(L.last))
        v.tensor_tensor(s_wide[:], b3(ident[0:2 * HEADS, 0:2 * HEADS], 2 * HEADS, NS), o3(s_ab[:], 2 * HEADS),
                             ALU.mult).then_inc(sem("s_wide_ready"), L.add("s_wide_ready"))
        v.wait_ge(sem("bank5_full"), L.next("bank5_full"))
        turned = psum[:, 5, 0:P].rearrange("p (c m h) -> p m h c", m=2, h=HEADS)
        three = [ab[:, n, 0:64].rearrange("p (h c) -> p h c", c=CH) for n in range(6)]
        s_three = [ab[:, n, 64:].rearrange("p (h c) -> p h c", c=CH) for n in range(6)]
        v.tensor_copy(three[0], turned[:, 0]).then_inc(sem("dve_order"), L.add("dve_order"))
        v.tensor_tensor(three[1], turned[:, 1], b3(dtb[:, 1], HEADS, CH), ALU.add
        ).then_inc(sem("bank5_free"), L.add("bank5_free"))
        v.wait_ge(sem("bank5_full"), L.next("bank5_full"))
        wide = psum[:, 5, 0:P].rearrange("p (m h n) -> p m h n", m=2, n=NS)
        v.tensor_copy(s_three[0], wide[:, 0]).then_inc(sem("dve_order"), L.add("dve_order"))
        v.tensor_tensor(s_three[1], wide[:, 1], b3(dtb[:, 1], HEADS, NS), ALU.add
        ).then_inc(sem("bank5_free"), L.add("bank5_free"))
        v.wait_ge(sem(L.last), L.value(L.last))
        v.scalar_tensor_tensor(ab[:, 2], ab[:, 1], -1.0, ab[:, 1], ALU.mult, ALU.max
        ).then_inc(sem("gate_args_ready"), L.add("gate_args_ready"))
        v.wait_ge(sem("gate_exps_ready"), L.next("gate_exps_ready"))
        v.tensor_scalar(ab[:, 0], ab[:, 0], 1.0, None, ALU.add).then_inc(sem("dve_order"), L.add("dve_order"))
        v.tensor_scalar(ab[:, 4], ab[:, 3], 1.0, None, ALU.add
        ).then_inc(sem("softplus_arg_ready"), L.add("softplus_arg_ready"))
        v.wait_ge(sem(L.last), L.value(L.last))
        v.reciprocal(beta, ab[:, 0, 0:64]).then_inc(sem("dve_order"), L.add("dve_order"))
        v.reciprocal(s_gate[:, 0], s_three[0]).then_inc(sem("dve_order"), L.add("dve_order"))
        v.scalar_tensor_tensor(ab[:, 2], ab[:, 4], -1.0, ab[:, 3], ALU.add, ALU.subtract
        ).then_inc(sem("dve_order"), L.add("dve_order"))
        v.wait_ge(sem("softplus_log_ready"), L.next("softplus_log_ready"))
        v.wait_ge(sem(L.last), L.value(L.last))
        v.tensor_tensor(ab[:, 5], ab[:, 5], ab[:, 2], ALU.subtract).then_inc(sem("dve_order"), L.add("dve_order"))
        v.wait_ge(sem(L.last), L.value(L.last))
        v.scalar_tensor_tensor(ab[:, 5], ab[:, 1], 0.0, ab[:, 5], ALU.max, ALU.add
        ).then_inc(sem("dve_order"), L.add("dve_order"))
        v.wait_ge(sem(L.last), L.value(L.last))
        v.scalar_tensor_tensor(s_three[3], s_three[5], -1.0, b3(dtb[:, 0], HEADS, NS), ALU.mult, ALU.mult
        ).then_inc(sem("dve_order"), L.add("dve_order"))
        v.scalar_tensor_tensor(three[3], three[5], -1.0, b3(dtb[:, 0], HEADS, CH), ALU.mult, ALU.mult
        ).then_inc(sem("g_ready"), L.add("g_ready"))
        v.wait_ge(sem("bank6_full"), L.next("bank6_full"))
        v.tensor_copy(g_sum, psum[:, 6, 0:64]).then_inc(sem("bank6_free"), L.add("bank6_free"))
        v.wait_ge(sem("bank7_full"), L.next("bank7_full"))
        v.tensor_copy(e_last, psum[:, 7, 0:64]).then_inc(sem("bank7_free"), L.add("bank7_free"))
        v.wait_ge(sem(L.last), L.value(L.last))
        v.tensor_tensor(e_rest, e_last, g_sum, ALU.subtract
        ).then_inc(sem("decay_sums_ready"), L.add("decay_sums_ready"))
        v.wait_ge(sem("decays_ready"), L.next("decays_ready"))
        v.tensor_scalar(e_neg, e_pos, -1.0, None, ALU.mult).then_inc(sem("dve_order"), L.add("dve_order"))
        v.wait_ge(sem(L.last), L.value(L.last))
        v.tensor_copy(g_keep[:], ab[:, 3, 0:64]).then_inc(sem("dve_order"), L.add("dve_order"))
        v.wait_ge(sem(L.last), L.value(L.last))
        v.memset(pre[:, :, 0:3], 0.0).then_inc(sem("dve_order"), L.add("dve_order"))
        v.wait_ge(sem(L.last), L.value(L.last))

        def take_product(n, first=False):
            tile, h = divmod(n, 2)
            if n == 1 and not first:
                v.wait_ge(sem("conv_stored"), L.next("conv_stored", 16))
            out = pre[:, tile, 3 + h * HALF:3 + (h + 1) * HALF] if tile < 3 else z_g[:, halves[h]]
            v.wait_ge(sem("product_full"), L.next("product_full"))
            v.tensor_tensor(out, psum[:, n % 2], rs[:, halves[h]], ALU.mult
            ).then_inc(sem("product_free"), L.add("product_free"))

        def sample_rows(head):
            v.wait_ge(sem("bank3_full"), L.next("bank3_full"))
            rows = psum[:, 3, 0:4 * NS].rearrange("p (k n) -> p k n", n=NS)
            s_in = s_ext[:, bass.ds(head, 1)].rearrange("p u k j n -> p (u k) j n")
            v.tensor_tensor(s_in[:, :, 3], rows[:, 0:3], o3(s_rs[:], 3), ALU.mult
            ).then_inc(sem("dve_order"), L.add("dve_order"))
            v.tensor_tensor(s_z[:], rows[:, 3], s_rs[:], ALU.mult).then_inc(sem("bank3_free"), L.add("bank3_free"))
            v.wait_ge(sem(L.last), L.value(L.last))
            taps = cw[:, bass.ds(head * 12, 12)].rearrange("p (k j) -> p k j", j=4).unsqueeze(3)
            v.tensor_tensor(s_taps[:], s_in, taps.to_broadcast([P, 3, 4, NS]), ALU.mult
            ).then_inc(sem("dve_order"), L.add("dve_order"))
            v.wait_ge(sem(L.last), L.value(L.last))
            v.tensor_reduce(s_qkv[:], s_taps[:].rearrange("p k j n -> p k n j"), AXX, ALU.add
            ).then_inc(sem("s_conv_ready"), L.add("s_conv_ready"))

        def conv(head):
            for n in range(3):
                v.wait_ge(sem("tap0_ready"), L.next("tap0_ready"))
                for j in range(1, 4):
                    if j > 1:
                        v.wait_ge(sem(L.last), L.value(L.last))
                    v.scalar_tensor_tensor(qkv[:, n], pre[:, n, j:j + SEQ],
                                                cw[:, bass.ds(head * 12 + n * 4 + j, 1)],
                                                qkv[:, n], ALU.mult, ALU.add
                                                ).then_inc(sem("taps_ready" if j == 3 else "dve_order"), L.add("taps_ready" if j == 3 else "dve_order"))

        def sample_step(head):
            one = bass.ds(head, 1)

            def gate(n):
                return s_gate[:, n, one].rearrange("p u n -> p (u n)")
            v.wait_ge(sem("s_silu_ready"), L.next("s_silu_ready"))
            v.tensor_tensor(s_u[:, 2:4], s_qkv[:, 0:2], s_qkv[:, 0:2], ALU.mult
            ).then_inc(sem("s_squares_ready"), L.add("s_squares_ready"))
            v.wait_ge(sem("bank3_free"), L.next("bank3_free"))
            L.skip("bank3_full")
            v.reciprocal(s_u[:, 0:2], s_u[:, 0:2]).then_inc(sem("dve_order"), L.add("dve_order"))
            v.wait_ge(sem(L.last), L.value(L.last))
            v.tensor_tensor(s_qkv[:, 0:2], s_qkv[:, 0:2], s_u[:, 0:2], ALU.mult
            ).then_inc(sem("dve_order"), L.add("dve_order"))
            v.wait_ge(sem(L.last), L.value(L.last))
            v.tensor_tensor(s_u[:, 2], s_qkv[:, 0], s_qkv[:, 1], ALU.mult
            ).then_inc(sem("s_qk_ready"), L.add("s_qk_ready"))
            v.wait_ge(sem("bank4_full"), L.next("bank4_full"))
            sk = psum[:, 4, 0:2 * NS].rearrange("p (n m) -> p m n", m=2)
            v.tensor_tensor(s_u[:, 3], sk[:, 1], gate(1), ALU.mult).then_inc(sem("dve_order"), L.add("dve_order"))
            v.tensor_tensor(s_u[:, 4], sk[:, 0], gate(1), ALU.mult).then_inc(sem("dve_order"), L.add("dve_order"))
            v.wait_ge(sem(L.last), L.value(L.last))
            v.tensor_tensor(s_u[:, 3], s_qkv[:, 2], s_u[:, 3], ALU.subtract
            ).then_inc(sem("dve_order"), L.add("dve_order"))
            v.wait_ge(sem(L.last), L.value(L.last))
            v.tensor_tensor(s_u[:, 5], s_u[:, 3], gate(0), ALU.mult).then_inc(sem("s_v_ready"), L.add("s_v_ready"))
            v.wait_ge(sem(L.last), L.value(L.last))
            v.tensor_tensor(s_u[:, 2], psum[:, 4, 2 * NS:3 * NS], s_u[:, 5], ALU.mult
            ).then_inc(sem("bank4_free"), L.add("bank4_free"))
            v.wait_ge(sem(L.last), L.value(L.last))
            v.tensor_tensor(s_u[:, 4], s_u[:, 4], s_u[:, 2], ALU.add).then_inc(sem("dve_order"), L.add("dve_order"))
            v.wait_ge(sem(L.last), L.value(L.last))
            v.tensor_tensor(s_u[:, 7], s_u[:, 4], s_u[:, 4], ALU.mult
            ).then_inc(sem("s_out_squares_ready"), L.add("s_out_squares_ready"))
            v.wait_ge(sem("bank5_free"), L.next("bank5_free"))
            L.skip("bank5_full")
            v.tensor_tensor(s_v_wide[0:NS], b3(ident[0:NS, 0:NS], NS), o3(s_rows[0:NS, 1], NS), ALU.mult
            ).then_inc(sem("s_v_wide_ready"), L.add("s_v_wide_ready"))
            v.tensor_tensor(s_state[:], s_state[:], b3(gate(1), NS), ALU.mult
            ).then_inc(sem("dve_order"), L.add("dve_order"))
            v.wait_ge(sem(L.last), L.value(L.last))
            for h in range(2):
                v.wait_ge(sem(f"bank{6 + h}_full"), L.next(f"bank{6 + h}_full"))
                v.tensor_tensor(s_state[:, hc(h)], s_state[:, hc(h)], psum[:, 6 + h].rearrange("p (c n) -> p c n", n=P),
                                     ALU.add).then_inc(sem(f"bank{6 + h}_free"), L.add(f"bank{6 + h}_free"))
            v.wait_ge(sem("bank3_free"), L.next("bank3_free"))
            L.skip("bank3_full")
            v.reciprocal(s_u[:, 6], s_u[:, 6]).then_inc(sem("s_state_ready"), L.add("s_state_ready"))
            v.wait_ge(sem(L.last), L.value(L.last))
            v.scalar_tensor_tensor(s_u[:, 4], s_u[:, 4], float(P) ** -0.5, s_u[:, 6], ALU.mult, ALU.mult
            ).then_inc(sem("dve_order"), L.add("dve_order"))
            v.wait_ge(sem(L.last), L.value(L.last))
            v.tensor_tensor(s_og[:, one].rearrange("p u n -> p (u n)"), s_u[:, 4], s_z[:], ALU.mult
            ).then_inc(sem("dve_order"), L.add("dve_order"))

        def gdn(head, slots, more):
            hs = bass.ds(head * CH, CH)
            four = "p (c n) -> p c n"
            v.tensor_tensor(inv[:], o3(tri[:], CH), b3(g_keep[:, hs], CH), ALU.mult
            ).then_inc(sem("decay_terms_ready"), L.add("decay_terms_ready"))
            for h in range(2):
                v.wait_ge(sem("bank5_full"), L.next("bank5_full"))
                v.tensor_copy(v_tok[:, hc(h)], psum[:, 5].rearrange(four, n=P)
                ).then_inc(sem("bank5_free"), L.add("bank5_free"))
                v.wait_ge(sem("bank4_free"), L.next("bank4_free"))
                L.skip("bank3_full"), L.skip("bank3_free"), L.skip("bank4_full")
                v.tensor_reduce(col[:, 0, hc(h)], blk[:, 0:4], AXX, ALU.add
                ).then_inc(sem("dve_order"), L.add("dve_order"))
                v.tensor_reduce(col[:, 1, hc(h)], blk[:, 4:8], AXX, ALU.add
                ).then_inc(sem("head_squares_free"), L.add("head_squares_free"))
            for h in range(2):
                v.wait_ge(sem(f"bank{6 + h}_full"), L.next(f"bank{6 + h}_full"))
                v.tensor_tensor(dec[:, hc(h)], psum[:, 6 + h].rearrange(four, n=P),
                                     b3(gt[:, 1, bass.ds(head * CH + 4 * h, 4)], 4), ALU.subtract
                                     ).then_inc(sem(f"bank{6 + h}_free"), L.add(f"bank{6 + h}_free"))
                v.wait_ge(sem(L.last), L.value(L.last))
                v.tensor_tensor(dec[:, hc(h)], dec[:, hc(h)], o3(msk[:], 4), ALU.min
                ).then_inc(sem("decay_args_ready"), L.add("decay_args_ready"))
            v.wait_ge(sem("norms_ready"), L.next("norms_ready"))
            v.reciprocal(col[:, 4:6], col[:, 2:4]).then_inc(sem("dve_order"), L.add("dve_order"))
            v.tensor_tensor(v_tok[:], v_tok[:], b3(col[:, 2], CH), ALU.mult
            ).then_inc(sem("dve_order"), L.add("dve_order"))
            v.wait_ge(sem(L.last), L.value(L.last))
            v.tensor_tensor(col[:, 6], col[:, 4], col[:, 4], ALU.mult).then_inc(sem("dve_order"), L.add("dve_order"))
            v.wait_ge(sem(L.last), L.value(L.last))
            v.tensor_tensor(col[:, 6], col[:, 6], gt[:, 0, hs], ALU.mult
            ).then_inc(sem("dve_order"), L.add("dve_order"))
            v.wait_ge(sem(L.last), L.value(L.last))
            v.tensor_tensor(col[:, 7], col[:, 6], gt[:, 4, hs], ALU.mult
            ).then_inc(sem("dve_order"), L.add("dve_order"))
            v.tensor_scalar(col[:, 5], col[:, 5], float(P) ** -0.5, None, ALU.mult
            ).then_inc(sem("dve_order"), L.add("dve_order"))
            for h in range(2):
                v.wait_ge(sem("decay_ready"), L.next("decay_ready"))
                v.tensor_tensor(blk[:, hc(h)], dec[:, hc(h)], b3(col[:, 6, hc(h)], 4), ALU.mult
                ).then_inc(sem("dve_order"), L.add("dve_order"))
            v.wait_ge(sem(L.last), L.value(L.last))
            for p, b in enumerate((3, 4, 5, 3)):
                v.wait_ge(sem(f"bank{b}_full"), L.next(f"bank{b}_full"))
                both = psum[:, b].rearrange("p (c m n) -> p m c n", m=2, n=P)
                two = slice(2 * p, 2 * p + 2)
                v.tensor_tensor(low[:, two], both[:, 0], blk[:, two], ALU.mult
                ).then_inc(sem("dve_order"), L.add("dve_order"))
                v.tensor_tensor(att[:, two], both[:, 1], dec[:, two], ALU.mult
                ).then_inc(sem(f"bank{b}_free"), L.add(f"bank{b}_free"))
            v.wait_ge(sem(L.last), L.value(L.last))
            v.tensor_tensor(blk[:], low[:], o3(lvl[:, 0], CH), ALU.mult
            ).then_inc(sem("blocks_ready"), L.add("blocks_ready"))
            v.wait_ge(sem(L.last), L.value(L.last))
            v.tensor_tensor(inv_t[:], o3(ident[:], CH), blk[:], ALU.subtract
            ).then_inc(sem("inverse_t_ready"), L.add("inverse_t_ready"))
            for h in range(2):
                v.wait_ge(sem(f"bank{6 + h}_full"), L.next(f"bank{6 + h}_full"))
                v.tensor_tensor(inv[:, hc(h)], o3(ident[:], 4), psum[:, 6 + h].rearrange(four, n=P), ALU.subtract
                ).then_inc(sem(f"bank{6 + h}_free"), L.add(f"bank{6 + h}_free"))
            v.wait_ge(sem(L.last), L.value(L.last))
            v.tensor_tensor(blk[:], low[:], o3(lvl[:, 1], CH), ALU.mult
            ).then_inc(sem("blocks_ready"), L.add("blocks_ready"))
            if more:
                take_product(2)
            for level in range(1, LEVELS + 1):
                for h in range(2):
                    v.wait_ge(sem(f"bank{3 + h}_full"), L.next(f"bank{3 + h}_full"))
                    L.skip(f"bank{3 + h}_free")
                if level < LEVELS:
                    v.tensor_tensor(blk[:], low[:], o3(lvl[:, level + 1], CH), ALU.mult
                    ).then_inc(sem("blocks_ready"), L.add("blocks_ready"))
                v.wait_ge(sem(L.last), L.value(L.last))
                for h in range(2):
                    if level < LEVELS:
                        v.wait_ge(sem(f"bank{5 + h}_full"), L.next(f"bank{5 + h}_full"))
                        v.tensor_tensor(inv[:, hc(h)], inv[:, hc(h)], psum[:, 5 + h].rearrange(four, n=P),
                                             ALU.subtract
                                             ).then_inc(sem(f"bank{5 + h}_free"), L.add(f"bank{5 + h}_free"))
                    b = (7, 3)[h]
                    v.wait_ge(sem(f"bank{b}_full"), L.next(f"bank{b}_full"))
                    v.tensor_tensor(inv_t[:, hc(h)], inv_t[:, hc(h)], psum[:, b].rearrange(four, n=P),
                                         ALU.subtract).then_inc(sem(f"bank{b}_free"), L.add(f"bank{b}_free"))
                if more and level <= 4:
                    which, part = divmod(level - 1, 2)
                    split_lo(2 * head + 4 + which, slots[which], (part,))
                if more and level == 3:
                    take_product(3)
            if more:
                take_product(4)
            v.wait_ge(sem(L.last), L.value(L.last))
            v.memset(state[:], 0.0).then_inc(sem("state_ready"), L.add("state_ready"))
            for c in range(CH):
                one = bass.ds(head * CH + c, 1)
                v.wait_ge(sem("bank4_full"), L.next("bank4_full"))
                v.wait_ge(sem(L.last), L.value(L.last))
                v.scalar_tensor_tensor(vz[:, 0], psum[:, 4, 0:P], gt[:, 3, one], v_tok[:, c], ALU.mult, ALU.add
                ).then_inc(sem("bank4_free"), L.add("bank4_free"))
                v.wait_ge(sem("bank5_full"), L.next("bank5_full"))
                v.tensor_scalar(vz[:, 2], psum[:, 5, 0:P], col[:, 7, c:c + 1], None, ALU.mult
                ).then_inc(sem("v_for_state_ready"), L.add("v_for_state_ready"))
                v.tensor_scalar(vz[:, 1], psum[:, 5, 0:P], col[:, 6, c:c + 1], None, ALU.mult
                ).then_inc(sem("bank5_free"), L.add("bank5_free"))
                v.wait_ge(sem("bank3_full"), L.next("bank3_full"))
                v.scalar_tensor_tensor(state[:], state[:], gt[:, 5, one], psum[:, 3, 0:P], ALU.mult, ALU.add
                ).then_inc(sem("bank3_free"), L.add("bank3_free"))
                v.wait_ge(sem("bank6_free"), L.next("bank6_free"))
                L.skip("bank6_full")
                if more and c == 5:
                    take_product(5)
                v.wait_ge(sem("bank7_full"), L.next("bank7_full"))
                v.tensor_tensor(o_tok[:, c], psum[:, 7, 0:P], tmp_o[:], ALU.add
                ).then_inc(sem("bank7_free"), L.add("bank7_free"))
            v.wait_ge(sem(L.last), L.value(L.last))
            v.tensor_tensor(inv[:], o_tok[:], o_tok[:], ALU.mult).then_inc(sem("dve_order"), L.add("dve_order"))
            v.wait_ge(sem(L.last), L.value(L.last))
            v.tensor_reduce(col[:, 8], inv[:], AXX, ALU.add).then_inc(sem("dve_order"), L.add("dve_order"))
            v.tensor_tensor(col[:, 11], col[:, 5], col[:, 5], ALU.mult).then_inc(sem("dve_order"), L.add("dve_order"))
            v.wait_ge(sem(L.last), L.value(L.last))
            v.tensor_tensor(col[:, 9], col[:, 8], col[:, 11], ALU.mult
            ).then_inc(sem("rms_arg_ready"), L.add("rms_arg_ready"))
            v.wait_ge(sem("rms_ready"), L.next("rms_ready"))
            v.reciprocal(col[:, 12], col[:, 10]).then_inc(sem("dve_order"), L.add("dve_order"))
            v.wait_ge(sem(L.last), L.value(L.last))
            v.tensor_tensor(col[:, 13], col[:, 12], col[:, 5], ALU.mult).then_inc(sem("dve_order"), L.add("dve_order"))
            v.wait_ge(sem(L.last), L.value(L.last))
            v.tensor_tensor(o_tok[:], o_tok[:], b3(col[:, 13], CH), ALU.mult
            ).then_inc(sem("o_tok_ready"), L.add("o_tok_ready"))
            v.wait_ge(sem("z_ready"), L.next("z_ready"))
            for h in range(2):
                b = 4 + h
                v.wait_ge(sem(f"bank{b}_full"), L.next(f"bank{b}_full"))
                v.tensor_tensor(head_out[:, hc(h)], psum[:, b].rearrange(four, n=P),
                                     z_g[:, halves[h]].rearrange(four, n=P), ALU.mult
                                     ).then_inc(sem(f"bank{b}_free"), L.add(f"bank{b}_free"))
            if more:
                v.wait_ge(sem(L.last), L.value(L.last))
                take_product(6)
                take_product(7)
            else:
                v.wait_ge(sem("conv_stored"), L.next("conv_stored", 16))
            sample_step(head)
            v.wait_ge(sem("head_output_stored"), L.next("head_output_stored", 16))
            v.wait_ge(sem("state_stored"), L.next("state_stored", 16))
            v.wait_ge(sem(L.last), L.value(L.last))
            v.wait_ge(sem("s_state_stored"), L.next("s_state_stored", 16))

        def step(head, slots, more=True):
            sample_rows(head)
            conv(head)
            if more:
                v.wait_ge(sem(L.last), L.value(L.last))
                take_product(0)
                take_product(1)
            gdn(head, slots, more)

        for n in range(8):
            if n in (1, 4):
                split_lo(2 + (n == 4), 2 + (n == 4))
            take_product(n, first=True)
        with L.loop(HEADS // 2 - 1, "dve heads") as i:
            step(2 * i, (0, 1))
            step(2 * i + 1, (2, 3))
        step(HEADS - 2, (0, 1))
        step(HEADS - 1, (2, 3), more=False)

        for k in range(KT):
            v.tensor_tensor(x[:, k], f(x_hi[:, k]), f(x_lo[:, k]), ALU.add).then_inc(sem("x_back"), L.add("x_back"))
        v.tensor_copy(s_lhs[:, :, 0:NS], s_og[:]).then_inc(sem("dve_order"), L.add("dve_order"))
        v.wait_ge(sem(L.last), L.value(L.last))
        v.tensor_tensor(s_lhs[:, :, NS:2 * NS], s_og[:], f(s_lhs[:, :, 0:NS]), ALU.subtract
        ).then_inc(sem("samples_ready"), L.add("samples_ready"))
        for k in range(KT):
            v.wait_ge(sem("o_hi_ready"), L.next("o_hi_ready"))
            v.tensor_tensor(x_lo[:, k], o_raw[:, k % 2], f(x_hi[:, k]), ALU.subtract
            ).then_inc(sem("o_raw_free"), L.add("o_raw_free"))

        def add_products(n, tile0):
            h, tile = divmod(n, 4)
            v.wait_ge(sem("product_full"), L.next("product_full"))
            out = x[:, tile0 + tile, halves[h]]
            v.tensor_tensor(out, out, psum[:, n % 2], ALU.add).then_inc(sem("product_free"), L.add("product_free"))

        for g in range(2):
            for n in range(8):
                if n in (1, 4):
                    u = 2 * g + 2 + (n == 4)
                    split_lo(U_OUT + u, u % RING)
                add_products(n, 4 * g)
            v.wait_ge(sem("bank3_full"), L.next("bank3_full"))
            out = s_x[:, 4 * g:4 * g + 4]
            v.tensor_tensor(out, out, psum[:, 3, 0:4 * NS].rearrange("p (k n) -> p k n", n=NS), ALU.add
            ).then_inc(sem("bank3_free"), L.add("bank3_free"))
        v.wait_ge(sem(L.last), L.value(L.last))

        def mlp(unit, name, more):
            v.memset(f(u_lhs[:]), 0.0).then_inc(sem("dve_order"), L.add("dve_order"))
            v.memset(s_acc[:], 0.0).then_inc(sem("dve_order"), L.add("dve_order"))
            v.wait_ge(sem(L.last), L.value(L.last))

            def block(b, last=False):
                u = unit + 4 * b
                for n in range(8):
                    if n in (1, 4):
                        split_lo(u + 2 + (n == 4), 2 + (n == 4))
                    h, tile = divmod(n, 4)
                    v.wait_ge(sem("product_full"), L.next("product_full"))
                    v.wait_ge(sem(L.last), L.value(L.last))
                    v.scalar_tensor_tensor(relu[:], psum[:, n % 2], 0.0, rs[:, halves[h]], ALU.max, ALU.mult
                    ).then_inc(sem("product_free"), L.add("product_free"))
                    v.wait_ge(sem(L.last), L.value(L.last))
                    v.tensor_tensor(relu[:], relu[:], relu[:], ALU.mult
                    ).then_inc(sem("relu_square_ready"), L.add("relu_square_ready"))
                    v.wait_ge(sem("u_hi_ready"), L.next("u_hi_ready"))
                    v.tensor_tensor(u_lo[:, tile, halves[h]], relu[:], f(u_hi[:, tile, halves[h]]), ALU.subtract
                    ).then_inc(sem("u_ready"), L.add("u_ready"))
                for j in range(2):
                    for n in range(8):
                        if n == 1 and not last:
                            split_lo(u + 4 + j, j)
                        if n == 3 and j == 0:
                            v.wait_ge(sem("bank3_full"), L.next("bank3_full"))
                            s4 = s_tmp[:, 0, 0:4 * NS].rearrange("p (k n) -> p k n", n=NS)
                            v.scalar_tensor_tensor(s4, psum[:, 3, 0:4 * NS].rearrange("p (k n) -> p k n", n=NS), 0.0,
                                                        o3(s_rs[:], 4), ALU.max, ALU.mult
                                                        ).then_inc(sem("bank3_free"), L.add("bank3_free"))
                            v.wait_ge(sem(L.last), L.value(L.last))
                            v.tensor_tensor(s4, s4, s4, ALU.mult).then_inc(sem("dve_order"), L.add("dve_order"))
                            v.wait_ge(sem(L.last), L.value(L.last))
                            v.tensor_copy(u_lhs[:, :, 0:NS], s4).then_inc(sem("dve_order"), L.add("dve_order"))
                            v.wait_ge(sem(L.last), L.value(L.last))
                            v.tensor_tensor(u_lhs[:, :, NS:2 * NS], s4, f(u_lhs[:, :, 0:NS]), ALU.subtract
                            ).then_inc(sem("u_samples_ready"), L.add("u_samples_ready"))
                        add_products(n, 4 * j)
                    v.wait_ge(sem(f"bank{4 + j}_full"), L.next(f"bank{4 + j}_full"))
                    v.tensor_tensor(s_acc[:, halves[j]], s_acc[:, halves[j]], psum[0:2 * NS, 4 + j], ALU.add
                    ).then_inc(sem(f"bank{4 + j}_free"), L.add(f"bank{4 + j}_free"))
            with L.loop(8 if more else 7, name) as b:
                block(b)
            if not more:
                block(7, last=True)
            v.wait_ge(sem("bank3_full"), L.next("bank3_full"))
            v.tensor_tensor(s_x[:], s_x[:], psum[:, 3, 0:KT * NS].rearrange("p (k n) -> p k n", n=NS), ALU.add
            ).then_inc(sem("bank3_free"), L.add("bank3_free"))
            v.wait_ge(sem(L.last), L.value(L.last))

        def attention_layer():
            norm()
            v.memset(k_mask[HD:P, :, 0], 0.0).then_inc(sem("dve_order"), L.add("dve_order"))
            v.memset(k_mask[0:HD, :, 1], 0.0).then_inc(sem("dve_order"), L.add("dve_order"))
            stored = [0, 0]
            for gi in range(5):
                tiles = 2 if gi == 1 else 4
                for n in range(2 * tiles):
                    if n in (1, tiles):
                        which = n == tiles
                        split_lo(U_KVQ + 2 * gi + 2 + which, (2 * gi + 2 + which) % RING)
                    h, tile = divmod(n, tiles)
                    b = gi - 2 if gi > 1 else 2 * gi + tile // 2
                    d = DIL[b]
                    I = HALF // d

                    def by_class(ap):
                        return ap.rearrange("p (r i) -> p i r", r=d)[:, h * I:(h + 1) * I]
                    src = psum[:, n % 2].rearrange("p (i r) -> p i r", r=d)
                    scale = rs[:, halves[h]].rearrange("p (i r) -> p i r", r=d)
                    v.wait_ge(sem("product_full"), L.next("product_full"))
                    if gi < 2 and tile % 2 == 0:
                        for g in range(2):
                            rows = slice(g * HD, (g + 1) * HD)
                            done = v.tensor_tensor(by_class(k_mask[rows, b, g]), src[rows], scale[rows], ALU.mult)
                            done.then_inc(sem("product_free" if g else "dve_order"), L.add("product_free" if g else "dve_order"))
                    elif gi < 2:
                        v.tensor_tensor(by_class(v_feat[:, b]), src, scale, ALU.mult
                        ).then_inc(sem("product_free"), L.add("product_free"))
                    else:
                        if stored[n % 2]:
                            v.wait_ge(sem(f"q{n % 2}_stored"), L.next(f"q{n % 2}_stored", 16))
                        stored[n % 2] = 1
                        v.scalar_tensor_tensor(q_stage[:, n % 2].rearrange("p (r i) -> p i r", r=d), src, HD ** -0.5,
                                                    scale, ALU.mult, ALU.mult
                                                    ).then_inc(sem("product_free"), L.add("product_free"))
                v.wait_ge(sem("bank3_full"), L.next("bank3_full"))
                rows = psum[:, 3, 0:tiles * NS].rearrange("p (k n) -> p k n", n=NS)
                if gi < 2:
                    v.tensor_tensor(s_kv[:, 4 * gi:4 * gi + tiles], rows, o3(s_rs[:], tiles), ALU.mult
                    ).then_inc(sem("bank3_free"), L.add("bank3_free"))
                else:
                    v.scalar_tensor_tensor(s_q[:, 4 * b:4 * b + 4], rows, HD ** -0.5, o3(s_rs[:], 4), ALU.mult,
                                                ALU.mult).then_inc(sem("bank3_free"), L.add("bank3_free"))
            v.wait_ge(sem(L.last), L.value(L.last))
            v.memset(s_qz[:], 0.0).then_inc(sem("kvq_done"), L.add("kvq_done"))
            skip(3, 4, 3, 4, 3, 4)
            L.skip("bank4_full")
            v.wait_ge(sem(L.last), L.value(L.last))
            for g in range(2):
                rows = slice(g * HD, (g + 1) * HD)
                for b in range(BRANCH):
                    v.tensor_copy(s_qz[rows, b].rearrange("p n (j g) -> p j g n", g=2)[:, :, g],
                                       s_q[rows, 4 * b:4 * b + 4]).then_inc(sem("dve_order"), L.add("dve_order"))
            v.wait_ge(sem("attention_constants_landed"), L.next("attention_constants_landed", 16 * 6))
            for b, at_key in ((1, SA + 64), (2, SA + 81), (0, SA + 82)):
                v.tensor_copy(s_keys[:, :, at_key], s_kv[:, 2 * b]).then_inc(sem("s_keys_ready"), L.add("s_keys_ready"))
            for k in range(4):
                v.wait_ge(sem(f"bank{k}_full"), L.next(f"bank{k}_full"))
                v.tensor_tensor(s_p[:, 2 * k:2 * k + 2],
                                     psum[0:8, k].rearrange("p (n c) -> p n c", c=256)[:, :, 0:SK],
                                     o3(s_bias[:], 2), ALU.add).then_inc(sem(f"bank{k}_free"), L.add(f"bank{k}_free"))
            v.wait_ge(sem(L.last), L.value(L.last))
            v.tensor_reduce(s_pm[:, 0], s_p[:], AXX, ALU.max).then_inc(sem("dve_order"), L.add("dve_order"))
            v.wait_ge(sem(L.last), L.value(L.last))
            v.tensor_tensor(s_p[:], s_p[:], b3(s_pm[:, 0], NS, SK), ALU.subtract
            ).then_inc(sem("s_scores_ready"), L.add("s_scores_ready"))
            v.wait_ge(sem("s_exp_ready"), L.next("s_exp_ready"))
            v.tensor_reduce(s_pm[:, 1], s_p[:], AXX, ALU.add).then_inc(sem("dve_order"), L.add("dve_order"))
            v.wait_ge(sem(L.last), L.value(L.last))
            v.reciprocal(s_pm[:, 0], s_pm[:, 1]).then_inc(sem("dve_order"), L.add("dve_order"))
            v.wait_ge(sem(L.last), L.value(L.last))
            v.tensor_tensor(s_p[:], s_p[:], b3(s_pm[:, 0], NS, SK), ALU.mult
            ).then_inc(sem("s_probs_ready"), L.add("s_probs_ready"))
            skip(4, 5)
            v.wait_ge(sem("bank6_full"), L.next("bank6_full"))
            s_out = s_tmp[:, 3, 0:4 * NS].rearrange("p (j n) -> p j n", n=NS)
            for g in range(2):
                rows = slice(g * HD, (g + 1) * HD)
                v.tensor_copy(s_out[rows], psum[rows, 6, 0:8 * NS].rearrange("p (n j g) -> p g j n", j=4, g=2)[:, g]
                ).then_inc(sem("bank6_free" if g else "dve_order"), L.add("bank6_free" if g else "dve_order"))

            def bias_of(b):
                v.wait_ge(sem(L.last), L.value(L.last))
                for kt, which in (((0, 0), (1, 1)) if b < 2 else ((1, 2),)):
                    v.tensor_tensor(bias[:, :, kt * P:(kt + 1) * P], o3(dist[:, which], 8), b3(slopes[:, b], 8),
                                         ALU.mult).then_inc(sem("dve_order"), L.add("dve_order"))
                v.wait_ge(sem(L.last), L.value(L.last))

            def tile_step(b, tile, par, nk, place):
                cols = slice((2 - nk) * P, 2 * P)
                v.wait_ge(sem(f"out{par}_stored"), L.next(f"out{par}_stored", 32))
                for j in range(4):
                    v.wait_ge(sem(f"bank{j}_full"), L.next(f"bank{j}_full"))
                    two = slice(2 * j, 2 * j + 2)
                    v.tensor_tensor(prob[:, two, cols], psum[:, j].rearrange("p (g c) -> p g c", g=2)[:, :, cols],
                                         bias[:, two, cols], ALU.add
                                         ).then_inc(sem(f"bank{j}_free"), L.add(f"bank{j}_free"))
                    if j % 2:
                        hs = j // 2
                        big = o_out[:, par, 8 * HD + 4 * hs:8 * HD + 4 * hs + 4]
                        v.wait_ge(sem(L.last), L.value(L.last))
                        v.tensor_reduce(big, prob[:, hc(hs), cols], AXX, ALU.max
                        ).then_inc(sem("dve_order"), L.add("dve_order"))
                        v.wait_ge(sem(L.last), L.value(L.last))
                        v.tensor_scalar(neg_max[:, hc(hs)], big, -1.0, None, ALU.mult
                        ).then_inc(sem("max_ready"), L.add("max_ready"))
                for hs in range(2):
                    if nk == 2:
                        skip(4)
                    v.wait_ge(sem("bank5_full"), L.next("bank5_full"))
                    v.tensor_copy(prob_t[:, 1, hc(hs)], psum[:, 5].rearrange("p (c n) -> p c n", n=P)
                    ).then_inc(sem("bank5_free"), L.add("bank5_free"))
                for hs in range(2):
                    v.wait_ge(sem(f"bank{6 + hs}_full"), L.next(f"bank{6 + hs}_full"))
                    for g in range(2):
                        dst = o_out[:, par, 0:8 * HD].rearrange("p (g j d) -> p g j d", g=2, j=4)[:, g, 2 * hs:2 * hs + 2]
                        src = psum[:, 6 + hs].rearrange("p (j g c) -> p g j c", g=2, c=P)[:, g, :, g * HD:(g + 1) * HD]
                        v.tensor_copy(dst, src
                        ).then_inc(sem(("bank6_free", "out_taken")[hs] if g else "dve_order"), L.add(("bank6_free", "out_taken")[hs] if g else "dve_order"))

            tiles_of(L, "dve", tile_step, before=bias_of)
            v.wait_ge(sem(L.last), L.value(L.last))
            with L.loop(CH // 2, "dve merge") as i:
                for par in range(2):
                    v.wait_ge(sem(f"merge{par}_landed"), L.next(f"merge{par}_landed", 16))
                    big = merge[:, par, :, 8 * HD:8 * HD + 8]
                    total = share[:, 4]
                    v.tensor_tensor(total[:, 0], big[:, 0], big[:, 1], ALU.max
                    ).then_inc(sem("dve_order"), L.add("dve_order"))
                    v.wait_ge(sem(L.last), L.value(L.last))
                    v.tensor_tensor(total[:, 0], total[:, 0], big[:, 2], ALU.max
                    ).then_inc(sem("dve_order"), L.add("dve_order"))
                    v.wait_ge(sem(L.last), L.value(L.last))
                    v.tensor_tensor(share[:, 0], big, o3(total[:, 0], 3), ALU.subtract
                    ).then_inc(sem("share_args_ready"), L.add("share_args_ready"))
                    v.wait_ge(sem("shares_ready"), L.next("shares_ready"))
                    v.tensor_tensor(share[:, 2], share[:, 1], merge[:, par, :, 8 * HD + 8:], ALU.mult
                    ).then_inc(sem("dve_order"), L.add("dve_order"))
                    v.wait_ge(sem(L.last), L.value(L.last))
                    v.tensor_tensor(total[:, 1], share[:, 2, 0], share[:, 2, 1], ALU.add
                    ).then_inc(sem("dve_order"), L.add("dve_order"))
                    v.wait_ge(sem(L.last), L.value(L.last))
                    v.tensor_tensor(total[:, 1], total[:, 1], share[:, 2, 2], ALU.add
                    ).then_inc(sem("dve_order"), L.add("dve_order"))
                    v.wait_ge(sem(L.last), L.value(L.last))
                    v.reciprocal(total[:, 2], total[:, 1]).then_inc(sem("dve_order"), L.add("dve_order"))
                    v.wait_ge(sem(L.last), L.value(L.last))
                    v.tensor_tensor(share[:, 3], share[:, 1], o3(total[:, 2], 3), ALU.mult
                    ).then_inc(sem("dve_order"), L.add("dve_order"))
                    v.wait_ge(sem(L.last), L.value(L.last))
                    out = merged[:, par].rearrange("p (j g d) -> p j g d", g=2, d=HD)
                    part = prob[:, 0:2].rearrange("p a c -> p (a c)").rearrange("p (j g d) -> p j g d", g=2, d=HD)
                    for b in range(BRANCH):
                        w = share[:, 3, b].rearrange("p (j g) -> p j g", g=2).unsqueeze(3).to_broadcast([P, 4, 2, HD])
                        v.tensor_tensor(part if b else out,
                                             merge[:, par, b, 0:8 * HD].rearrange("p (g j d) -> p j g d", g=2, j=4), w,
                                             ALU.mult
                                             ).then_inc(sem("merge_free" if b == 2 else "dve_order"), L.add("merge_free" if b == 2 else "dve_order"))
                        if b:
                            v.wait_ge(sem(L.last), L.value(L.last))
                            v.tensor_tensor(out, out, part, ALU.add
                            ).then_inc(sem("merged_ready" if b == 2 else "dve_order"), L.add("merged_ready" if b == 2 else "dve_order"))
                        if b == 1:
                            v.wait_ge(sem(L.last), L.value(L.last))
                    v.wait_ge(sem("u_hi_ready"), L.next("u_hi_ready"))
                    toks = bass.ds((2 * i + par) * P, P)
                    L.skip(f"bank{4 + par}_full")
                    v.tensor_tensor(u_lo[:, :, toks], psum[:, 4 + par].rearrange("p (c n) -> p c n", n=P),
                                         f(u_hi[:, :, toks]), ALU.subtract
                                         ).then_inc(sem(f"bank{4 + par}_free"), L.add(f"bank{4 + par}_free"))
                    v.wait_ge(sem(L.last), L.value(L.last))
            v.memset(f(u_lhs[:]), 0.0).then_inc(sem("dve_order"), L.add("dve_order"))
            v.wait_ge(sem(L.last), L.value(L.last))
            v.tensor_copy(u_lhs[:, :, 0:NS], s_out).then_inc(sem("dve_order"), L.add("dve_order"))
            v.wait_ge(sem(L.last), L.value(L.last))
            v.tensor_tensor(u_lhs[:, :, NS:2 * NS], s_out, f(u_lhs[:, :, 0:NS]), ALU.subtract
            ).then_inc(sem("u_samples_ready"), L.add("u_samples_ready"))
            for j in range(2):
                for n in range(8):
                    if n == 1:
                        split_lo(U_MLP1 + j, j)
                    add_products(n, 4 * j)
                v.wait_ge(sem(f"bank{4 + j}_full"), L.next(f"bank{4 + j}_full"))
                v.tensor_copy(s_acc[:, halves[j]], psum[0:2 * NS, 4 + j]
                ).then_inc(sem(f"bank{4 + j}_free"), L.add(f"bank{4 + j}_free"))
            v.wait_ge(sem("bank3_full"), L.next("bank3_full"))
            v.tensor_tensor(s_x[:], s_x[:], psum[:, 3, 0:KT * NS].rearrange("p (k n) -> p k n", n=NS), ALU.add
            ).then_inc(sem("bank3_free"), L.add("bank3_free"))
            v.wait_ge(sem(L.last), L.value(L.last))

        norm()
        mlp(U_MLP0, "dve mlp0", True)
        attention_layer()
        norm()
        mlp(U_MLP1, "dve mlp1", False)
        norm(split=False)
        for k in range(KT):
            v.scalar_tensor_tensor(x[:, k], x[:, k], g_fin[:, k:k + 1], rs[:], ALU.mult, ALU.mult
            ).then_inc(sem("y_ready"), L.add("y_ready"))
        v.tensor_tensor(s_x[:], s_x[:], o3(s_rs[:], KT), ALU.mult).then_inc(sem("dve_order"), L.add("dve_order"))
        v.wait_ge(sem(L.last), L.value(L.last))
        v.tensor_tensor(s_x[:], s_x[:], b3(g_fin[:], KT, NS), ALU.mult).then_inc(sem("y_ready"), L.add("y_ready"))

    @block.tensor
    def _(pe):
        L = Lane(pe, sem, room=["product_free", "sample_free", "out_taken"] + [f"bank{b}_free" for b in range(8)])
        mm = nc.tensor.matmul

        def product(n, slots, tile, h, xh, xl, kts, width=P):
            pe.wait_ge(sem("product_free"), L.next("product_free"))
            for k in range(kts):
                slot, kk = slots[k // UW], k % UW
                whi = w_hi[:, slot, kk, tile * P:(tile + 1) * P]
                wlo = w_lo[:, slot, kk, tile * P:(tile + 1) * P]
                mm(psum[:, n % 2], whi, xh[:, k, halves[h]], start=k == 0, stop=False)
                mm(psum[:, n % 2], whi, xl[:, k, halves[h]], start=False, stop=False)
                done = mm(psum[:, n % 2], wlo, xh[:, k, halves[h]], start=False, stop=k == kts - 1)
            done.then_inc(sem("product_full"), L.add("product_full"))

        def sample_product(slots, kts, lhs, name, bank):
            for k in range(kts):
                slot, kk = slots[k // UW], k % UW
                mm(psum[:, bank], lhs[:, k], w_hi[:, slot, kk], start=k == 0, stop=False)
                done = mm(psum[:, bank], lhs[:, k], w_lo[:, slot, kk], start=False, stop=k == kts - 1)
            done.then_inc(sem(name), L.add(name))

        def transposes(bank, pairs, began=None):
            pe.wait_ge(sem(f"bank{bank}_free"), L.next(f"bank{bank}_free"))
            at_col = 0
            for src in pairs:
                rows, cols = src.shape[0], src.shape[1]
                done = nc.tensor.transpose(psum[0:cols, bank, at_col:at_col + rows], src, ident[0:rows, 0:rows])
                if began and at_col == 0:
                    done.then_inc(sem(began), L.add(began))
                at_col += rows
            done.then_inc(sem(f"bank{bank}_full"), L.add(f"bank{bank}_full"))

        def fold_samples(bank, rows, tiles):
            pe.wait_ge(sem(f"bank{bank}_free"), L.next(f"bank{bank}_free"))
            for n in range(tiles):
                done = mm(psum[:, bank, n * NS:(n + 1) * NS], rows[:, n * P:(n + 1) * P], fold[:], start=True, stop=True)
            done.then_inc(sem(f"bank{bank}_full"), L.add(f"bank{bank}_full"))

        def norm(split=True):
            pe.wait_ge(sem("sample_squares_ready"), L.next("sample_squares_ready"))
            pe.wait_ge(sem("bank5_free"), L.next("bank5_free"))
            mm(psum[:, 5, 0:NS], ones[:], s_tmp[:, 1, 0:NS], start=True, stop=True
            ).then_inc(sem("bank5_full"), L.add("bank5_full"))
            pe.wait_ge(sem("square_free"), L.next("square_free", KT))
            for h in range(2):
                pe.wait_ge(sem(f"bank{3 + h}_free"), L.next(f"bank{3 + h}_free"))
                mm(psum[:, 3 + h], ones[:], sq_sum[:, halves[h]], start=True, stop=True
                ).then_inc(sem(f"bank{3 + h}_full"), L.add(f"bank{3 + h}_full"))

        pe.wait_ge(sem("ones_set"), L.next("ones_set"))
        pe.wait_ge(sem("constants_landed"), L.next("constants_landed", 16 * len(CONSTS)))
        pe.wait_ge(sem("w_ab_ready"), L.next("w_ab_ready"))
        pe.wait_ge(sem("x_landed"), L.next("x_landed", 16 * KT))
        norm()
        for h in range(2):
            pe.wait_ge(sem(f"bank{3 + h}_free"), L.next(f"bank{3 + h}_free"))
            for k in range(KT):
                done = mm(psum[0:2 * HEADS, 3 + h], w_ab[:, k], x[:, k, halves[h]], start=k == 0, stop=k == KT - 1)
            done.then_inc(sem(f"bank{3 + h}_full"), L.add(f"bank{3 + h}_full"))
        pe.wait_ge(sem("bank5_free"), L.next("bank5_free"))
        for k in range(KT):
            done = mm(psum[0:2 * HEADS, 5, 0:NS], w_ab[:, k], s_x[:, k], start=k == 0, stop=k == KT - 1)
        done.then_inc(sem("bank5_full"), L.add("bank5_full"))
        pe.wait_ge(sem("bank3_free"), L.value("bank3_free"))
        pe.wait_ge(sem("bank3_free"), L.next("bank3_free")), pe.wait_ge(sem("bank4_free"), L.next("bank4_free"))
        transposes(5, [ab_feat[:, c * P:(c + 1) * P] for c in range(CH)])
        pe.wait_ge(sem("s_wide_ready"), L.next("s_wide_ready"))
        pe.wait_ge(sem("bank5_free"), L.next("bank5_free"))
        mm(psum[:, 5, 0:P], ones[0:2 * HEADS], s_wide[:].rearrange("p m n -> p (m n)"), start=True, stop=True
        ).then_inc(sem("bank5_full"), L.add("bank5_full"))
        pe.wait_ge(sem("g_ready"), L.next("g_ready"))
        pe.wait_ge(sem("bank6_free"), L.next("bank6_free"))
        mm(psum[:, 6, 0:64], tri[:], ab[:, 3, 0:64], start=True, stop=True
        ).then_inc(sem("bank6_full"), L.add("bank6_full"))
        pe.wait_ge(sem("bank7_free"), L.next("bank7_free"))
        mm(psum[:, 7, 0:64], ones[:], ab[:, 3, 0:64], start=True, stop=True
        ).then_inc(sem("bank7_full"), L.add("bank7_full"))
        L.skip("bank3_free", -1), L.skip("bank4_free", -1)

        pe.wait_ge(sem("x_ready"), L.next("x_ready", KT))
        pe.wait_ge(sem("samples_ready"), L.next("samples_ready"))

        def dense_quarters(first, last, slots):
            if slots is None:
                return
            for m in range(first, last):
                n, quarter = divmod(m, 4)
                tile, h = divmod(n, 2)
                if quarter == 0:
                    pe.wait_ge(sem("product_free"), L.next("product_free"))
                for k in (2 * quarter, 2 * quarter + 1):
                    slot, kk = slots[k // UW], k % UW
                    whi = w_hi[:, slot, kk, tile * P:(tile + 1) * P]
                    wlo = w_lo[:, slot, kk, tile * P:(tile + 1) * P]
                    mm(psum[:, n % 2], whi, x_hi[:, k, halves[h]], start=k == 0, stop=False)
                    mm(psum[:, n % 2], whi, x_lo[:, k, halves[h]], start=False, stop=False)
                    done = mm(psum[:, n % 2], wlo, x_hi[:, k, halves[h]], start=False, stop=k == KT - 1)
                if quarter == 3:
                    done.then_inc(sem("product_full"), L.add("product_full"))

        def samples_in(slots):
            pe.wait_ge(sem("sample_free"), L.next("sample_free"))
            sample_product(slots, KT, s_lhs, "sample_full", 2)

        def gdn(slots):
            pe.wait_ge(sem("sample_free"), L.next("sample_free"))
            L.skip("sample_free", -1)
            fold_samples(3, s_tok, 4)
            if slots:
                pe.wait_ge(sem("raw_free"), L.next("raw_free", 4))
            dense_quarters(0, 8, slots)
            pe.wait_ge(sem("qkv_ready"), L.next("qkv_ready", 3))
            for h in range(2):
                for b, n in ((3, 1), (4, 0), (5, 2)):
                    transposes(b, [qkv[:, n, (4 * h + c) * P:(4 * h + c + 1) * P] for c in range(4)])
            pe.wait_ge(sem("decay_terms_ready"), L.next("decay_terms_ready"))
            for h in range(2):
                pe.wait_ge(sem(f"bank{6 + h}_free"), L.next(f"bank{6 + h}_free"))
                mm(psum[:, 6 + h], ones[:], inv[:, hc(h)], start=True, stop=True
                ).then_inc(sem(f"bank{6 + h}_full"), L.add(f"bank{6 + h}_full"))
            for p, b in enumerate((3, 4, 5, 3)):
                pe.wait_ge(sem(f"bank{b}_free"), L.next(f"bank{b}_free"))
                for c in (2 * p, 2 * p + 1):
                    lo = (c % 2) * 2 * P
                    toks = slice(c * P, (c + 1) * P)
                    mm(psum[:, b, lo:lo + P], qkv[:, 1, toks], qkv[:, 1, toks], start=True, stop=True)
                    done = mm(psum[:, b, lo + P:lo + 2 * P], qkv[:, 1, toks], qkv[:, 0, toks], start=True, stop=True)
                done.then_inc(sem(f"bank{b}_full"), L.add(f"bank{b}_full"))
            dense_quarters(8, 14, slots)
            pe.wait_ge(sem("blocks_ready"), L.next("blocks_ready"))
            for h in range(2):
                transposes(6 + h, [blk[:, 4 * h + c] for c in range(4)])
            pe.wait_ge(sem("inverse_t_ready"), L.next("inverse_t_ready"))

            def four(bank, h, lhs, rhs):
                pe.wait_ge(sem(f"bank{bank}_free"), L.next(f"bank{bank}_free"))
                for c in range(4):
                    done = mm(psum[:, bank, c * P:(c + 1) * P], lhs[:, 4 * h + c], rhs[:, 4 * h + c], start=True, stop=True)
                done.then_inc(sem(f"bank{bank}_full"), L.add(f"bank{bank}_full"))
            for level in range(1, LEVELS + 1):
                pe.wait_ge(sem("blocks_ready"), L.next("blocks_ready"))
                if level == 1:
                    pe.wait_ge(sem("bank6_free"), L.next("bank6_free")), pe.wait_ge(sem("bank7_free"), L.next("bank7_free"))
                    L.skip("bank6_free", -1), L.skip("bank7_free", -1)
                for h in range(2):
                    if level > 1:
                        pe.wait_ge(sem(f"bank{5 + h}_free"), L.next(f"bank{5 + h}_free"))
                        L.skip(f"bank{5 + h}_free", -1)
                    four(3 + h, h, blk, inv)
                for h in range(2):
                    pe.wait_ge(sem(f"bank{3 + h}_free"), L.next(f"bank{3 + h}_free"))
                    L.skip(f"bank{3 + h}_free", -1)
                    if h == 0:
                        pe.wait_ge(sem("bank7_free"), L.next("bank7_free"))
                        L.skip("bank7_free", -1)
                    if level < LEVELS:
                        four(5 + h, h, inv_t, prod)
                    four((7, 3)[h], h, prod, inv_t)
                dense_quarters(13 + level, 14 + level, slots)
            for c in range(CH):
                toks = slice(c * P, (c + 1) * P)
                if c == 0:
                    pe.wait_ge(sem("state_ready"), L.next("state_ready"))
                else:
                    pe.wait_ge(sem("bank3_free"), L.next("bank3_free"))
                    L.skip("bank3_free", -1)
                for b, lhs, rhs in ((4, qkv[:, 1, toks], state[:]), (6, qkv[:, 0, toks], state[:])):
                    pe.wait_ge(sem(f"bank{b}_free"), L.next(f"bank{b}_free"))
                    mm(psum[:, b, 0:P], lhs, rhs, start=True, stop=True
                    ).then_inc(sem(f"bank{b}_full"), L.add(f"bank{b}_full"))
                dense_quarters(20 + c, 21 + c, slots)
                pe.wait_ge(sem("bank4_free"), L.next("bank4_free"))
                L.skip("bank4_free", -1)
                pe.wait_ge(sem("bank5_free"), L.next("bank5_free"))
                mm(psum[:, 5, 0:P], inv_t[:, c], vz[:, 0], start=True, stop=True
                ).then_inc(sem("bank5_full"), L.add("bank5_full"))
                pe.wait_ge(sem("v_for_state_ready"), L.next("v_for_state_ready"))
                pe.wait_ge(sem("bank3_free"), L.next("bank3_free"))
                mm(psum[:, 3, 0:P], k_tok[:, c], vz[:, 2], start=True, stop=True
                ).then_inc(sem("bank3_full"), L.add("bank3_full"))
                pe.wait_ge(sem("bank5_free"), L.next("bank5_free"))
                L.skip("bank5_free", -1)
                pe.wait_ge(sem("bank7_free"), L.next("bank7_free"))
                mm(psum[:, 7, 0:P], att[:, c], vz[:, 1], start=True, stop=True
                ).then_inc(sem("bank7_full"), L.add("bank7_full"))
            dense_quarters(28, 32, slots)
            pe.wait_ge(sem("o_tok_ready"), L.next("o_tok_ready"))
            for h in range(2):
                transposes(4 + h, [o_tok[:, 4 * h + c] for c in range(4)])
            pe.wait_ge(sem("s_squares_ready"), L.next("s_squares_ready"))
            pe.wait_ge(sem("bank3_free"), L.next("bank3_free"))
            mm(psum[:, 3, 0:2 * NS], ones[:], s_u[:, 2:4].rearrange("p k n -> p (k n)"), start=True, stop=True
            ).then_inc(sem("bank3_full"), L.add("bank3_full"))
            pe.wait_ge(sem("s_qk_ready"), L.next("s_qk_ready"))
            pe.wait_ge(sem("s_state_landed"), L.next("s_state_landed", 16))
            pe.wait_ge(sem("bank4_free"), L.next("bank4_free"))
            for n in range(NS):
                mm(psum[:, 4, 2 * n:2 * n + 2], s_state[:, n], s_qkv[:, 0:2, n], start=True, stop=True)
            mm(psum[:, 4, 2 * NS:3 * NS], ones[:], s_u[:, 2], start=True, stop=True
            ).then_inc(sem("bank4_full"), L.add("bank4_full"))
            pe.wait_ge(sem("s_v_ready"), L.next("s_v_ready"))
            pe.wait_ge(sem("bank5_free"), L.next("bank5_free"))
            mm(psum[0:NS, 5, 0:P], s_qkv[:, 1], ident[:], start=True, stop=True)
            mm(psum[0:NS, 5, P:2 * P], s_u[:, 5], ident[:], start=True, stop=True
            ).then_inc(sem("bank5_full"), L.add("bank5_full"))
            if slots:
                samples_in(slots)
            pe.wait_ge(sem("s_v_wide_ready"), L.next("s_v_wide_ready"))
            for h in range(2):
                pe.wait_ge(sem(f"bank{6 + h}_free"), L.next(f"bank{6 + h}_free"))
                mm(psum[:, 6 + h], s_rows[0:NS, 0], s_v_wide[0:NS, hc(h)], start=True, stop=True
                ).then_inc(sem(f"bank{6 + h}_full"), L.add(f"bank{6 + h}_full"))
            pe.wait_ge(sem("s_out_squares_ready"), L.next("s_out_squares_ready"))
            pe.wait_ge(sem("bank3_free"), L.next("bank3_free"))
            mm(psum[:, 3, 0:NS], ones[:], s_u[:, 7], start=True, stop=True
            ).then_inc(sem("bank3_full"), L.add("bank3_full"))

        pe.wait_ge(sem("raw_free"), L.next("raw_free", 4))
        dense_quarters(0, 32, (0, 1))
        samples_in((0, 1))
        with L.loop(HEADS // 2 - 1, "pe heads"):
            gdn((2, 3))
            gdn((0, 1))
        gdn((2, 3))
        gdn(None)

        pe.wait_ge(sem("samples_ready"), L.next("samples_ready"))
        pe.wait_ge(sem("o_raw_free"), L.next("o_raw_free", KT))
        for g in range(2):
            pe.wait_ge(sem("raw_free"), L.next("raw_free", 4))
            for n in range(8):
                h, tile = divmod(n, 4)
                product(n, ((0, 1), (2, 3))[g], tile, h, x_hi, x_lo, KT)
            pe.wait_ge(sem("sample_free"), L.next("sample_free"))
            sample_product(((0, 1), (2, 3))[g], KT, s_lhs, "sample_full", 2)
            pe.wait_ge(sem("sample_free"), L.next("sample_free")), L.skip("sample_free", -1)
            fold_samples(3, s_tok, 4)

        def mlp(name, more):
            def block():
                pe.wait_ge(sem("raw_free"), L.next("raw_free", 4))
                for n in range(8):
                    h, tile = divmod(n, 4)
                    product(n, (0, 1), tile, h, x_hi, x_lo, KT)
                pe.wait_ge(sem("sample_free"), L.next("sample_free"))
                sample_product((0, 1), KT, s_lhs, "sample_full", 2)
                for j in range(2):
                    pe.wait_ge(sem("raw_free"), L.next("raw_free", 2))
                    for n in range(8):
                        h, tile = divmod(n, 4)
                        if j == 0 and n in (0, 4):
                            pe.wait_ge(sem("u_ready"), L.next("u_ready", 4))
                        product(n, (2 + j,), tile, h, u_hi, u_lo, UW)
                        if j == 0 and n == 1:
                            pe.wait_ge(sem("sample_free"), L.next("sample_free")), L.skip("sample_free", -1)
                            fold_samples(3, s_tok, 4)
                    if j == 0:
                        pe.wait_ge(sem("u_samples_ready"), L.next("u_samples_ready"))
                    pe.wait_ge(sem(f"bank{4 + j}_free"), L.next(f"bank{4 + j}_free"))
                    sample_product((2 + j,), UW, u_lhs, f"bank{4 + j}_full", 4 + j)
            pe.wait_ge(sem("x_ready"), L.next("x_ready", KT))
            pe.wait_ge(sem("samples_ready"), L.next("samples_ready"))
            with L.loop(8 if more else 7, name):
                block()
            if not more:
                block()
            for bank in (4, 5):
                pe.wait_ge(sem(f"bank{bank}_free"), L.next(f"bank{bank}_free")), L.skip(f"bank{bank}_free", -1)
            fold_samples(3, s_acc, KT)

        def attention_layer():
            norm()
            pe.wait_ge(sem("x_ready"), L.next("x_ready", KT))
            pe.wait_ge(sem("samples_ready"), L.next("samples_ready"))
            for gi in range(5):
                tiles = 2 if gi == 1 else 4
                slots = ((0, 1), (2, 3))[gi % 2]
                pe.wait_ge(sem("raw_free"), L.next("raw_free", 4))
                for n in range(2 * tiles):
                    h, tile = divmod(n, tiles)
                    product(n, slots, tile, h, x_hi, x_lo, KT)
                pe.wait_ge(sem("sample_free"), L.next("sample_free"))
                sample_product(slots, KT, s_lhs, "sample_full", 2)
                pe.wait_ge(sem("sample_free"), L.next("sample_free")), L.skip("sample_free", -1)
                fold_samples(3, s_tok, tiles)
            pe.wait_ge(sem("kvq_done"), L.next("kvq_done"))
            for b in range(BRANCH):
                for h in range(2):
                    transposes(3 + h, [v_feat[:, b, (4 * h + c) * P:(4 * h + c + 1) * P] for c in range(4)])
            pe.wait_ge(sem("bank4_free"), L.next("bank4_free"))
            for b in range(BRANCH):
                done = mm(psum[0:NS, 4, b * P:(b + 1) * P], s_kv[:, 2 * b + 1], ident[:], start=True, stop=True)
            done.then_inc(sem("bank4_full"), L.add("bank4_full"))
            pe.wait_ge(sem("s_keys_ready"), L.next("s_keys_ready", 3))
            pe.wait_ge(sem("product_free"), L.next("product_free", 2)), L.skip("product_free", -2)
            for n in range(NS):
                k, lo = n // 2, (n % 2) * 256
                if n % 2 == 0:
                    pe.wait_ge(sem(f"bank{k}_free"), L.next(f"bank{k}_free"))
                for b, first, last in ((0, 0, SA), (1, SA, SA + 65), (2, SA + 65, SA + 82), (0, SA + 82, SK)):
                    done = mm(psum[0:8, k, lo + first:lo + last], s_qz[:, b, n], s_keys[:, n, first:last],
                              start=True, stop=True)
                if n % 2:
                    done.then_inc(sem(f"bank{k}_full"), L.add(f"bank{k}_full"))
            pe.wait_ge(sem("s_probs_ready"), L.next("s_probs_ready"))
            for bank, first, last in ((4, 0, SA), (5, SA, SK)):
                pe.wait_ge(sem("bank5_free" if bank == 5 else "s_vrow_ready"), L.next("bank5_free" if bank == 5 else "s_vrow_ready"))
                for n in range(NS):
                    done = nc.tensor.transpose(psum[0:last - first, bank, 8 * n:8 * n + 8], s_p[:, n, first:last],
                                               ident[0:8, 0:8])
                done.then_inc(sem(f"bank{bank}_full"), L.add(f"bank{bank}_full"))
            pe.wait_ge(sem("s_vown_landed"), L.next("s_vown_landed", 48))
            for bank in (4, 5):
                pe.wait_ge(sem(f"bank{bank}_free"), L.next(f"bank{bank}_free")), L.skip(f"bank{bank}_free", -1)
            pe.wait_ge(sem("bank6_free"), L.next("bank6_free"))
            for n in range(NS):
                mm(psum[:, 6, 8 * n:8 * n + 8], s_va[:, n], s_pt[:, 0, 8 * n:8 * n + 8], start=True, stop=False)
                done = mm(psum[:, 6, 8 * n:8 * n + 8], s_vb[:, n], s_pt[0:SB, 1, 8 * n:8 * n + 8], start=False, stop=True)
            done.then_inc(sem("bank6_full"), L.add("bank6_full"))

            def tile_step(b, tile, par, nk, place):
                cols = slice((2 - nk) * P, 2 * P)
                pe.wait_ge(sem(f"q_tile{par}_landed"), L.next(f"q_tile{par}_landed", 16))
                for j in range(4):
                    pe.wait_ge(sem(f"bank{j}_free"), L.next(f"bank{j}_free"))
                    for g in range(2):
                        done = mm(psum[:, j, g * 256 + (2 - nk) * P:(g + 1) * 256], q_tile[:, par, j],
                                  k_mask[:, b, g, bass.ds((tile + 1 - nk) * P, nk * P)], start=True, stop=True)
                    done.then_inc(sem(f"bank{j}_full"), L.add(f"bank{j}_full"))
                for hs in range(2):
                    pe.wait_ge(sem("probs_ready"), L.next("probs_ready", 4))
                    for kt in range(2 - nk, 2):
                        transposes(4 + kt, [prob[:, s, kt * P:(kt + 1) * P] for s in range(4 * hs, 4 * hs + 4)],
                                   "q_tile_free" if (hs, kt) == (0, 1) else None)
                for hs in range(2):
                    if hs == 0:
                        for kt in range(2 - nk, 2):
                            pe.wait_ge(sem(f"bank{4 + kt}_free"), L.next(f"bank{4 + kt}_free")), L.skip(f"bank{4 + kt}_free", -1)
                    pe.wait_ge(sem(("bank6_free", "out_taken")[hs]), L.next(("bank6_free", "out_taken")[hs]))
                    for s in range(4):
                        for kt in range(2 - nk, 2):
                            done = mm(psum[:, 6 + hs, s * P:(s + 1) * P], prob_t[:, kt, 4 * hs + s],
                                      v_keys[:, b, bass.ds(tile + kt - 1, 1)].rearrange("p u n -> p (u n)"),
                                      start=kt == 2 - nk, stop=kt == 1)
                    done.then_inc(sem(f"bank{6 + hs}_full"), L.add(f"bank{6 + hs}_full"))
            tiles_of(L, "pe", tile_step)
            with L.loop(CH // 2, "pe merge"):
                for par in range(2):
                    pe.wait_ge(sem("merged_ready"), L.next("merged_ready"))
                    transposes(4 + par, [merged[:, par, j * P:(j + 1) * P] for j in range(4)])
            for bank in (4, 5):
                pe.wait_ge(sem(f"bank{bank}_free"), L.next(f"bank{bank}_free")), L.skip(f"bank{bank}_free", -1)
            pe.wait_ge(sem("u_samples_ready"), L.next("u_samples_ready"))
            pe.wait_ge(sem("raw_free"), L.next("raw_free", 4))
            for bank in (0, 1):
                pe.wait_ge(sem(f"bank{bank}_free"), L.next(f"bank{bank}_free")), L.skip(f"bank{bank}_free", -1)
            for j in range(2):
                for n in range(8):
                    h, tile = divmod(n, 4)
                    product(n, (2 + j,), tile, h, u_hi, u_lo, UW)
                pe.wait_ge(sem(f"bank{4 + j}_free"), L.next(f"bank{4 + j}_free"))
                sample_product((2 + j,), UW, u_lhs, f"bank{4 + j}_full", 4 + j)
            for bank in (4, 5):
                pe.wait_ge(sem(f"bank{bank}_free"), L.next(f"bank{bank}_free")), L.skip(f"bank{bank}_free", -1)
            fold_samples(3, s_acc, KT)

        norm()
        mlp("pe mlp0", True)
        attention_layer()
        norm()
        mlp("pe mlp1", False)
        norm()
    ctx.close()


CONSTS = [("ident", "ident"), ("w_ab", "w_ab"), ("g_ab", "g_ab"), ("dtb", "dtb"), ("lvl", "lvl"), ("tri", "tri"),
          ("msk", "msk"), ("cw", "cw"), ("fold", "fold"), ("s_ext", "s_ext"), ("g_fin", "g_fin"), ("s_x", "xs"), ("gains", "gains")]


def pack(i):
    c = np.ascontiguousarray

    def feat(x):
        return c(x.reshape(x.shape[0], -1, P).transpose(2, 1, 0))

    def units(w):
        k, n = w.shape
        w = w.reshape(k // (UW * P), 2, 2, P, n // HALF, HALF).transpose(4, 0, 1, 3, 2, 5)
        return w.reshape(-1, P, 2, HALF)

    w_in = i["w_in_a"][0]
    heads = w_in[:, :4 * D_MODEL].reshape(D_MODEL, 4, HEADS, P).transpose(0, 2, 1, 3).reshape(D_MODEL, -1)
    up, down = i["w_up"], i["w_down"]

    def mlp(l):
        parts = []
        for b in range(D_FF // HALF):
            parts += [units(up[l][:, b * HALF:(b + 1) * HALF]), units(down[l][b * HALF:(b + 1) * HALF])]
        return parts
    q = i["w_q_b"][0].reshape(D_MODEL, BRANCH, 2, 4, HD).transpose(0, 1, 3, 2, 4).reshape(D_MODEL, -1)
    wo = i["w_o_b"][0].reshape(2, 4, HD, D_MODEL).transpose(1, 0, 2, 3).reshape(-1, D_MODEL)
    kv = np.concatenate([i["w_kv"], np.zeros((D_MODEL, 256), np.float32)], axis=1)
    w = np.concatenate([units(heads), units(i["w_out_a"][0]), *mlp(0), units(kv), units(q), units(wo), *mlp(1)])

    def rows(g):
        return g.reshape(-1, P).T
    one = np.ones((P, UW), np.float32)
    mix, nm = i["norm_mix"], i["norm_mlp"]

    def mlp_gain(l):
        return [rows(nm[l]), one, one] * (D_FF // HALF)
    go = np.repeat(i["norm_o_a"][0][:, None], KT, axis=1)
    gains = np.concatenate([rows(mix[0])] * 8 + [go] * 2 + mlp_gain(0) + [rows(i["norm_kv"])] * 2 + [rows(mix[1])] * 3
                           + [one] * 2 + mlp_gain(1), axis=1)
    j, k = np.arange(P)[:, None], np.arange(P)[None, :]
    lvl = np.zeros((P, LEVELS + 1, P), np.float32)
    for n in range(LEVELS + 1):
        b = 1 << n
        lvl[:, n] = (j // (2 * b) == k // (2 * b)) & (k // b % 2 == 1) & (j // b % 2 == 0)
    cw = i["conv_a"][0].reshape(4, 3, HEADS, P).transpose(3, 2, 1, 0)
    se = np.zeros((P, HEADS, 3, 4, NS), np.float32)
    se[:, :, :, 0:3] = i["state_a_conv"][0].reshape(NS, 3, 3, HEADS, P).transpose(4, 3, 2, 1, 0)
    slot_slope = np.array([2.0 ** -(4 * g + jj + 1) for jj in range(4) for g in range(2)], np.float32)
    dist = np.full((P, 3, P), NEG, np.float32)
    dist[:, 0] = np.where(k >= j, -(P + j - k), NEG)
    dist[:, 1] = np.where(k <= j, -(j - k), NEG)
    dist[:, 2] = np.where((k <= j) & (k // HD == j // HD), -(j - k), NEG)
    slopes = np.broadcast_to((np.array(DIL, np.float32)[:, None] * slot_slope).astype(np.float32), (P, BRANCH, 8))
    far = np.concatenate([np.arange(128, 0, -1), np.arange(256, -1, -4), np.arange(256, -1, -16), [0]])
    taken = [i[f"cache_b{b}_kv"][:, ::DIL[b]] for b in range(BRANCH)]

    def keys(kv):
        own = np.zeros((NS, 1, 2, HD), np.float32)
        parts = [x[:, :, kv] for x in taken]
        return np.concatenate([parts[0], parts[1], own, parts[2], own, own], axis=1).reshape(NS, SK, P)
    all_k, all_v = keys(0), keys(1)
    caches = [c(i[f"cache_b{b}_kv"].reshape(NS, -1, 256)) for b in range(BRANCH)]
    return {
        "dist": dist, "slopes": c(slopes), "s_bias": (-slot_slope[:, None] * far).astype(np.float32), "s_keys": c(all_k.transpose(2, 0, 1)),
        "s_va": c(all_v[:, :SA].transpose(1, 0, 2)), "s_vb": c(all_v[:, SA:].transpose(1, 0, 2)),
        "cache0": c(caches[0][:, 1:]), "cache1": caches[1], "cache2": caches[2], "g_fin": c(rows(i["norm_final"])),
        "s_ext": se, "s_rec_in": c(i["state_a_rec"][0].transpose(2, 1, 0, 3)),
        "x": feat(i["x_prompt"][0]), "xs": feat(i["x_sample"][:, 0]), "w": c(w), "gains": c(gains),
        "w_ab": c(w_in[:, 4 * D_MODEL:].reshape(KT, P, 2 * HEADS).transpose(1, 0, 2)), "g_ab": c(rows(mix[0])),
        "dtb": c(np.broadcast_to(np.stack([i["a_log"][0], i["dt_bias"][0]]), (P, 2, HEADS))),
        "cw": c(cw.reshape(P, -1)),
        "fold": np.tile(np.eye(NS, dtype=np.float32), (2, 1)), "ident": np.eye(P, dtype=np.float32), "lvl": lvl, "tri": (j <= k).astype(np.float32),
        "msk": np.where(j <= k, 0, NEG).astype(np.float32),
    }


def declare(nc, arrays):
    t = {n: nc.dram_tensor(f"in_{n}", a.shape, mybir.dt.from_np(a.dtype), kind="ExternalInput").ap() for n, a in arrays.items()}
    t["w"] = t["w"].rearrange("u p k n -> p u k n")
    for n, shape in OUTS.items():
        t[n] = nc.dram_tensor(f"out_{n}", shape, F32, kind="ExternalOutput").ap()
    for n, shape in SCRATCH.items():
        t[n] = nc.dram_tensor(f"scratch_{n}", shape, F32, kind="Internal").ap()
    return t


OUTS = {
    "y": (P, KT, SEQ), "s_y": (P, KT, NS), "p_conv": (P, 3 * HEADS, 3), "p_rec": (P, HEADS, P),
    "s_rec": (P, HEADS, NS, P), "s_conv": (P, 3 * HEADS, 3, NS),
    "p_k": (P, BRANCH, SEQ), "p_v": (P, BRANCH, SEQ), "s_kv_new": (P, 2 * BRANCH, NS),
    "s_kv0_old": (NS, 127, 256), "s_kv1_old": (NS, 256, 256), "s_kv2_old": (NS, 256, 256),
}
SCRATCH = {"q": (P, 4 * BRANCH, SEQ), "att": (SEQ, BRANCH, OW), "s_vnew": (NS, BRANCH, P), "o_heads": (P, HEADS, SEQ)}


def unpack(o):
    def tokens(x):
        return x.transpose(2, 1, 0).reshape(x.shape[2], -1)

    def window(b):
        both = [o[name][:, b].reshape(P, DIL[b], SEQ // DIL[b]).transpose(2, 1, 0).reshape(SEQ, P) for name in ("p_k", "p_v")]
        return np.stack(both, axis=1)[-min(DIL[b] * P, SEQ):].reshape(1, -1, 2, 2, HD)

    def cache(b):
        new = o["s_kv_new"][:, 2 * b:2 * b + 2].transpose(2, 1, 0).reshape(NS, 1, 2 * P)
        return np.concatenate([o[f"s_kv{b}_old"], new], axis=1).reshape(NS, -1, 2, 2, HD)
    return (
        tokens(o["y"])[None], tokens(o["s_y"])[:, None],
        o["p_rec"].transpose(1, 0, 2)[None, None],
        o["p_conv"].reshape(P, HEADS, 3, 3).transpose(3, 2, 1, 0).reshape(1, 1, 3, -1),
        window(0), window(1), window(2),
        o["s_rec"].transpose(2, 1, 0, 3)[None],
        o["s_conv"].reshape(P, HEADS, 3, 3, NS).transpose(4, 3, 2, 1, 0).reshape(1, NS, 3, -1),
        cache(0), cache(1), cache(2),
    )


def kernel(**inputs):
    import concourse.bacc as _bacc
    from concourse.bass_utils import run_bass_kernel_spmd as _run

    arrays = pack({name: np.asarray(a) for name, a in inputs.items()})
    nc = _bacc.Bacc("TRN2", target_bir_lowering=False, num_devices=1, dynamic_dma_scratch_size=1024)
    build(nc, declare(nc, arrays))
    result = _run(nc, [{f"in_{name}": a for name, a in arrays.items()}], core_ids=[0]).results[0]
    return unpack({name: result[f"out_{name}"] for name in OUTS})
```

```python
from contextlib import ExitStack, contextmanager

import numpy as np

import concourse.bass as bass
from concourse import mybir

F32 = mybir.dt.float32
F32R = mybir.dt.float32r
BF16 = mybir.dt.bfloat16
ALU = mybir.AluOpType
ACT = mybir.ActivationFunctionType
AXX = mybir.AxisListType.X

P = 128
D_MODEL = 1024
SEQ = 1024
NS = 8
HEADS = 8
D_FF = 4096
EPS = 1e-6
KT = D_MODEL // P
CH = SEQ // P
HALF = 512
HD = 64
OW = 8 * HD + 16
SA = 128
SB = 64 + 1 + 16 + 1 + 1
SK = SA + SB
BRANCH = 3
DIL = (1, 4, 16)
CACHE = (128, 64, 16)
NEG = -1.0e30
TAKES = (0, 1, 6, 7)
UW = 4
RING = 4
LEVELS = 6

U_IN, U_OUT = 0, 16
U_MLP0, U_KVQ = 20, 52
U_WO, U_MLP1 = 62, 64
UNITS = 96
CREDIT = {"raw_free": 2, "product_free": 2, "sample_free": 1, "square_free": 2,
          "head_squares_free": 1, "q_tile_free": 2, "merge_free": 2,
          "head_output_stored": 16, "state_stored": 16, "s_state_stored": 16, "out0_stored": 32, "out1_stored": 32, "out_taken": 1,
          **{f"bank{b}_free": 1 for b in range(8)}}


PER = {
    "weights": {"raw_free": 2, "raw0_landed": 16, "raw1_landed": 16},
    "act heads": {"bank3_full": 54, "bank3_free": 54, "bank4_full": 38, "bank4_free": 38, "bank5_full": 36,
        "bank5_free": 36, "raw0_landed": 64, "weight_half_hi": 8, "raw1_landed": 64, "act_order": 6,
        "bank6_full": 32, "bank6_free": 32, "bank7_full": 34, "bank7_free": 34, "sample_full": 2, "sample_free": 2,
        "product_free": 16, "tap0_ready": 6, "taps_ready": 6, "qkv_ready": 6, "z_ready": 2, "conv_stored": 32,
        "head_squares_free": 4, "norms_ready": 2, "decay_args_ready": 4, "decay_ready": 4, "rms_arg_ready": 2,
        "rms_ready": 2, "s_state_landed": 32, "s_conv_ready": 2, "s_silu_ready": 2, "s_state_ready": 2,
        "s_state_stored": 32, "head_output_stored": 32, "state_stored": 32},
    "dve heads": {"dve_order": 72, "bank5_free": 36, "bank5_full": 36, "bank3_free": 54, "bank3_full": 54,
        "bank4_full": 38, "bank4_free": 38, "weight_half_hi": 8, "raw_free": 8, "bank6_full": 32, "bank6_free": 32,
        "bank7_full": 34, "bank7_free": 34, "product_full": 16, "product_free": 16, "s_conv_ready": 2,
        "tap0_ready": 6, "taps_ready": 6, "conv_stored": 32, "decay_terms_ready": 2, "head_squares_free": 4,
        "head_output_stored": 32, "decay_args_ready": 4, "norms_ready": 2, "decay_ready": 4, "blocks_ready": 14,
        "inverse_t_ready": 2, "state_stored": 32, "state_ready": 2, "v_for_state_ready": 16, "rms_arg_ready": 2,
        "rms_ready": 2, "o_tok_ready": 2, "z_ready": 2, "s_silu_ready": 2, "s_squares_ready": 2, "s_qk_ready": 2,
        "s_v_ready": 2, "s_out_squares_ready": 2, "s_v_wide_ready": 2, "s_state_ready": 2},
    "pe heads": {"bank5_free": 36, "bank5_full": 36, "bank3_free": 54, "bank3_full": 54, "bank4_free": 38,
        "bank4_full": 38, "bank6_free": 32, "bank6_full": 32, "bank7_free": 34, "bank7_full": 34, "raw_free": 8,
        "product_free": 16, "product_full": 16, "sample_free": 2, "sample_full": 2, "qkv_ready": 6,
        "decay_terms_ready": 2, "blocks_ready": 14, "inverse_t_ready": 2, "state_ready": 2,
        "v_for_state_ready": 16, "o_tok_ready": 2, "s_squares_ready": 2, "s_qk_ready": 2, "s_state_landed": 32,
        "s_v_ready": 2, "s_v_wide_ready": 2, "s_out_squares_ready": 2},
    "act mlp0": {"bank3_full": 1, "bank3_free": 1, "bank4_full": 1, "bank4_free": 1, "bank5_full": 1,
        "bank5_free": 1, "raw0_landed": 64, "weight_half_hi": 8, "raw1_landed": 64, "sample_full": 1,
        "sample_free": 1, "product_free": 24, "relu_square_ready": 8, "u_hi_ready": 8},
    "dve mlp0": {"dve_order": 2, "bank3_free": 1, "bank3_full": 1, "bank4_free": 1, "bank4_full": 1,
        "bank5_free": 1, "bank5_full": 1, "weight_half_hi": 8, "raw_free": 8, "product_full": 24,
        "product_free": 24, "relu_square_ready": 8, "u_hi_ready": 8, "u_ready": 8, "u_samples_ready": 1},
    "pe mlp0": {"bank5_free": 1, "bank5_full": 1, "bank3_free": 1, "bank3_full": 1, "bank4_free": 1,
        "bank4_full": 1, "raw_free": 8, "product_free": 24, "product_full": 24, "sample_free": 1, "sample_full": 1,
        "u_ready": 8, "u_samples_ready": 1},
    "sp branch 0": {"q_tile_free": 2, "q_tile0_landed": 16, "q_tile1_landed": 16},
    "sp branch 1": {"q_tile_free": 2, "q_tile0_landed": 16, "q_tile1_landed": 16},
    "sp branch 2": {"q_tile_free": 2, "q_tile0_landed": 16, "q_tile1_landed": 16},
    "sp merge": {"merge_free": 2, "merge0_landed": 16, "merge1_landed": 16},
    "act branch 0": {"bank3_full": 2, "bank3_free": 2, "bank4_full": 4, "bank4_free": 4, "bank5_full": 4,
        "bank5_free": 4, "bank6_full": 2, "bank6_free": 2, "bank7_full": 2, "bank0_full": 2, "bank0_free": 2,
        "bank1_full": 2, "bank1_free": 2, "bank2_full": 2, "bank2_free": 2, "max_ready": 4, "probs_ready": 16,
        "out_taken": 2, "out0_stored": 32, "out1_stored": 32},
    "act branch 1": {"bank3_full": 2, "bank3_free": 2, "bank4_full": 2, "bank4_free": 2, "bank5_full": 4,
        "bank5_free": 4, "bank6_full": 2, "bank6_free": 2, "bank7_full": 2, "bank0_full": 2, "bank0_free": 2,
        "bank1_full": 2, "bank1_free": 2, "bank2_full": 2, "bank2_free": 2, "max_ready": 4, "probs_ready": 16,
        "out_taken": 2, "out0_stored": 32, "out1_stored": 32},
    "act branch 2": {"bank3_full": 2, "bank3_free": 2, "bank5_full": 4, "bank5_free": 4, "bank6_full": 2,
        "bank6_free": 2, "bank7_full": 2, "bank0_full": 2, "bank0_free": 2, "bank1_full": 2, "bank1_free": 2,
        "bank2_full": 2, "bank2_free": 2, "max_ready": 4, "probs_ready": 16, "out_taken": 2, "out0_stored": 32,
        "out1_stored": 32},
    "act merge": {"bank4_full": 1, "bank4_free": 1, "bank5_full": 1, "bank5_free": 1, "u_hi_ready": 2},
    "act mlp1": {"bank3_full": 1, "bank3_free": 1, "bank4_full": 1, "bank4_free": 1, "bank5_full": 1,
        "bank5_free": 1, "raw0_landed": 64, "weight_half_hi": 8, "raw1_landed": 64, "sample_full": 1,
        "sample_free": 1, "product_free": 24, "relu_square_ready": 8, "u_hi_ready": 8},
    "dve branch 0": {"dve_order": 10, "bank3_free": 2, "bank3_full": 2, "bank4_free": 4, "bank4_full": 4,
        "bank5_free": 4, "bank5_full": 4, "bank6_full": 2, "bank6_free": 2, "bank7_full": 2, "bank0_full": 2,
        "bank0_free": 2, "bank1_full": 2, "bank1_free": 2, "bank2_full": 2, "bank2_free": 2, "max_ready": 4,
        "out0_stored": 32, "out_taken": 2, "out1_stored": 32},
    "dve branch 1": {"dve_order": 10, "bank3_free": 2, "bank3_full": 2, "bank4_free": 2, "bank4_full": 2,
        "bank5_free": 4, "bank5_full": 4, "bank6_full": 2, "bank6_free": 2, "bank7_full": 2, "bank0_full": 2,
        "bank0_free": 2, "bank1_full": 2, "bank1_free": 2, "bank2_full": 2, "bank2_free": 2, "max_ready": 4,
        "out0_stored": 32, "out_taken": 2, "out1_stored": 32},
    "dve branch 2": {"dve_order": 10, "bank3_free": 2, "bank3_full": 2, "bank5_free": 4, "bank5_full": 4,
        "bank6_full": 2, "bank6_free": 2, "bank7_full": 2, "bank0_full": 2, "bank0_free": 2, "bank1_full": 2,
        "bank1_free": 2, "bank2_full": 2, "bank2_free": 2, "max_ready": 4, "out0_stored": 32, "out_taken": 2,
        "out1_stored": 32},
    "dve merge": {"dve_order": 6, "bank4_free": 1, "bank4_full": 1, "bank5_free": 1, "bank5_full": 1,
        "u_hi_ready": 2, "merge0_landed": 16, "merge_free": 2, "merged_ready": 2, "merge1_landed": 16},
    "dve mlp1": {"dve_order": 2, "bank3_free": 1, "bank3_full": 1, "bank4_free": 1, "bank4_full": 1,
        "bank5_free": 1, "bank5_full": 1, "weight_half_hi": 8, "raw_free": 8, "product_full": 24,
        "product_free": 24, "relu_square_ready": 8, "u_hi_ready": 8, "u_ready": 8, "u_samples_ready": 1},
    "pe branch 0": {"bank5_free": 4, "bank5_full": 4, "bank3_free": 2, "bank3_full": 2, "bank4_free": 4,
        "bank4_full": 4, "bank6_free": 2, "bank6_full": 2, "bank7_full": 2, "bank0_free": 2, "bank0_full": 2,
        "bank1_free": 2, "bank1_full": 2, "bank2_free": 2, "bank2_full": 2, "q_tile0_landed": 16,
        "probs_ready": 16, "q_tile_free": 2, "out_taken": 2, "q_tile1_landed": 16},
    "pe branch 1": {"bank5_free": 4, "bank5_full": 4, "bank3_free": 2, "bank3_full": 2, "bank4_free": 2,
        "bank4_full": 2, "bank6_free": 2, "bank6_full": 2, "bank7_full": 2, "bank0_free": 2, "bank0_full": 2,
        "bank1_free": 2, "bank1_full": 2, "bank2_free": 2, "bank2_full": 2, "q_tile0_landed": 16,
        "probs_ready": 16, "q_tile_free": 2, "out_taken": 2, "q_tile1_landed": 16},
    "pe branch 2": {"bank5_free": 4, "bank5_full": 4, "bank3_free": 2, "bank3_full": 2, "bank6_free": 2,
        "bank6_full": 2, "bank7_full": 2, "bank0_free": 2, "bank0_full": 2, "bank1_free": 2, "bank1_full": 2,
        "bank2_free": 2, "bank2_full": 2, "q_tile0_landed": 16, "probs_ready": 16, "q_tile_free": 2,
        "out_taken": 2, "q_tile1_landed": 16},
    "pe merge": {"bank5_free": 1, "bank5_full": 1, "bank4_free": 1, "bank4_full": 1, "merged_ready": 2},
    "pe mlp1": {"bank5_free": 1, "bank5_full": 1, "bank3_free": 1, "bank3_full": 1, "bank4_free": 1,
        "bank4_full": 1, "raw_free": 8, "product_free": 24, "product_full": 24, "sample_free": 1, "sample_full": 1,
        "u_ready": 8, "u_samples_ready": 1},
}


class Lane:

    def __init__(self, eng, sem, room=()):
        self.eng, self.sem = eng, sem
        self.room = set(room)
        self.n, self.turn, self.per, self.last = {}, None, {}, None

    def first(self, name):
        return 0 if name in self.room else CREDIT.get(name, 0)

    def value(self, name):
        n = self.n.get(name, self.first(name))
        assert n > 0, name
        return n if self.turn is None else n + self.turn * self.per.get(name, 0)

    def skip(self, name, n=1):
        self.n[name] = self.n.get(name, self.first(name)) + n

    def next(self, name, n=1):
        self.skip(name, n)
        return self.value(name)

    def add(self, name, n=1):
        self.skip(name, n)
        self.last = name
        return n

    @contextmanager
    def loop(self, trips, name):
        per = PER.get(name, {})
        first = dict(self.n)
        with self.eng.Fori(0, trips) as i:
            self.turn, self.per = i, per
            yield i
            if self.last in self.per and not self.last.endswith(("landed", "stored")):
                self.eng.wait_ge(self.sem(self.last), self.value(self.last))
            self.turn, self.per = None, {}
        moved = {c: self.n[c] - first.get(c, self.first(c)) for c in self.n}
        moved = {c: m for c, m in moved.items() if m}
        if moved != per:
            raise ValueError(f"PER[{name!r}] = {moved}")
        for c, m in moved.items():
            self.n[c] += m * (trips - 1)


def build(nc, t):
    ctx = ExitStack()
    made = {}

    def sem(name):
        if name not in made:
            made[name] = ctx.enter_context(nc.semaphore(name))
        return made[name]

    offset = [1152]

    def at(name, shape, dt, where=None, word=4):
        size = int(np.prod(shape[1:])) * word
        if where is None:
            place = offset[0]
            offset[0] += -(-size // 32) * 32
        else:
            place = where[0]
            where[0] += -(-size // 32) * 32
            assert where[0] <= where[1], (name, where)
        return nc.alloc_sbuf_tensor_at(name, list(shape), dt, offset=place)

    w_hi = at("w_hi", [P, RING, UW, HALF], F32R)
    w_lo = at("w_lo", [P, RING, UW, HALF], F32R)
    w_raw = at("w_raw", [P, 2, 2, HALF], F32)
    gains = at("gains", [P, UNITS * UW], F32)
    ident = at("ident", [P, P], F32)
    ones = at("ones", [P, P], F32)
    fold = at("fold", [2 * NS, NS], F32)
    rs = at("rs", [P, SEQ], F32)
    s_x = at("s_x", [P, KT, NS], F32)
    s_rs = at("s_rs", [P, NS], F32)
    rs_tok = at("rs_tok", [P, 2, CH], F32)
    s_tok = at("s_tok", [2 * NS, HALF], F32)
    s_lhs = at("s_lhs", [P, KT, P], F32R)
    s_tmp = at("s_tmp", [P, 4, KT * NS], F32)
    eps = at("eps", [P, 1], F32)
    g_fin = at("g_fin", [P, KT], F32)
    x_start = offset[0]
    x_hi = at("x_hi", [P, KT, SEQ], F32R)
    x_lo = at("x_lo", [P, KT, SEQ], F32R)
    region = offset[0]
    END = 229368
    assert region < END

    def area(start=region):
        return [start, END]

    a = area()
    x = at("x", [P, KT, SEQ], F32, a)
    sq = at("sq", [P, 2, SEQ], F32, a)
    sq_sum = at("sq_sum", [P, SEQ], F32, a)
    w_ab = at("w_ab", [P, KT, 2 * HEADS], F32, a)
    g_ab = at("g_ab", [P, KT], F32, a)
    ab_feat = at("ab_feat", [2 * HEADS, SEQ], F32, a)
    ab = at("ab", [P, 6, 2 * HEADS * CH], F32, a)
    dtb = at("dtb", [P, 2, HEADS], F32, a)
    s_wide = at("s_wide", [2 * HEADS, 2 * HEADS, NS], F32, a)
    s_ab = at("s_ab", [2 * HEADS, NS], F32, a)
    lvl_in = at("lvl_in", [P, LEVELS + 1, P], F32, a)
    start_end = a[0]

    a = area()
    pre = at("pre", [P, 3, SEQ + 8], F32, a)
    z_g = at("z_g", [P, SEQ], F32, a)
    qkv = at("qkv", [P, 3, SEQ], F32, a)
    k_tok = at("k_tok", [P, CH, P], F32, a)
    v_tok = at("v_tok", [P, CH, P], F32, a)
    dec = at("dec", [P, CH, P], F32, a)
    low = at("low", [P, CH, P], F32, a)
    att = at("att", [P, CH, P], F32, a)
    blk = at("blk", [P, CH, P], F32, a)
    inv = at("inv", [P, CH, P], F32, a)
    inv_t = at("inv_t", [P, CH, P], F32, a)
    prod, head_out = dec, dec
    o_tok = low
    a = [max(start_end, a[0]), END]
    lvl = at("lvl", [P, LEVELS + 1, P], BF16, a, 2)
    tri = at("tri", [P, P], F32, a)
    msk = at("msk", [P, P], F32, a)
    state = at("state", [P, P], F32, a)
    gt = at("gt", [P, 6, HEADS * CH], F32, a)
    beta, g_sum, e_pos, e_neg, e_rest, e_last = (gt[:, n] for n in range(6))
    cw = at("cw", [P, HEADS * 12], F32, a)
    col = at("col", [P, 14, CH], F32, a)
    tmp_o = at("tmp_o", [P, P], F32, a)
    g_keep = at("g_keep", [P, HEADS * CH], F32, a)
    vz = at("vz", [P, 3, P], F32, a)
    s_gate = at("s_gate", [P, 2, HEADS, NS], F32, a)
    s_ext = at("s_ext", [P, HEADS, 3, 4, NS], F32, a)
    s_z = at("s_z", [P, NS], F32, a)
    s_taps = at("s_taps", [P, 3, 4, NS], F32, a)
    s_qkv = at("s_qkv", [P, 3, NS], F32, a)
    s_u = at("s_u", [P, 8, NS], F32, a)
    s_og = at("s_og", [P, HEADS, NS], F32, a)
    s_state = blk
    s_v_wide = inv
    s_rows = vz
    a = area()
    a[0] += KT * SEQ * 4
    o_raw = at("o_raw", [P, KT, SEQ], F32, a)
    a = area()
    a[0] += KT * SEQ * 4
    u_hi = at("u_hi", [P, UW, SEQ], F32R, a)
    u_lo = at("u_lo", [P, UW, SEQ], F32R, a)
    relu = at("relu", [P, HALF], F32, a)
    u_lhs = at("u_lhs", [P, UW, P], F32R, a)
    s_acc = at("s_acc", [2 * NS, SEQ], F32, a)

    a = area()
    a[0] += KT * SEQ * 4
    k_mask = at("k_mask", [P, BRANCH, 2, SEQ], F32, a)
    v_feat = at("v_feat", [P, BRANCH, SEQ], F32, a)
    q_stage = at("q_stage", [P, 2, HALF], F32, a)
    s_kv = at("s_kv", [P, 2 * BRANCH, NS], F32, a)
    s_q = at("s_q", [P, 4 * BRANCH, NS], F32, a)

    a = [x_start, region]
    v_keys = at("v_keys", [P, BRANCH, CH, P], F32, a)
    q_tile = at("q_tile", [P, 2, 4, P], F32, a)
    prob = at("prob", [P, 2, 8, 2 * P], F32, a)
    prob_t = at("prob_t", [P, 2, 8, P], F32, a)
    bias = at("bias", [P, 8, 2 * P], F32, a)
    o_out = at("o_out", [P, 2, OW], F32, a)
    dist = at("dist", [P, 3, P], F32, a)
    slopes = at("slopes", [P, BRANCH, 8], F32, a)
    neg_max = at("neg_max", [P, 2, 8], F32, a)
    stats = at("stats", [P, 2, 2, 8], F32, a)
    a = [x_start, region]
    merge = at("merge", [P, 2, BRANCH, 8 * HD], F32, a)
    merge_stats = at("merge_stats", [P, CH, BRANCH, 2, 8], F32, a)
    merged = at("merged", [P, 2, 8 * HD], F32, a)
    part = at("part", [P, 8 * HD], F32, a)
    share = at("share", [P, 4, CH, BRANCH, 8], F32, a)
    total = at("total", [P, 4, CH, 8], F32, a)
    a = [x_start, region]
    a[0] += 4 * (BRANCH * CH * P + 2 * 4 * P)
    s_keys = at("s_keys", [P, NS, SK], F32, a)
    s_va = at("s_va", [P, NS, P], F32, a)
    s_vb = at("s_vb", [SB, NS, P], F32, a)
    s_bias = at("s_bias", [8, SK], F32, a)
    s_qz = at("s_qz", [P, BRANCH, NS, 8], F32, a)
    s_p = at("s_p", [8, NS, SK], F32, a)
    s_pm = at("s_pm", [8, 2, NS], F32, a)
    s_pt = at("s_pt", [P, 2, NS * 8], F32, a)
    s_vrow = at("s_vrow", [NS, BRANCH, P], F32, a)

    psum = ctx.enter_context(nc.psum_tensor("psum", [P, 8, HALF], F32))
    for name in CREDIT:
        sem(name)
    block = ctx.enter_context(nc.Block())
    halves = [slice(0, HALF), slice(HALF, SEQ)]

    def f(ap):
        return ap.bitcast(F32)

    def b3(ap, n, m=P):
        return ap.unsqueeze(2).to_broadcast([ap.shape[0], n, m])

    def o3(ap, n):
        return ap.unsqueeze(1).to_broadcast([ap.shape[0], n, ap.shape[-1]])

    def hc(h):
        return slice(4 * h, 4 * h + 4)

    def tiles_of(L, lane, step):
        def at_tile(b, n, par):
            if b == 0:
                return (0, n, par, 2, n)
            if b == 1:
                return (1, 2 * n + par, par, 1 + par, n)
            return (2, 2 * n + par, par, 1, 2 * n + par)
        first = (0, 0, 0, 1, 0)
        step(None, first)
        step(first, at_tile(0, 1, 1))
        with L.loop(3, f"{lane} branch 0") as i:
            step(at_tile(0, 2 * i + 1, 1), at_tile(0, 2 * i + 2, 0))
            step(at_tile(0, 2 * i + 2, 0), at_tile(0, 2 * i + 3, 1))
        step(at_tile(0, 7, 1), at_tile(1, 0, 0))
        for b in (1, 2):
            with L.loop(3, f"{lane} branch {b}") as i:
                step(at_tile(b, i, 0), at_tile(b, i, 1))
                step(at_tile(b, i, 1), at_tile(b, i + 1, 0))
            step(at_tile(b, 3, 0), at_tile(b, 3, 1))
            step(at_tile(b, 3, 1), at_tile(2, 0, 0) if b == 1 else None)

    @block.sync
    def _(sp):
        L = Lane(sp, sem, room=["raw_free", "q_tile_free", "merge_free"])
        for dst, name in CONSTS:
            dst_tiles = {"ident": ident, "w_ab": w_ab, "g_ab": g_ab, "dtb": dtb, "lvl": lvl_in, "tri": tri, "msk": msk,
                               "cw": cw, "fold": fold, "s_ext": s_ext, "g_fin": g_fin, "s_x": s_x, "gains": gains}
            sp.dma_start(dst_tiles[dst][:], t[name]).then_inc(sem("constants_landed"), L.add("constants_landed", 16))
        for k in range(KT):
            sp.dma_start(x[:, k, :], t["x"][:, k, :]).then_inc(sem("x_landed"), L.add("x_landed", 16))

        def stream(first, last):
            with L.loop(last - first, "weights") as i:
                for part in range(2):
                    sp.wait_ge(sem("raw_free"), L.next("raw_free"))
                    sp.dma_start(w_raw[:, part:part + 1], t["w"][:, bass.ds((i + first) * 2 + part, 1)]
                    ).then_inc(sem(f"raw{part}_landed"), L.add(f"raw{part}_landed", 16))

        def attention_traffic():
            sp.wait_ge(sem("kvq_done"), L.next("kvq_done"))
            for dst, name in ((dist, "dist"), (slopes, "slopes"), (s_keys, "s_keys"), (s_va, "s_va"), (s_vb, "s_vb"),
                              (s_bias, "s_bias")):
                sp.dma_start(dst[:], t[name]
                ).then_inc(sem("attention_constants_landed"), L.add("attention_constants_landed", 16))
            for g in range(2):
                rows = slice(g * HD, (g + 1) * HD)
                sp.dma_start(t["p_k"][rows], k_mask[rows, :, g]
                ).then_inc(sem("outputs_stored"), L.add("outputs_stored", 16))
            sp.dma_start(t["p_v"], v_feat[:]).then_inc(sem("outputs_stored"), L.add("outputs_stored", 16))
            sp.dma_start(t["s_kv_new"], s_kv[:]).then_inc(sem("outputs_stored"), L.add("outputs_stored", 16))
            sp.wait_ge(sem("s_vrow_ready"), L.next("s_vrow_ready"))
            sp.dma_start(t["s_vnew"], s_vrow[:]).then_inc(sem("s_vnew_stored"), L.add("s_vnew_stored", 16))
            sp.wait_ge(sem("s_vnew_stored"), L.value("s_vnew_stored"))
            sp.wait_ge(sem("attention_constants_landed"), L.value("attention_constants_landed"))
            for b, row in ((1, 64), (2, 81), (0, 82)):
                sp.dma_start(s_vb[row:row + 1], t["s_vnew"][:, b].unsqueeze(0)
                ).then_inc(sem("s_vown_landed"), L.add("s_vown_landed", 16))
            sp.wait_ge(sem("q0_stored"), L.next("q0_stored", 16 * 12))
            sp.wait_ge(sem("q1_stored"), L.next("q1_stored", 16 * 12))

            def load(cur, nxt):
                if nxt is None:
                    return
                b, tile, par, _, _ = nxt
                sp.wait_ge(sem("q_tile_free"), L.next("q_tile_free"))
                sp.dma_start(q_tile[:, par], t["q"][:, 4 * b:4 * b + 4, bass.ds(tile * P, P)]
                ).then_inc(sem(f"q_tile{par}_landed"), L.add(f"q_tile{par}_landed", 16))
            tiles_of(L, "sp", load)
            sp.wait_ge(sem("out0_stored"), L.next("out0_stored", 32 * 12))
            sp.wait_ge(sem("out1_stored"), L.next("out1_stored", 32 * 12))
            for b in range(BRANCH):
                sp.dma_start(merge_stats[:, :, b].rearrange("p c m s -> p c (m s)"),
                             t["att"].rearrange("(c p) b w -> p c b w", p=P)[:, :, b, 8 * HD:]
                ).then_inc(sem("merge_stats_landed"), L.add("merge_stats_landed", 16))
            with L.loop(CH // 2, "sp merge") as i:
                for par in range(2):
                    sp.wait_ge(sem("merge_free"), L.next("merge_free"))
                    sp.dma_start(merge[:, par], t["att"][bass.ds((2 * i + par) * P, P), :, 0:8 * HD]
                    ).then_inc(sem(f"merge{par}_landed"), L.add(f"merge{par}_landed", 16))

        stream(0, U_OUT + 2)
        for b in range(BRANCH):
            sp.dma_start(t[f"s_kv{b}_old"], t[f"cache{b}"]).then_inc(sem("outputs_stored"), L.add("outputs_stored", 16))
        sp.wait_ge(sem("head_output_stored"), L.next("head_output_stored", 16 * HEADS))
        sp.wait_ge(sem("state_stored"), L.next("state_stored", 16 * HEADS))
        sp.wait_ge(sem("conv_stored"), L.next("conv_stored", 16 * HEADS))
        sp.wait_ge(sem("s_state_stored"), L.next("s_state_stored", 16 * HEADS))
        sp.wait_ge(sem("x_back"), L.next("x_back"))
        sp.dma_start(t["s_conv"], s_ext[:].rearrange("p h k j n -> p (h k) j n")[:, :, 1:4]
        ).then_inc(sem("outputs_stored"), L.add("outputs_stored", 16))
        for k in range(KT):
            sp.dma_start(o_raw[:, k], t["o_heads"][:, k]
            ).then_inc(sem(f"o_raw{k}_landed"), L.add(f"o_raw{k}_landed", 16))
        stream(U_OUT + 2, U_KVQ + 2)
        stream(U_KVQ + 2, U_WO + 2)
        attention_traffic()
        stream(U_WO + 2, UNITS)
        sp.wait_ge(sem("y_ready"), L.next("y_ready", KT + 1))
        for k in range(KT):
            sp.dma_start(t["y"][:, k], x[:, k]).then_inc(sem("outputs_stored"), L.add("outputs_stored", 16))
        sp.dma_start(t["s_y"], s_x[:]).then_inc(sem("outputs_stored"), L.add("outputs_stored", 16))
        sp.wait_ge(sem("outputs_stored"), L.value("outputs_stored"))

    @block.scalar
    def _(act):
        L = Lane(act, sem, room=["square_free", "head_squares_free"])

        def split_hi(unit, slot, parts=(0, 1)):
            for part in parts:
                act.wait_ge(sem(f"raw{part}_landed"), L.next(f"raw{part}_landed", 16))
                for k in range(2):
                    done = act.activation(w_hi[:, slot, 2 * part + k], w_raw[:, part, k], ACT.Copy,
                                          scale=gains[:, bass.ds(unit * UW + 2 * part + k, 1)])
                done.then_inc(sem("weight_half_hi"), L.add("weight_half_hi"))

        def norm(split=True):
            if split:
                for k in range(KT):
                    act.activation(x_hi[:, k], x[:, k], ACT.Copy).then_inc(sem("x_hi_ready"), L.add("x_hi_ready"))
            for k in range(KT):
                act.wait_ge(sem("square_free"), L.next("square_free"))
                act.activation(sq[:, k % 2], x[:, k], ACT.Square).then_inc(sem("square_ready"), L.add("square_ready"))
            act.wait_ge(sem("bank5_full"), L.next("bank5_full"))
            act.activation(s_rs[:], psum[:, 5, 0:NS], ACT.Sqrt, scale=1.0 / D_MODEL, bias=eps[:, 0:1]
            ).then_inc(sem("bank5_free"), L.add("bank5_free"))
            act.wait_ge(sem("bank3_full"), L.next("bank3_full"))
            act.activation(rs_tok[:, 0], psum[:, 3, 0:CH], ACT.Sqrt, scale=1.0 / D_MODEL, bias=eps[:, 0:1]
            ).then_inc(sem("bank3_free"), L.add("bank3_free"))
            skip(3, 4)

        def skip(*banks):
            for b in banks:
                L.skip(f"bank{b}_full"), L.skip(f"bank{b}_free")

        act.wait_ge(sem("constants_landed"), L.next("constants_landed", 16 * len(CONSTS)))
        act.wait_ge(sem("eps_set"), L.next("eps_set"))
        act.wait_ge(sem("x_landed"), L.next("x_landed", 16 * KT))
        norm()
        split_hi(0, 0)
        split_hi(1, 1)

        skip(6, 7, 5, 5, 5)
        act.wait_ge(sem("gate_args_ready"), L.next("gate_args_ready"))
        act.activation(ab[:, 0:1], ab[:, 0:1], ACT.Exp, scale=-1.0
        ).then_inc(sem("act_order"), L.add("act_order"))
        act.activation(dtb[:, 0], dtb[:, 0], ACT.Exp).then_inc(sem("act_order"), L.add("act_order"))
        act.activation(ab[:, 3], ab[:, 2], ACT.Exp, scale=-1.0
        ).then_inc(sem("gate_exps_ready"), L.add("gate_exps_ready"))
        act.wait_ge(sem("softplus_arg_ready"), L.next("softplus_arg_ready"))
        act.activation(ab[:, 5], ab[:, 4], ACT.Ln
        ).then_inc(sem("softplus_log_ready"), L.add("softplus_log_ready"))
        skip(6, 7)
        act.wait_ge(sem("decay_sums_ready"), L.next("decay_sums_ready"))
        act.activation(e_pos, g_sum, ACT.Exp).then_inc(sem("act_order"), L.add("act_order"))
        act.activation(e_last, e_last, ACT.Exp).then_inc(sem("act_order"), L.add("act_order"))
        act.activation(e_rest, e_rest, ACT.Exp).then_inc(sem("act_order"), L.add("act_order"))
        act.activation(s_gate[:, 1], ab[:, 3, 64:].rearrange("p (h n) -> p h n", n=NS), ACT.Exp
        ).then_inc(sem("decays_ready"), L.add("decays_ready"))

        def conv_silu(head):
            act.wait_ge(sem("product_free"), L.next("product_free", 8))
            act.dma_start(t["p_conv"][:, bass.ds(head * 3, 3)], pre[:, :, SEQ:SEQ + 3]
            ).then_inc(sem("conv_stored"), L.add("conv_stored", 16))
            for n in range(3):
                act.activation(qkv[:, n], pre[:, n, 0:SEQ], ACT.Copy, scale=cw[:, bass.ds(head * 12 + n * 4, 1)]
                ).then_inc(sem("tap0_ready"), L.add("tap0_ready"))
            act.wait_ge(sem("s_conv_ready"), L.next("s_conv_ready"))
            act.activation(s_qkv[:], s_qkv[:], ACT.Silu).then_inc(sem("act_order"), L.add("act_order"))
            act.activation(s_z[:], s_z[:], ACT.Silu).then_inc(sem("s_silu_ready"), L.add("s_silu_ready"))
            for n in range(3):
                act.wait_ge(sem("taps_ready"), L.next("taps_ready"))
                act.activation(qkv[:, n], qkv[:, n], ACT.Silu).then_inc(sem("qkv_ready"), L.add("qkv_ready"))

        def gdn(head, slots, more):
            act.wait_ge(sem("s_state_stored"), L.value("s_state_stored"))
            act.wait_ge(sem("bank3_full"), L.next("bank3_full"))
            L.skip("bank3_free")
            for h in range(2):
                act.wait_ge(sem("bank3_full"), L.next("bank3_full"))
                act.wait_ge(sem("head_squares_free"), L.next("head_squares_free"))
                act.activation(k_tok[:, hc(h)], psum[:, 3].rearrange("p (c n) -> p c n", n=P), ACT.Copy
                ).then_inc(sem("act_order"), L.add("act_order"))
                act.activation(blk[:, 0:4], psum[:, 3].rearrange("p (c n) -> p c n", n=P), ACT.Square
                ).then_inc(sem("bank3_free"), L.add("bank3_free"))
                act.wait_ge(sem("bank4_full"), L.next("bank4_full"))
                act.activation(blk[:, 4:8], psum[:, 4].rearrange("p (c n) -> p c n", n=P), ACT.Square
                ).then_inc(sem("bank4_free"), L.add("bank4_free"))
                skip(5)
            act.activation(z_g[:], z_g[:], ACT.Silu).then_inc(sem("z_ready"), L.add("z_ready"))
            act.wait_ge(sem("head_squares_free"), L.next("head_squares_free"))
            L.skip("head_squares_free", -1)
            act.activation(col[:, 2:4], col[:, 0:2], ACT.Sqrt, bias=eps[:, 0:1]
            ).then_inc(sem("norms_ready"), L.add("norms_ready"))
            for h in range(2):
                act.wait_ge(sem("decay_args_ready"), L.next("decay_args_ready"))
                act.activation(dec[:, hc(h)], dec[:, hc(h)], ACT.Exp).then_inc(sem("decay_ready"), L.add("decay_ready"))
            skip(6, 7, 3, 4, 5, 3, 6, 7)
            for level in range(1, LEVELS + 1):
                for h in range(2):
                    act.wait_ge(sem(f"bank{3 + h}_full"), L.next(f"bank{3 + h}_full"))
                    act.activation(prod[:, hc(h)], psum[:, 3 + h].rearrange("p (c n) -> p c n", n=P), ACT.Copy
                    ).then_inc(sem(f"bank{3 + h}_free"), L.add(f"bank{3 + h}_free"))
                    skip(*((5 + h,) if level < LEVELS else ()))
                skip(7, 3)
                if more and level <= 4:
                    which, part = divmod(level - 1, 2)
                    split_hi(2 * head + 4 + which, slots[which], (part,))
            for c in range(CH):
                act.wait_ge(sem("bank6_full"), L.next("bank6_full"))
                if c:
                    act.wait_ge(sem("bank7_free"), L.next("bank7_free"))
                act.activation(tmp_o[:], psum[:, 6, 0:P], ACT.Copy, scale=gt[:, 2, bass.ds(head * CH + c, 1)]
                ).then_inc(sem("bank6_free"), L.add("bank6_free"))
                skip(4, 5, 3)
                L.skip("bank7_full")
            act.wait_ge(sem("bank7_free"), L.next("bank7_free"))
            act.wait_ge(sem("rms_arg_ready"), L.next("rms_arg_ready"))
            act.activation(col[:, 10], col[:, 9], ACT.Sqrt, scale=1.0 / P, bias=eps[:, 0:1]
            ).then_inc(sem("rms_ready"), L.add("rms_ready"))
            for b in (4, 5):
                L.skip(f"bank{b}_full")
                act.wait_ge(sem(f"bank{b}_free"), L.next(f"bank{b}_free"))
            act.dma_start(s_state[:].unsqueeze(1), t["s_rec_in"][:, bass.ds(head, 1)]
            ).then_inc(sem("s_state_landed"), L.add("s_state_landed", 16))
            act.wait_ge(sem("bank3_full"), L.next("bank3_full"))
            act.activation(s_u[:, 0:2], psum[:, 3, 0:2 * NS].rearrange("p (k n) -> p k n", n=NS), ACT.Sqrt,
                                bias=eps[:, 0:1]).then_inc(sem("bank3_free"), L.add("bank3_free"))
            skip(4)
            act.wait_ge(sem("bank5_full"), L.next("bank5_full"))
            act.activation(s_rows[0:NS, 0:2], psum[0:NS, 5, 0:2 * P].rearrange("p (k n) -> p k n", n=P), ACT.Copy
            ).then_inc(sem("bank5_free"), L.add("bank5_free"))
            skip(6, 7)
            act.wait_ge(sem("bank3_full"), L.next("bank3_full"))
            act.activation(s_u[:, 6], psum[:, 3, 0:NS], ACT.Sqrt, scale=1.0 / P / P, bias=eps[:, 0:1]
            ).then_inc(sem("bank3_free"), L.add("bank3_free"))
            act.wait_ge(sem("s_state_ready"), L.next("s_state_ready"))
            act.dma_start(t["s_rec"][:, bass.ds(head, 1)], s_state[:].unsqueeze(1)
            ).then_inc(sem("s_state_stored"), L.add("s_state_stored", 16))
            act.dma_start(t["o_heads"][:, bass.ds(head, 1)], head_out[:].rearrange("p c n -> p (c n)").unsqueeze(1)
            ).then_inc(sem("head_output_stored"), L.add("head_output_stored", 16))
            act.dma_start(t["p_rec"][:, bass.ds(head, 1)], state[:].unsqueeze(1)
            ).then_inc(sem("state_stored"), L.add("state_stored", 16))

        def samples_out():
            act.wait_ge(sem("sample_full"), L.next("sample_full"))
            act.activation(s_tok[:], psum[0:2 * NS, 2], ACT.Copy).then_inc(sem("sample_free"), L.add("sample_free"))

        def step(head, slots, more=True):
            samples_out()
            conv_silu(head)
            gdn(head, slots, more)

        split_hi(2, 2)
        split_hi(3, 3)
        with L.loop(HEADS // 2 - 1, "act heads") as i:
            step(2 * i, (0, 1))
            step(2 * i + 1, (2, 3))
        step(HEADS - 2, (0, 1))
        step(HEADS - 1, (2, 3), more=False)

        for k in range(KT):
            act.wait_ge(sem(f"o_raw{k}_landed"), L.next(f"o_raw{k}_landed", 16))
            act.wait_ge(sem("x_back"), L.next("x_back"))
            act.activation(x_hi[:, k], o_raw[:, k], ACT.Copy).then_inc(sem("o_hi_ready"), L.add("o_hi_ready"))
        for g in range(2):
            split_hi(U_OUT + 2 * g + 2, (2 * g + 2) % RING)
            split_hi(U_OUT + 2 * g + 3, (2 * g + 3) % RING)
            samples_out()
            act.wait_ge(sem("bank3_full"), L.next("bank3_full"))
            L.skip("bank3_free")
        act.wait_ge(sem("product_free"), L.next("product_free", 16))

        def mlp(unit, name, more):
            def block(b, last=False):
                u = unit + 4 * b
                for n in range(8):
                    if n == 1:
                        split_hi(u + 2, 2)
                    if n == 4:
                        split_hi(u + 3, 3)
                    h, tile = divmod(n, 4)
                    act.wait_ge(sem("relu_square_ready"), L.next("relu_square_ready"))
                    act.activation(u_hi[:, tile, halves[h]], relu[:], ACT.Copy
                    ).then_inc(sem("u_hi_ready"), L.add("u_hi_ready"))
                samples_out()
                if not last:
                    split_hi(u + 4, 0)
                    split_hi(u + 5, 1)
                act.wait_ge(sem("bank3_full"), L.next("bank3_full"))
                L.skip("bank3_free")
                for bank in (4, 5):
                    act.wait_ge(sem(f"bank{bank}_full"), L.next(f"bank{bank}_full")), L.skip(f"bank{bank}_free")
                act.wait_ge(sem("product_free"), L.next("product_free", 24))
            with L.loop(8 if more else 7, name) as b:
                block(b)
            if not more:
                block(7, last=True)
            skip(3)

        def attention_layer():
            norm()
            for gi in range(5):
                split_hi(U_KVQ + 2 * gi + 2, (2 * gi + 2) % RING)
                split_hi(U_KVQ + 2 * gi + 3, (2 * gi + 3) % RING)
                if gi < 2:
                    act.wait_ge(sem("product_free"), L.next("product_free", 8 if gi == 0 else 4))
                else:
                    b = gi - 2
                    d = DIL[b]
                    I = HALF // d
                    for n in range(8):
                        h, tile = divmod(n, 4)
                        act.wait_ge(sem("product_free"), L.next("product_free"))
                        dst = t["q"][:, 4 * b + tile].rearrange("p (r i) -> p r i", r=d)[:, :, h * I:(h + 1) * I]
                        act.dma_start(dst, q_stage[:, n % 2].rearrange("p (r i) -> p r i", r=d)
                        ).then_inc(sem(f"q{n % 2}_stored"), L.add(f"q{n % 2}_stored", 16))
                samples_out()
                act.wait_ge(sem("bank3_full"), L.next("bank3_full")), L.skip("bank3_free")
            act.wait_ge(sem("kvq_done"), L.next("kvq_done"))
            for b in range(BRANCH):
                for h in range(2):
                    act.wait_ge(sem(f"bank{3 + h}_full"), L.next(f"bank{3 + h}_full"))
                    act.activation(v_keys[:, b, hc(h)], psum[:, 3 + h].rearrange("p (c n) -> p c n", n=P), ACT.Copy
                    ).then_inc(sem(f"bank{3 + h}_free"), L.add(f"bank{3 + h}_free"))
            act.wait_ge(sem("bank4_full"), L.next("bank4_full"))
            act.activation(s_vrow[:], psum[0:NS, 4, 0:BRANCH * P].rearrange("p (b n) -> p b n", n=P), ACT.Copy
            ).then_inc(sem("s_vrow_ready"), L.add("s_vrow_ready"))
            skip(0, 1, 2, 3)
            act.wait_ge(sem("s_scores_ready"), L.next("s_scores_ready"))
            act.activation(s_p[:], s_p[:], ACT.Exp).then_inc(sem("s_exp_ready"), L.add("s_exp_ready"))
            act.wait_ge(sem("bank4_full"), L.next("bank4_full"))
            act.activation(s_pt[:, 0], psum[:, 4, 0:8 * NS], ACT.Copy).then_inc(sem("bank4_free"), L.add("bank4_free"))
            act.wait_ge(sem("bank5_full"), L.next("bank5_full"))
            act.activation(s_pt[0:SB, 1], psum[0:SB, 5, 0:8 * NS], ACT.Copy
            ).then_inc(sem("bank5_free"), L.add("bank5_free"))
            skip(6)

            def exps(tile_, hs):
                _, _, par, nk, _ = tile_
                cols = slice((2 - nk) * P, 2 * P)
                act.wait_ge(sem("max_ready"), L.next("max_ready"))
                for n in range(4 * hs, 4 * hs + 4):
                    act.activation(prob[:, par, n, cols], prob[:, par, n, cols], ACT.Exp,
                                   bias=neg_max[:, par, n:n + 1], accum_out=stats[:, par, 1, n:n + 1]
                    ).then_inc(sem("probs_ready"), L.add("probs_ready"))

            def step(cur, nxt):
                if nxt:
                    skip(0, 1, 2, 3)
                if cur:
                    b, tile, par, nk, place = cur
                    skip(5, 5, 6)
                    L.skip("bank7_full")
                for hs in range(2):
                    if cur and nk == 2:
                        act.wait_ge(sem("bank4_full"), L.next("bank4_full"))
                        act.activation(prob_t[:, 0, hc(hs)], psum[:, 4].rearrange("p (c n) -> p c n", n=P), ACT.Copy
                        ).then_inc(sem("bank4_free"), L.add("bank4_free"))
                    if nxt:
                        exps(nxt, hs)
                if not cur:
                    return
                act.wait_ge(sem("out_taken"), L.next("out_taken"))
                for g in range(2):
                    rows = slice(g * HD, (g + 1) * HD)
                    if b == 0:
                        dst = t["att"][bass.ds(place * P + g * HD, HD), 0]
                        src = o_out[rows, par]
                    elif b == 1:
                        dst = t["att"][:, 1].rearrange("(n r) w -> n r w", r=4)[
                            par * P + g * HD:par * P + (g + 1) * HD, bass.ds(place, 1)]
                        src = o_out[rows, par].unsqueeze(1)
                    else:
                        dst = t["att"][:, 2].rearrange("(n r) w -> n r w", r=16)[:, bass.ds(2 * place + g, 1)]
                        src = o_out[rows, par].unsqueeze(1)
                    act.dma_start(dst, src).then_inc(sem(f"out{par}_stored"), L.add(f"out{par}_stored", 16))
            tiles_of(L, "act", step)
            act.wait_ge(sem("share_args_ready"), L.next("share_args_ready"))
            act.activation(share[:, 1], share[:, 0], ACT.Exp).then_inc(sem("shares_ready"), L.add("shares_ready"))
            with L.loop(CH // 2, "act merge") as i:
                for par in range(2):
                    act.wait_ge(sem(f"bank{4 + par}_full"), L.next(f"bank{4 + par}_full"))
                    L.skip(f"bank{4 + par}_free")
                    act.activation(u_hi[:, :, bass.ds((2 * i + par) * P, P)],
                                   psum[:, 4 + par].rearrange("p (c n) -> p c n", n=P), ACT.Copy
                    ).then_inc(sem("u_hi_ready"), L.add("u_hi_ready"))
            split_hi(U_MLP1, 0)
            split_hi(U_MLP1 + 1, 1)
            for bank in (4, 5):
                act.wait_ge(sem(f"bank{bank}_full"), L.next(f"bank{bank}_full")), L.skip(f"bank{bank}_free")
            skip(3)

        norm()
        mlp(U_MLP0, "act mlp0", True)
        attention_layer()
        act.wait_ge(sem("product_free"), L.next("product_free", 16))
        norm()
        mlp(U_MLP1, "act mlp1", False)
        norm(split=False)

    @block.vector
    def _(dve):
        L = Lane(dve, sem, room=["out0_stored", "out1_stored", "head_output_stored", "state_stored"])
        v = dve
        for name, n in CREDIT.items():
            v.sem_inc(sem(name), n)

        def split_lo(unit, slot, parts=(0, 1)):
            for part in parts:
                v.wait_ge(sem("weight_half_hi"), L.next("weight_half_hi"))
                for k in range(2):
                    done = v.scalar_tensor_tensor(w_lo[:, slot, 2 * part + k], w_raw[:, part, k],
                                                  gains[:, bass.ds(unit * UW + 2 * part + k, 1)],
                                                  f(w_hi[:, slot, 2 * part + k]), ALU.mult, ALU.subtract)
                done.then_inc(sem("raw_free"), L.add("raw_free"))

        def norm(split=True):
            if split:
                for k in range(KT):
                    v.wait_ge(sem("x_hi_ready"), L.next("x_hi_ready"))
                    v.tensor_tensor(x_lo[:, k], x[:, k], f(x_hi[:, k]), ALU.subtract
                    ).then_inc(sem("x_ready"), L.add("x_ready"))
                v.tensor_copy(s_lhs[:, :, 0:NS], s_x[:]).then_inc(sem("dve_order"), L.add("dve_order"))
                v.wait_ge(sem(L.last), L.value(L.last))
                v.tensor_tensor(s_lhs[:, :, NS:2 * NS], s_x[:], f(s_lhs[:, :, 0:NS]), ALU.subtract
                ).then_inc(sem("samples_ready"), L.add("samples_ready"))
            flat = s_x[:].rearrange("p k n -> p (k n)")
            v.tensor_tensor(s_tmp[:, 0], flat, flat, ALU.mult).then_inc(sem("dve_order"), L.add("dve_order"))
            v.wait_ge(sem(L.last), L.value(L.last))
            v.tensor_reduce(s_tmp[:, 1, 0:NS], s_tmp[:, 0].rearrange("p (k n) -> p n k", n=NS), AXX, ALU.add
            ).then_inc(sem("sample_squares_ready"), L.add("sample_squares_ready"))
            for k in range(KT):
                v.wait_ge(sem("square_ready"), L.next("square_ready"))
                if k == 1:
                    v.tensor_tensor(sq_sum[:], sq[:, 0], sq[:, 1], ALU.add
                    ).then_inc(sem("square_free"), L.add("square_free", 2))
                elif k > 1:
                    v.wait_ge(sem(L.last), L.value(L.last))
                    v.tensor_tensor(sq_sum[:], sq_sum[:], sq[:, k % 2], ALU.add
                    ).then_inc(sem("square_free"), L.add("square_free"))
            v.wait_ge(sem("bank5_free"), L.next("bank5_free"))
            L.skip("bank5_full")
            v.reciprocal(s_rs[:], s_rs[:]).then_inc(sem("dve_order"), L.add("dve_order"))
            v.wait_ge(sem("bank3_free"), L.next("bank3_free"))
            L.skip("bank3_full")
            v.reciprocal(rs_tok[:, 1], rs_tok[:, 0]).then_inc(sem("dve_order"), L.add("dve_order"))
            v.wait_ge(sem(L.last), L.value(L.last))
            v.tensor_tensor(sq[:, 0].rearrange("p (c n) -> p c n", n=P), o3(ident[:], CH), b3(rs_tok[:, 1], CH), ALU.mult
            ).then_inc(sem("rs_wide_ready"), L.add("rs_wide_ready"))
            for h in range(2):
                v.wait_ge(sem(f"bank{4 - h}_full"), L.next(f"bank{4 - h}_full"))
                v.tensor_copy(rs[:, halves[h]], psum[:, 4 - h]
                ).then_inc(sem(f"bank{4 - h}_free"), L.add(f"bank{4 - h}_free"))
            v.wait_ge(sem(L.last), L.value(L.last))

        def skip(*banks):
            for b in banks:
                L.skip(f"bank{b}_full"), L.skip(f"bank{b}_free")


        v.memset(eps[:], EPS).then_inc(sem("eps_set"), L.add("eps_set"))
        v.memset(ones[:], 1.0).then_inc(sem("ones_set"), L.add("ones_set"))
        v.memset(f(s_lhs[:]), 0.0).then_inc(sem("dve_order"), L.add("dve_order"))
        v.wait_ge(sem(L.last), L.value(L.last))
        v.wait_ge(sem("constants_landed"), L.next("constants_landed", 16 * len(CONSTS)))
        v.tensor_copy(lvl[:], lvl_in[:]).then_inc(sem("dve_order"), L.add("dve_order"))
        v.wait_ge(sem("x_landed"), L.next("x_landed", 16 * KT))
        v.tensor_tensor(w_ab[:], w_ab[:], b3(g_ab[:], KT, 2 * HEADS), ALU.mult
        ).then_inc(sem("w_ab_ready"), L.add("w_ab_ready"))
        norm()
        split_lo(0, 0)
        split_lo(1, 1)

        for h in range(2):
            v.wait_ge(sem(f"bank{6 + h}_full"), L.next(f"bank{6 + h}_full"))
            v.tensor_tensor(ab_feat[:, halves[h]], psum[0:2 * HEADS, 6 + h], rs[0:2 * HEADS, halves[h]], ALU.mult
            ).then_inc(sem(f"bank{6 + h}_free"), L.add(f"bank{6 + h}_free"))
        v.wait_ge(sem("bank5_full"), L.next("bank5_full"))
        v.tensor_tensor(s_ab[:], psum[0:2 * HEADS, 5, 0:NS], s_rs[0:2 * HEADS], ALU.mult
        ).then_inc(sem("bank5_free"), L.add("bank5_free"))
        v.wait_ge(sem(L.last), L.value(L.last))
        v.tensor_tensor(s_wide[:], b3(ident[0:2 * HEADS, 0:2 * HEADS], 2 * HEADS, NS), o3(s_ab[:], 2 * HEADS),
                             ALU.mult).then_inc(sem("s_wide_ready"), L.add("s_wide_ready"))
        v.wait_ge(sem("bank5_full"), L.next("bank5_full"))
        turned = psum[:, 5, 0:P].rearrange("p (c m h) -> p m h c", m=2, h=HEADS)
        three = [ab[:, n, 0:64].rearrange("p (h c) -> p h c", c=CH) for n in range(6)]
        s_three = [ab[:, n, 64:].rearrange("p (h c) -> p h c", c=CH) for n in range(6)]
        v.tensor_copy(three[0], turned[:, 0]).then_inc(sem("dve_order"), L.add("dve_order"))
        v.tensor_tensor(three[1], turned[:, 1], b3(dtb[:, 1], HEADS, CH), ALU.add
        ).then_inc(sem("bank5_free"), L.add("bank5_free"))
        v.wait_ge(sem("bank5_full"), L.next("bank5_full"))
        wide = psum[:, 5, 0:P].rearrange("p (m h n) -> p m h n", m=2, n=NS)
        v.tensor_copy(s_three[0], wide[:, 0]).then_inc(sem("dve_order"), L.add("dve_order"))
        v.tensor_tensor(s_three[1], wide[:, 1], b3(dtb[:, 1], HEADS, NS), ALU.add
        ).then_inc(sem("bank5_free"), L.add("bank5_free"))
        v.wait_ge(sem(L.last), L.value(L.last))
        v.scalar_tensor_tensor(ab[:, 2], ab[:, 1], -1.0, ab[:, 1], ALU.mult, ALU.max
        ).then_inc(sem("gate_args_ready"), L.add("gate_args_ready"))
        v.wait_ge(sem("gate_exps_ready"), L.next("gate_exps_ready"))
        v.tensor_scalar(ab[:, 0], ab[:, 0], 1.0, None, ALU.add).then_inc(sem("dve_order"), L.add("dve_order"))
        v.tensor_scalar(ab[:, 4], ab[:, 3], 1.0, None, ALU.add
        ).then_inc(sem("softplus_arg_ready"), L.add("softplus_arg_ready"))
        v.wait_ge(sem(L.last), L.value(L.last))
        v.reciprocal(beta, ab[:, 0, 0:64]).then_inc(sem("dve_order"), L.add("dve_order"))
        v.reciprocal(s_gate[:, 0], s_three[0]).then_inc(sem("dve_order"), L.add("dve_order"))
        v.scalar_tensor_tensor(ab[:, 2], ab[:, 4], -1.0, ab[:, 3], ALU.add, ALU.subtract
        ).then_inc(sem("dve_order"), L.add("dve_order"))
        v.wait_ge(sem("softplus_log_ready"), L.next("softplus_log_ready"))
        v.wait_ge(sem(L.last), L.value(L.last))
        v.tensor_tensor(ab[:, 5], ab[:, 5], ab[:, 2], ALU.subtract).then_inc(sem("dve_order"), L.add("dve_order"))
        v.wait_ge(sem(L.last), L.value(L.last))
        v.scalar_tensor_tensor(ab[:, 5], ab[:, 1], 0.0, ab[:, 5], ALU.max, ALU.add
        ).then_inc(sem("dve_order"), L.add("dve_order"))
        v.wait_ge(sem(L.last), L.value(L.last))
        v.scalar_tensor_tensor(s_three[3], s_three[5], -1.0, b3(dtb[:, 0], HEADS, NS), ALU.mult, ALU.mult
        ).then_inc(sem("dve_order"), L.add("dve_order"))
        v.scalar_tensor_tensor(three[3], three[5], -1.0, b3(dtb[:, 0], HEADS, CH), ALU.mult, ALU.mult
        ).then_inc(sem("g_ready"), L.add("g_ready"))
        v.wait_ge(sem("bank6_full"), L.next("bank6_full"))
        v.tensor_copy(g_sum, psum[:, 6, 0:64]).then_inc(sem("bank6_free"), L.add("bank6_free"))
        v.wait_ge(sem("bank7_full"), L.next("bank7_full"))
        v.tensor_copy(e_last, psum[:, 7, 0:64]).then_inc(sem("bank7_free"), L.add("bank7_free"))
        v.wait_ge(sem(L.last), L.value(L.last))
        v.tensor_tensor(e_rest, e_last, g_sum, ALU.subtract
        ).then_inc(sem("decay_sums_ready"), L.add("decay_sums_ready"))
        v.wait_ge(sem("decays_ready"), L.next("decays_ready"))
        v.tensor_scalar(e_neg, e_pos, -1.0, None, ALU.mult).then_inc(sem("dve_order"), L.add("dve_order"))
        v.wait_ge(sem(L.last), L.value(L.last))
        v.tensor_copy(g_keep[:], ab[:, 3, 0:64]).then_inc(sem("dve_order"), L.add("dve_order"))
        v.wait_ge(sem(L.last), L.value(L.last))
        v.memset(pre[:, :, 0:3], 0.0).then_inc(sem("dve_order"), L.add("dve_order"))
        v.wait_ge(sem(L.last), L.value(L.last))

        def take_product(n, first=False):
            tile, h = divmod(n, 2)
            if n == 1 and not first:
                v.wait_ge(sem("conv_stored"), L.next("conv_stored", 16))
            out = pre[:, tile, 3 + h * HALF:3 + (h + 1) * HALF] if tile < 3 else z_g[:, halves[h]]
            v.wait_ge(sem("product_full"), L.next("product_full"))
            v.tensor_tensor(out, psum[:, n % 2], rs[:, halves[h]], ALU.mult
            ).then_inc(sem("product_free"), L.add("product_free"))

        def sample_rows(head):
            v.wait_ge(sem("bank3_full"), L.next("bank3_full"))
            rows = psum[:, 3, 0:4 * NS].rearrange("p (k n) -> p k n", n=NS)
            s_in = s_ext[:, bass.ds(head, 1)].rearrange("p u k j n -> p (u k) j n")
            v.tensor_tensor(s_in[:, :, 3], rows[:, 0:3], o3(s_rs[:], 3), ALU.mult
            ).then_inc(sem("dve_order"), L.add("dve_order"))
            v.tensor_tensor(s_z[:], rows[:, 3], s_rs[:], ALU.mult).then_inc(sem("bank3_free"), L.add("bank3_free"))
            v.wait_ge(sem(L.last), L.value(L.last))
            taps = cw[:, bass.ds(head * 12, 12)].rearrange("p (k j) -> p k j", j=4).unsqueeze(3)
            v.tensor_tensor(s_taps[:], s_in, taps.to_broadcast([P, 3, 4, NS]), ALU.mult
            ).then_inc(sem("dve_order"), L.add("dve_order"))
            v.wait_ge(sem(L.last), L.value(L.last))
            v.tensor_reduce(s_qkv[:], s_taps[:].rearrange("p k j n -> p k n j"), AXX, ALU.add
            ).then_inc(sem("s_conv_ready"), L.add("s_conv_ready"))

        def conv(head):
            for n in range(3):
                v.wait_ge(sem("tap0_ready"), L.next("tap0_ready"))
                for j in range(1, 4):
                    if j > 1:
                        v.wait_ge(sem(L.last), L.value(L.last))
                    v.scalar_tensor_tensor(qkv[:, n], pre[:, n, j:j + SEQ],
                                                cw[:, bass.ds(head * 12 + n * 4 + j, 1)],
                                                qkv[:, n], ALU.mult, ALU.add
                                                ).then_inc(sem("taps_ready" if j == 3 else "dve_order"), L.add("taps_ready" if j == 3 else "dve_order"))

        def sample_step(head):
            one = bass.ds(head, 1)

            def gate(n):
                return s_gate[:, n, one].rearrange("p u n -> p (u n)")
            v.wait_ge(sem("s_silu_ready"), L.next("s_silu_ready"))
            v.tensor_tensor(s_u[:, 2:4], s_qkv[:, 0:2], s_qkv[:, 0:2], ALU.mult
            ).then_inc(sem("s_squares_ready"), L.add("s_squares_ready"))
            v.wait_ge(sem("bank3_free"), L.next("bank3_free"))
            L.skip("bank3_full")
            v.reciprocal(s_u[:, 0:2], s_u[:, 0:2]).then_inc(sem("dve_order"), L.add("dve_order"))
            v.wait_ge(sem(L.last), L.value(L.last))
            v.tensor_tensor(s_qkv[:, 0:2], s_qkv[:, 0:2], s_u[:, 0:2], ALU.mult
            ).then_inc(sem("dve_order"), L.add("dve_order"))
            v.wait_ge(sem(L.last), L.value(L.last))
            v.tensor_tensor(s_u[:, 2], s_qkv[:, 0], s_qkv[:, 1], ALU.mult
            ).then_inc(sem("s_qk_ready"), L.add("s_qk_ready"))
            v.wait_ge(sem("bank4_full"), L.next("bank4_full"))
            sk = psum[:, 4, 0:2 * NS].rearrange("p (n m) -> p m n", m=2)
            v.tensor_tensor(s_u[:, 3], sk[:, 1], gate(1), ALU.mult).then_inc(sem("dve_order"), L.add("dve_order"))
            v.tensor_tensor(s_u[:, 4], sk[:, 0], gate(1), ALU.mult).then_inc(sem("dve_order"), L.add("dve_order"))
            v.wait_ge(sem(L.last), L.value(L.last))
            v.tensor_tensor(s_u[:, 3], s_qkv[:, 2], s_u[:, 3], ALU.subtract
            ).then_inc(sem("dve_order"), L.add("dve_order"))
            v.wait_ge(sem(L.last), L.value(L.last))
            v.tensor_tensor(s_u[:, 5], s_u[:, 3], gate(0), ALU.mult).then_inc(sem("s_v_ready"), L.add("s_v_ready"))
            v.wait_ge(sem(L.last), L.value(L.last))
            v.tensor_tensor(s_u[:, 2], psum[:, 4, 2 * NS:3 * NS], s_u[:, 5], ALU.mult
            ).then_inc(sem("bank4_free"), L.add("bank4_free"))
            v.wait_ge(sem(L.last), L.value(L.last))
            v.tensor_tensor(s_u[:, 4], s_u[:, 4], s_u[:, 2], ALU.add).then_inc(sem("dve_order"), L.add("dve_order"))
            v.wait_ge(sem(L.last), L.value(L.last))
            v.tensor_tensor(s_u[:, 7], s_u[:, 4], s_u[:, 4], ALU.mult
            ).then_inc(sem("s_out_squares_ready"), L.add("s_out_squares_ready"))
            v.wait_ge(sem("bank5_free"), L.next("bank5_free"))
            L.skip("bank5_full")
            v.tensor_tensor(s_v_wide[0:NS], b3(ident[0:NS, 0:NS], NS), o3(s_rows[0:NS, 1], NS), ALU.mult
            ).then_inc(sem("s_v_wide_ready"), L.add("s_v_wide_ready"))
            v.tensor_tensor(s_state[:], s_state[:], b3(gate(1), NS), ALU.mult
            ).then_inc(sem("dve_order"), L.add("dve_order"))
            v.wait_ge(sem(L.last), L.value(L.last))
            for h in range(2):
                v.wait_ge(sem(f"bank{6 + h}_full"), L.next(f"bank{6 + h}_full"))
                v.tensor_tensor(s_state[:, hc(h)], s_state[:, hc(h)], psum[:, 6 + h].rearrange("p (c n) -> p c n", n=P),
                                     ALU.add).then_inc(sem(f"bank{6 + h}_free"), L.add(f"bank{6 + h}_free"))
            v.wait_ge(sem("bank3_free"), L.next("bank3_free"))
            L.skip("bank3_full")
            v.reciprocal(s_u[:, 6], s_u[:, 6]).then_inc(sem("s_state_ready"), L.add("s_state_ready"))
            v.wait_ge(sem(L.last), L.value(L.last))
            v.scalar_tensor_tensor(s_u[:, 4], s_u[:, 4], float(P) ** -0.5, s_u[:, 6], ALU.mult, ALU.mult
            ).then_inc(sem("dve_order"), L.add("dve_order"))
            v.wait_ge(sem(L.last), L.value(L.last))
            v.tensor_tensor(s_og[:, one].rearrange("p u n -> p (u n)"), s_u[:, 4], s_z[:], ALU.mult
            ).then_inc(sem("dve_order"), L.add("dve_order"))

        def gdn(head, slots, more):
            hs = bass.ds(head * CH, CH)
            four = "p (c n) -> p c n"
            v.tensor_tensor(inv[:], o3(tri[:], CH), b3(g_keep[:, hs], CH), ALU.mult
            ).then_inc(sem("decay_terms_ready"), L.add("decay_terms_ready"))
            for h in range(2):
                v.wait_ge(sem("bank5_full"), L.next("bank5_full"))
                v.tensor_copy(v_tok[:, hc(h)], psum[:, 5].rearrange(four, n=P)
                ).then_inc(sem("bank5_free"), L.add("bank5_free"))
                v.wait_ge(sem("bank4_free"), L.next("bank4_free"))
                L.skip("bank3_full"), L.skip("bank3_free"), L.skip("bank4_full")
                v.tensor_reduce(col[:, 0, hc(h)], blk[:, 0:4], AXX, ALU.add
                ).then_inc(sem("dve_order"), L.add("dve_order"))
                v.tensor_reduce(col[:, 1, hc(h)], blk[:, 4:8], AXX, ALU.add
                ).then_inc(sem("head_squares_free"), L.add("head_squares_free"))
            v.wait_ge(sem("head_output_stored"), L.next("head_output_stored", 16))
            for h in range(2):
                v.wait_ge(sem(f"bank{6 + h}_full"), L.next(f"bank{6 + h}_full"))
                v.tensor_tensor(dec[:, hc(h)], psum[:, 6 + h].rearrange(four, n=P),
                                     b3(gt[:, 1, bass.ds(head * CH + 4 * h, 4)], 4), ALU.subtract
                                     ).then_inc(sem(f"bank{6 + h}_free"), L.add(f"bank{6 + h}_free"))
                v.wait_ge(sem(L.last), L.value(L.last))
                v.tensor_tensor(dec[:, hc(h)], dec[:, hc(h)], o3(msk[:], 4), ALU.min
                ).then_inc(sem("decay_args_ready"), L.add("decay_args_ready"))
            v.wait_ge(sem("norms_ready"), L.next("norms_ready"))
            v.reciprocal(col[:, 4:6], col[:, 2:4]).then_inc(sem("dve_order"), L.add("dve_order"))
            v.tensor_tensor(v_tok[:], v_tok[:], b3(col[:, 2], CH), ALU.mult
            ).then_inc(sem("dve_order"), L.add("dve_order"))
            v.wait_ge(sem(L.last), L.value(L.last))
            v.tensor_tensor(col[:, 6], col[:, 4], col[:, 4], ALU.mult).then_inc(sem("dve_order"), L.add("dve_order"))
            v.wait_ge(sem(L.last), L.value(L.last))
            v.tensor_tensor(col[:, 6], col[:, 6], gt[:, 0, hs], ALU.mult
            ).then_inc(sem("dve_order"), L.add("dve_order"))
            v.wait_ge(sem(L.last), L.value(L.last))
            v.tensor_tensor(col[:, 7], col[:, 6], gt[:, 4, hs], ALU.mult
            ).then_inc(sem("dve_order"), L.add("dve_order"))
            v.tensor_scalar(col[:, 5], col[:, 5], float(P) ** -0.5, None, ALU.mult
            ).then_inc(sem("dve_order"), L.add("dve_order"))
            for h in range(2):
                v.wait_ge(sem("decay_ready"), L.next("decay_ready"))
                v.tensor_tensor(blk[:, hc(h)], dec[:, hc(h)], b3(col[:, 6, hc(h)], 4), ALU.mult
                ).then_inc(sem("dve_order"), L.add("dve_order"))
            v.wait_ge(sem(L.last), L.value(L.last))
            for p, b in enumerate((3, 4, 5, 3)):
                v.wait_ge(sem(f"bank{b}_full"), L.next(f"bank{b}_full"))
                both = psum[:, b].rearrange("p (c m n) -> p m c n", m=2, n=P)
                two = slice(2 * p, 2 * p + 2)
                v.tensor_tensor(low[:, two], both[:, 0], blk[:, two], ALU.mult
                ).then_inc(sem("dve_order"), L.add("dve_order"))
                v.tensor_tensor(att[:, two], both[:, 1], dec[:, two], ALU.mult
                ).then_inc(sem(f"bank{b}_free"), L.add(f"bank{b}_free"))
            v.wait_ge(sem(L.last), L.value(L.last))
            v.tensor_tensor(blk[:], low[:], o3(lvl[:, 0], CH), ALU.mult
            ).then_inc(sem("blocks_ready"), L.add("blocks_ready"))
            v.wait_ge(sem(L.last), L.value(L.last))
            v.tensor_tensor(inv_t[:], o3(ident[:], CH), blk[:], ALU.subtract
            ).then_inc(sem("inverse_t_ready"), L.add("inverse_t_ready"))
            for h in range(2):
                v.wait_ge(sem(f"bank{6 + h}_full"), L.next(f"bank{6 + h}_full"))
                v.tensor_tensor(inv[:, hc(h)], o3(ident[:], 4), psum[:, 6 + h].rearrange(four, n=P), ALU.subtract
                ).then_inc(sem(f"bank{6 + h}_free"), L.add(f"bank{6 + h}_free"))
            v.wait_ge(sem(L.last), L.value(L.last))
            v.tensor_tensor(blk[:], low[:], o3(lvl[:, 1], CH), ALU.mult
            ).then_inc(sem("blocks_ready"), L.add("blocks_ready"))
            if more:
                take_product(2)
                take_product(3)
            for level in range(1, LEVELS + 1):
                for h in range(2):
                    v.wait_ge(sem(f"bank{3 + h}_full"), L.next(f"bank{3 + h}_full"))
                    L.skip(f"bank{3 + h}_free")
                if level < LEVELS:
                    v.tensor_tensor(blk[:], low[:], o3(lvl[:, level + 1], CH), ALU.mult
                    ).then_inc(sem("blocks_ready"), L.add("blocks_ready"))
                v.wait_ge(sem(L.last), L.value(L.last))
                for h in range(2):
                    if level < LEVELS:
                        v.wait_ge(sem(f"bank{5 + h}_full"), L.next(f"bank{5 + h}_full"))
                        v.tensor_tensor(inv[:, hc(h)], inv[:, hc(h)], psum[:, 5 + h].rearrange(four, n=P),
                                             ALU.subtract
                                             ).then_inc(sem(f"bank{5 + h}_free"), L.add(f"bank{5 + h}_free"))
                    b = (7, 3)[h]
                    v.wait_ge(sem(f"bank{b}_full"), L.next(f"bank{b}_full"))
                    v.tensor_tensor(inv_t[:, hc(h)], inv_t[:, hc(h)], psum[:, b].rearrange(four, n=P),
                                         ALU.subtract).then_inc(sem(f"bank{b}_free"), L.add(f"bank{b}_free"))
                if more and level <= 4:
                    which, part = divmod(level - 1, 2)
                    split_lo(2 * head + 4 + which, slots[which], (part,))
                if more and level == 5:
                    take_product(4)
            v.wait_ge(sem(L.last), L.value(L.last))
            v.wait_ge(sem("state_stored"), L.next("state_stored", 16))
            v.memset(state[:], 0.0).then_inc(sem("state_ready"), L.add("state_ready"))
            for c in range(CH):
                one = bass.ds(head * CH + c, 1)
                v.wait_ge(sem("bank4_full"), L.next("bank4_full"))
                v.wait_ge(sem(L.last), L.value(L.last))
                v.scalar_tensor_tensor(vz[:, 0], psum[:, 4, 0:P], gt[:, 3, one], v_tok[:, c], ALU.mult, ALU.add
                ).then_inc(sem("bank4_free"), L.add("bank4_free"))
                v.wait_ge(sem("bank5_full"), L.next("bank5_full"))
                v.tensor_scalar(vz[:, 2], psum[:, 5, 0:P], col[:, 7, c:c + 1], None, ALU.mult
                ).then_inc(sem("v_for_state_ready"), L.add("v_for_state_ready"))
                v.tensor_scalar(vz[:, 1], psum[:, 5, 0:P], col[:, 6, c:c + 1], None, ALU.mult
                ).then_inc(sem("bank5_free"), L.add("bank5_free"))
                v.wait_ge(sem("bank3_full"), L.next("bank3_full"))
                v.scalar_tensor_tensor(state[:], state[:], gt[:, 5, one], psum[:, 3, 0:P], ALU.mult, ALU.add
                ).then_inc(sem("bank3_free"), L.add("bank3_free"))
                v.wait_ge(sem("bank6_free"), L.next("bank6_free"))
                L.skip("bank6_full")
                if more and c == 3:
                    take_product(5)
                v.wait_ge(sem("bank7_full"), L.next("bank7_full"))
                v.tensor_tensor(o_tok[:, c], psum[:, 7, 0:P], tmp_o[:], ALU.add
                ).then_inc(sem("bank7_free"), L.add("bank7_free"))
            v.wait_ge(sem(L.last), L.value(L.last))
            v.tensor_tensor(inv[:], o_tok[:], o_tok[:], ALU.mult).then_inc(sem("dve_order"), L.add("dve_order"))
            v.wait_ge(sem(L.last), L.value(L.last))
            v.tensor_reduce(col[:, 8], inv[:], AXX, ALU.add).then_inc(sem("dve_order"), L.add("dve_order"))
            v.tensor_tensor(col[:, 11], col[:, 5], col[:, 5], ALU.mult).then_inc(sem("dve_order"), L.add("dve_order"))
            v.wait_ge(sem(L.last), L.value(L.last))
            v.tensor_tensor(col[:, 9], col[:, 8], col[:, 11], ALU.mult
            ).then_inc(sem("rms_arg_ready"), L.add("rms_arg_ready"))
            v.wait_ge(sem("rms_ready"), L.next("rms_ready"))
            v.reciprocal(col[:, 12], col[:, 10]).then_inc(sem("dve_order"), L.add("dve_order"))
            v.wait_ge(sem(L.last), L.value(L.last))
            v.tensor_tensor(col[:, 13], col[:, 12], col[:, 5], ALU.mult).then_inc(sem("dve_order"), L.add("dve_order"))
            v.wait_ge(sem(L.last), L.value(L.last))
            v.tensor_tensor(o_tok[:], o_tok[:], b3(col[:, 13], CH), ALU.mult
            ).then_inc(sem("o_tok_ready"), L.add("o_tok_ready"))
            v.wait_ge(sem("z_ready"), L.next("z_ready"))
            for h in range(2):
                b = 4 + h
                v.wait_ge(sem(f"bank{b}_full"), L.next(f"bank{b}_full"))
                v.tensor_tensor(head_out[:, hc(h)], psum[:, b].rearrange(four, n=P),
                                     z_g[:, halves[h]].rearrange(four, n=P), ALU.mult
                                     ).then_inc(sem(f"bank{b}_free"), L.add(f"bank{b}_free"))
            if more:
                v.wait_ge(sem(L.last), L.value(L.last))
                take_product(6)
                take_product(7)
            else:
                v.wait_ge(sem("conv_stored"), L.next("conv_stored", 16))
            sample_step(head)
            v.wait_ge(sem(L.last), L.value(L.last))

        def step(head, slots, more=True):
            sample_rows(head)
            conv(head)
            if more:
                v.wait_ge(sem(L.last), L.value(L.last))
                take_product(0)
                take_product(1)
            gdn(head, slots, more)

        for n in range(8):
            if n in (1, 4):
                split_lo(2 + (n == 4), 2 + (n == 4))
            take_product(n, first=True)
        with L.loop(HEADS // 2 - 1, "dve heads") as i:
            step(2 * i, (0, 1))
            step(2 * i + 1, (2, 3))
        step(HEADS - 2, (0, 1))
        step(HEADS - 1, (2, 3), more=False)

        def x_back(k):
            v.tensor_tensor(x[:, k], f(x_hi[:, k]), f(x_lo[:, k]), ALU.add).then_inc(sem("x_back"), L.add("x_back"))
        x_back(0)
        v.tensor_copy(s_lhs[:, :, 0:NS], s_og[:]).then_inc(sem("dve_order"), L.add("dve_order"))
        v.wait_ge(sem(L.last), L.value(L.last))
        v.tensor_tensor(s_lhs[:, :, NS:2 * NS], s_og[:], f(s_lhs[:, :, 0:NS]), ALU.subtract
        ).then_inc(sem("samples_ready"), L.add("samples_ready"))
        for k in range(KT):
            if k + 1 < KT:
                x_back(k + 1)
            v.wait_ge(sem("o_hi_ready"), L.next("o_hi_ready"))
            v.tensor_tensor(x_lo[:, k], o_raw[:, k], f(x_hi[:, k]), ALU.subtract
            ).then_inc(sem("o_split"), L.add("o_split"))

        def add_products(n, tile0):
            h, tile = divmod(n, 4)
            v.wait_ge(sem("product_full"), L.next("product_full"))
            out = x[:, tile0 + tile, halves[h]]
            v.tensor_tensor(out, out, psum[:, TAKES[n % 4]], ALU.add).then_inc(sem("product_free"), L.add("product_free"))

        for g in range(2):
            for n in range(8):
                if n in (1, 4):
                    u = 2 * g + 2 + (n == 4)
                    split_lo(U_OUT + u, u % RING)
                add_products(n, 4 * g)
            v.wait_ge(sem("bank3_full"), L.next("bank3_full"))
            out = s_x[:, 4 * g:4 * g + 4]
            v.tensor_tensor(out, out, psum[:, 3, 0:4 * NS].rearrange("p (k n) -> p k n", n=NS), ALU.add
            ).then_inc(sem("bank3_free"), L.add("bank3_free"))
        v.wait_ge(sem(L.last), L.value(L.last))

        def mlp(unit, name, more):
            v.memset(f(u_lhs[:]), 0.0).then_inc(sem("dve_order"), L.add("dve_order"))
            v.memset(s_acc[:], 0.0).then_inc(sem("dve_order"), L.add("dve_order"))
            v.wait_ge(sem(L.last), L.value(L.last))

            def block(b, last=False):
                u = unit + 4 * b
                for n in range(8):
                    if n in (1, 4):
                        split_lo(u + 2 + (n == 4), 2 + (n == 4))
                    h, tile = divmod(n, 4)
                    v.wait_ge(sem("product_full"), L.next("product_full"))
                    v.wait_ge(sem(L.last), L.value(L.last))
                    v.scalar_tensor_tensor(relu[:], psum[:, TAKES[n % 4]], 0.0, rs[:, halves[h]], ALU.max, ALU.mult
                    ).then_inc(sem("product_free"), L.add("product_free"))
                    v.wait_ge(sem(L.last), L.value(L.last))
                    v.tensor_tensor(relu[:], relu[:], relu[:], ALU.mult
                    ).then_inc(sem("relu_square_ready"), L.add("relu_square_ready"))
                    v.wait_ge(sem("u_hi_ready"), L.next("u_hi_ready"))
                    v.tensor_tensor(u_lo[:, tile, halves[h]], relu[:], f(u_hi[:, tile, halves[h]]), ALU.subtract
                    ).then_inc(sem("u_ready"), L.add("u_ready"))
                for j in range(2):
                    for n in range(8):
                        if n == 1 and not last:
                            split_lo(u + 4 + j, j)
                        if n == 3 and j == 0:
                            v.wait_ge(sem("bank3_full"), L.next("bank3_full"))
                            s4 = s_tmp[:, 0, 0:4 * NS].rearrange("p (k n) -> p k n", n=NS)
                            v.scalar_tensor_tensor(s4, psum[:, 3, 0:4 * NS].rearrange("p (k n) -> p k n", n=NS), 0.0,
                                                        o3(s_rs[:], 4), ALU.max, ALU.mult
                                                        ).then_inc(sem("bank3_free"), L.add("bank3_free"))
                            v.wait_ge(sem(L.last), L.value(L.last))
                            v.tensor_tensor(s4, s4, s4, ALU.mult).then_inc(sem("dve_order"), L.add("dve_order"))
                            v.wait_ge(sem(L.last), L.value(L.last))
                            v.tensor_copy(u_lhs[:, :, 0:NS], s4).then_inc(sem("dve_order"), L.add("dve_order"))
                            v.wait_ge(sem(L.last), L.value(L.last))
                            v.tensor_tensor(u_lhs[:, :, NS:2 * NS], s4, f(u_lhs[:, :, 0:NS]), ALU.subtract
                            ).then_inc(sem("u_samples_ready"), L.add("u_samples_ready"))
                        add_products(n, 4 * j)
                    v.wait_ge(sem(f"bank{4 + j}_full"), L.next(f"bank{4 + j}_full"))
                    v.tensor_tensor(s_acc[:, halves[j]], s_acc[:, halves[j]], psum[0:2 * NS, 4 + j], ALU.add
                    ).then_inc(sem(f"bank{4 + j}_free"), L.add(f"bank{4 + j}_free"))
            with L.loop(8 if more else 7, name) as b:
                block(b)
            if not more:
                block(7, last=True)
            v.wait_ge(sem("bank3_full"), L.next("bank3_full"))
            v.tensor_tensor(s_x[:], s_x[:], psum[:, 3, 0:KT * NS].rearrange("p (k n) -> p k n", n=NS), ALU.add
            ).then_inc(sem("bank3_free"), L.add("bank3_free"))
            v.wait_ge(sem(L.last), L.value(L.last))

        def attention_layer():
            norm()
            stored = [0, 0]
            for gi in range(5):
                tiles = 2 if gi == 1 else 4
                if gi in (2, 3):
                    v.memset(k_mask[(3 - gi) * HD:(4 - gi) * HD, :, gi - 2], 0.0
                    ).then_inc(sem("dve_order"), L.add("dve_order"))
                for n in range(2 * tiles):
                    if n in (1, tiles):
                        which = n == tiles
                        split_lo(U_KVQ + 2 * gi + 2 + which, (2 * gi + 2 + which) % RING)
                    h, tile = divmod(n, tiles)
                    b = gi - 2 if gi > 1 else 2 * gi + tile // 2
                    d = DIL[b]
                    I = HALF // d

                    def by_class(ap):
                        return ap.rearrange("p (r i) -> p i r", r=d)[:, h * I:(h + 1) * I]
                    src = psum[:, TAKES[n % 4]].rearrange("p (i r) -> p i r", r=d)
                    scale = rs[:, halves[h]].rearrange("p (i r) -> p i r", r=d)
                    v.wait_ge(sem("product_full"), L.next("product_full"))
                    if gi < 2 and tile % 2 == 0:
                        for g in range(2):
                            rows = slice(g * HD, (g + 1) * HD)
                            done = v.tensor_tensor(by_class(k_mask[rows, b, g]), src[rows], scale[rows], ALU.mult)
                            done.then_inc(sem("product_free" if g else "dve_order"), L.add("product_free" if g else "dve_order"))
                    elif gi < 2:
                        v.tensor_tensor(by_class(v_feat[:, b]), src, scale, ALU.mult
                        ).then_inc(sem("product_free"), L.add("product_free"))
                    else:
                        if stored[n % 2]:
                            v.wait_ge(sem(f"q{n % 2}_stored"), L.next(f"q{n % 2}_stored", 16))
                        stored[n % 2] = 1
                        v.scalar_tensor_tensor(q_stage[:, n % 2].rearrange("p (r i) -> p i r", r=d), src, HD ** -0.5,
                                                    scale, ALU.mult, ALU.mult
                                                    ).then_inc(sem("product_free"), L.add("product_free"))
                v.wait_ge(sem("bank3_full"), L.next("bank3_full"))
                rows = psum[:, 3, 0:tiles * NS].rearrange("p (k n) -> p k n", n=NS)
                if gi < 2:
                    v.tensor_tensor(s_kv[:, 4 * gi:4 * gi + tiles], rows, o3(s_rs[:], tiles), ALU.mult
                    ).then_inc(sem("bank3_free"), L.add("bank3_free"))
                else:
                    v.scalar_tensor_tensor(s_q[:, 4 * b:4 * b + 4], rows, HD ** -0.5, o3(s_rs[:], 4), ALU.mult,
                                                ALU.mult).then_inc(sem("bank3_free"), L.add("bank3_free"))
            v.wait_ge(sem(L.last), L.value(L.last))
            v.memset(s_qz[:], 0.0).then_inc(sem("kvq_done"), L.add("kvq_done"))
            skip(3, 4, 3, 4, 3, 4)
            L.skip("bank4_full")
            v.wait_ge(sem(L.last), L.value(L.last))
            for g in range(2):
                rows = slice(g * HD, (g + 1) * HD)
                for b in range(BRANCH):
                    v.tensor_copy(s_qz[rows, b].rearrange("p n (j g) -> p j g n", g=2)[:, :, g],
                                       s_q[rows, 4 * b:4 * b + 4]).then_inc(sem("dve_order"), L.add("dve_order"))
            v.wait_ge(sem("attention_constants_landed"), L.next("attention_constants_landed", 16 * 6))
            for b, at_key in ((1, SA + 64), (2, SA + 81), (0, SA + 82)):
                v.tensor_copy(s_keys[:, :, at_key], s_kv[:, 2 * b]).then_inc(sem("s_keys_ready"), L.add("s_keys_ready"))
            for k in range(4):
                v.wait_ge(sem(f"bank{k}_full"), L.next(f"bank{k}_full"))
                v.tensor_tensor(s_p[:, 2 * k:2 * k + 2],
                                     psum[0:8, k].rearrange("p (n c) -> p n c", c=256)[:, :, 0:SK],
                                     o3(s_bias[:], 2), ALU.add).then_inc(sem(f"bank{k}_free"), L.add(f"bank{k}_free"))
            v.wait_ge(sem(L.last), L.value(L.last))
            v.tensor_reduce(s_pm[:, 0], s_p[:], AXX, ALU.max).then_inc(sem("dve_order"), L.add("dve_order"))
            v.wait_ge(sem(L.last), L.value(L.last))
            v.tensor_tensor(s_p[:], s_p[:], b3(s_pm[:, 0], NS, SK), ALU.subtract
            ).then_inc(sem("s_scores_ready"), L.add("s_scores_ready"))
            v.wait_ge(sem("s_exp_ready"), L.next("s_exp_ready"))
            v.tensor_reduce(s_pm[:, 1], s_p[:], AXX, ALU.add).then_inc(sem("dve_order"), L.add("dve_order"))
            v.wait_ge(sem(L.last), L.value(L.last))
            v.reciprocal(s_pm[:, 0], s_pm[:, 1]).then_inc(sem("dve_order"), L.add("dve_order"))
            v.wait_ge(sem(L.last), L.value(L.last))
            v.tensor_tensor(s_p[:], s_p[:], b3(s_pm[:, 0], NS, SK), ALU.mult
            ).then_inc(sem("s_probs_ready"), L.add("s_probs_ready"))
            skip(4, 5)
            v.wait_ge(sem("bank6_full"), L.next("bank6_full"))
            s_out = s_tmp[:, 3, 0:4 * NS].rearrange("p (j n) -> p j n", n=NS)
            for g in range(2):
                rows = slice(g * HD, (g + 1) * HD)
                v.tensor_copy(s_out[rows], psum[rows, 6, 0:8 * NS].rearrange("p (n j g) -> p g j n", j=4, g=2)[:, g]
                ).then_inc(sem("bank6_free" if g else "dve_order"), L.add("bank6_free" if g else "dve_order"))

            def bias_of(b):
                v.wait_ge(sem(L.last), L.value(L.last))
                for kt, which in (((0, 0), (1, 1)) if b < 2 else ((1, 2),)):
                    v.tensor_tensor(bias[:, :, kt * P:(kt + 1) * P], o3(dist[:, which], 8), b3(slopes[:, b], 8),
                                         ALU.mult).then_inc(sem("dve_order"), L.add("dve_order"))
                v.wait_ge(sem(L.last), L.value(L.last))

            def biased(tile_, hs):
                _, _, par, nk, _ = tile_
                cols = slice((2 - nk) * P, 2 * P)
                for j in (2 * hs, 2 * hs + 1):
                    v.wait_ge(sem(f"bank{j}_full"), L.next(f"bank{j}_full"))
                    two = slice(2 * j, 2 * j + 2)
                    v.tensor_tensor(prob[:, par, two, cols], psum[:, j].rearrange("p (g c) -> p g c", g=2)[:, :, cols],
                                    bias[:, two, cols], ALU.add).then_inc(sem(f"bank{j}_free"), L.add(f"bank{j}_free"))

            def maxima(tile_, hs):
                _, _, par, nk, _ = tile_
                big = stats[:, par, 0, hc(hs)]
                v.wait_ge(sem(L.last), L.value(L.last))
                v.tensor_reduce(big, prob[:, par, hc(hs), (2 - nk) * P:2 * P], AXX, ALU.max
                ).then_inc(sem("dve_order"), L.add("dve_order"))
                v.wait_ge(sem(L.last), L.value(L.last))
                v.tensor_scalar(neg_max[:, par, hc(hs)], big, -1.0, None, ALU.mult
                ).then_inc(sem("max_ready"), L.add("max_ready"))

            def turned(nk, hs):
                if nk == 2:
                    skip(4)
                v.wait_ge(sem("bank5_full"), L.next("bank5_full"))
                v.tensor_copy(prob_t[:, 1, hc(hs)], psum[:, 5].rearrange("p (c n) -> p c n", n=P)
                ).then_inc(sem("bank5_free"), L.add("bank5_free"))

            def outputs(par):
                v.wait_ge(sem(f"out{par}_stored"), L.next(f"out{par}_stored", 32))
                v.tensor_copy(o_out[:, par, 8 * HD:], stats[:, par].rearrange("p m s -> p (m s)")
                ).then_inc(sem("dve_order"), L.add("dve_order"))
                for hs in range(2):
                    v.wait_ge(sem(f"bank{6 + hs}_full"), L.next(f"bank{6 + hs}_full"))
                    for g in range(2):
                        dst = o_out[:, par, 0:8 * HD].rearrange("p (g j d) -> p g j d", g=2, j=4)[:, g, 2 * hs:2 * hs + 2]
                        src = psum[:, 6 + hs].rearrange("p (j g c) -> p g j c", g=2, c=P)[:, g, :, g * HD:(g + 1) * HD]
                        mark = ("bank6_free", "out_taken")[hs] if g else "dve_order"
                        v.tensor_copy(dst, src).then_inc(sem(mark), L.add(mark))

            def step(cur, nxt):
                if nxt and (cur is None or nxt[0] != cur[0]):
                    bias_of(nxt[0])
                if cur:
                    turned(cur[3], 0)
                if nxt:
                    v.wait_ge(sem(L.last), L.value(L.last))
                    biased(nxt, 0)
                    maxima(nxt, 0)
                    biased(nxt, 1)
                if cur:
                    turned(cur[3], 1)
                if nxt:
                    maxima(nxt, 1)
                if cur:
                    outputs(cur[2])
            tiles_of(L, "dve", step)

            v.wait_ge(sem("merge_stats_landed"), L.next("merge_stats_landed", 16 * BRANCH))
            v.wait_ge(sem(L.last), L.value(L.last))
            big, sums = merge_stats[:, :, :, 0], merge_stats[:, :, :, 1]
            v.tensor_tensor(total[:, 0], big[:, :, 0], big[:, :, 1], ALU.max).then_inc(sem("dve_order"), L.add("dve_order"))
            v.wait_ge(sem(L.last), L.value(L.last))
            v.tensor_tensor(total[:, 1], total[:, 0], big[:, :, 2], ALU.max).then_inc(sem("dve_order"), L.add("dve_order"))
            v.wait_ge(sem(L.last), L.value(L.last))
            for b in range(BRANCH):
                mark = "share_args_ready" if b == 2 else "dve_order"
                v.tensor_tensor(share[:, 0, :, b], big[:, :, b], total[:, 1], ALU.subtract).then_inc(sem(mark), L.add(mark))
            v.wait_ge(sem("shares_ready"), L.next("shares_ready"))
            v.tensor_tensor(share[:, 2], share[:, 1], sums, ALU.mult).then_inc(sem("dve_order"), L.add("dve_order"))
            v.wait_ge(sem(L.last), L.value(L.last))
            v.tensor_tensor(total[:, 0], share[:, 2, :, 0], share[:, 2, :, 1], ALU.add
            ).then_inc(sem("dve_order"), L.add("dve_order"))
            v.wait_ge(sem(L.last), L.value(L.last))
            v.tensor_tensor(total[:, 2], total[:, 0], share[:, 2, :, 2], ALU.add
            ).then_inc(sem("dve_order"), L.add("dve_order"))
            v.wait_ge(sem(L.last), L.value(L.last))
            v.reciprocal(total[:, 3], total[:, 2]).then_inc(sem("dve_order"), L.add("dve_order"))
            v.wait_ge(sem(L.last), L.value(L.last))
            for b in range(BRANCH):
                v.tensor_tensor(share[:, 3, :, b], share[:, 1, :, b], total[:, 3], ALU.mult
                ).then_inc(sem("dve_order"), L.add("dve_order"))
            v.wait_ge(sem(L.last), L.value(L.last))
            with L.loop(CH // 2, "dve merge") as i:
                for par in range(2):
                    out = merged[:, par].rearrange("p (j g d) -> p j g d", g=2, d=HD)
                    more = part[:].rearrange("p (j g d) -> p j g d", g=2, d=HD)
                    v.wait_ge(sem(f"merge{par}_landed"), L.next(f"merge{par}_landed", 16))
                    for b in range(BRANCH):
                        w = share[:, 3, bass.ds(2 * i + par, 1), b].rearrange("p u (j g) -> p (u j) g", g=2)
                        mark = "merge_free" if b == 2 else "dve_order"
                        v.tensor_tensor(more if b else out, merge[:, par, b].rearrange("p (g j d) -> p j g d", g=2, j=4),
                                        w.unsqueeze(3).to_broadcast([P, 4, 2, HD]), ALU.mult
                        ).then_inc(sem(mark), L.add(mark))
                        if b:
                            v.wait_ge(sem(L.last), L.value(L.last))
                            mark = "merged_ready" if b == 2 else "dve_order"
                            v.tensor_tensor(out, out, more, ALU.add).then_inc(sem(mark), L.add(mark))
                            v.wait_ge(sem(L.last), L.value(L.last))
                for par in range(2):
                    v.wait_ge(sem("u_hi_ready"), L.next("u_hi_ready"))
                    toks = bass.ds((2 * i + par) * P, P)
                    L.skip(f"bank{4 + par}_full")
                    v.tensor_tensor(u_lo[:, :, toks], psum[:, 4 + par].rearrange("p (c n) -> p c n", n=P),
                                    f(u_hi[:, :, toks]), ALU.subtract
                    ).then_inc(sem(f"bank{4 + par}_free"), L.add(f"bank{4 + par}_free"))
            v.wait_ge(sem(L.last), L.value(L.last))
            v.memset(f(u_lhs[:]), 0.0).then_inc(sem("dve_order"), L.add("dve_order"))
            v.wait_ge(sem(L.last), L.value(L.last))
            v.tensor_copy(u_lhs[:, :, 0:NS], s_out).then_inc(sem("dve_order"), L.add("dve_order"))
            v.wait_ge(sem(L.last), L.value(L.last))
            v.tensor_tensor(u_lhs[:, :, NS:2 * NS], s_out, f(u_lhs[:, :, 0:NS]), ALU.subtract
            ).then_inc(sem("u_samples_ready"), L.add("u_samples_ready"))
            for j in range(2):
                for n in range(8):
                    if n == 1:
                        split_lo(U_MLP1 + j, j)
                    add_products(n, 4 * j)
                v.wait_ge(sem(f"bank{4 + j}_full"), L.next(f"bank{4 + j}_full"))
                v.tensor_copy(s_acc[:, halves[j]], psum[0:2 * NS, 4 + j]
                ).then_inc(sem(f"bank{4 + j}_free"), L.add(f"bank{4 + j}_free"))
            v.wait_ge(sem("bank3_full"), L.next("bank3_full"))
            v.tensor_tensor(s_x[:], s_x[:], psum[:, 3, 0:KT * NS].rearrange("p (k n) -> p k n", n=NS), ALU.add
            ).then_inc(sem("bank3_free"), L.add("bank3_free"))
            v.wait_ge(sem(L.last), L.value(L.last))

        norm()
        mlp(U_MLP0, "dve mlp0", True)
        attention_layer()
        norm()
        mlp(U_MLP1, "dve mlp1", False)
        norm(split=False)
        for k in range(KT):
            v.scalar_tensor_tensor(x[:, k], x[:, k], g_fin[:, k:k + 1], rs[:], ALU.mult, ALU.mult
            ).then_inc(sem("y_ready"), L.add("y_ready"))
        v.tensor_tensor(s_x[:], s_x[:], o3(s_rs[:], KT), ALU.mult).then_inc(sem("dve_order"), L.add("dve_order"))
        v.wait_ge(sem(L.last), L.value(L.last))
        v.tensor_tensor(s_x[:], s_x[:], b3(g_fin[:], KT, NS), ALU.mult).then_inc(sem("y_ready"), L.add("y_ready"))

    @block.tensor
    def _(pe):
        L = Lane(pe, sem, room=["product_free", "sample_free", "out_taken"] + [f"bank{b}_free" for b in range(8)])
        mm = nc.tensor.matmul

        def product(n, slots, tile, h, xh, xl, kts, width=P):
            pe.wait_ge(sem("product_free"), L.next("product_free"))
            for k in range(kts):
                slot, kk = slots[k // UW], k % UW
                whi = w_hi[:, slot, kk, tile * P:(tile + 1) * P]
                wlo = w_lo[:, slot, kk, tile * P:(tile + 1) * P]
                mm(psum[:, TAKES[n % 4]], whi, xh[:, k, halves[h]], start=k == 0, stop=False)
                mm(psum[:, TAKES[n % 4]], whi, xl[:, k, halves[h]], start=False, stop=False)
                done = mm(psum[:, TAKES[n % 4]], wlo, xh[:, k, halves[h]], start=False, stop=k == kts - 1)
            done.then_inc(sem("product_full"), L.add("product_full"))

        def first_products(slots, ready):
            pe.wait_ge(sem("product_free"), L.next("product_free", 4))
            for k in range(KT):
                pe.wait_ge(sem(ready), L.next(ready))
                slot, kk = slots[k // UW], k % UW
                for n in range(4):
                    whi = w_hi[:, slot, kk, n * P:(n + 1) * P]
                    wlo = w_lo[:, slot, kk, n * P:(n + 1) * P]
                    mm(psum[:, TAKES[n]], whi, x_hi[:, k, halves[0]], start=k == 0, stop=False)
                    mm(psum[:, TAKES[n]], whi, x_lo[:, k, halves[0]], start=False, stop=False)
                    done = mm(psum[:, TAKES[n]], wlo, x_hi[:, k, halves[0]], start=False, stop=k == KT - 1)
                    if k == KT - 1:
                        done.then_inc(sem("product_full"), L.add("product_full"))

        def sample_product(slots, kts, lhs, name, bank):
            for k in range(kts):
                slot, kk = slots[k // UW], k % UW
                mm(psum[:, bank], lhs[:, k], w_hi[:, slot, kk], start=k == 0, stop=False)
                done = mm(psum[:, bank], lhs[:, k], w_lo[:, slot, kk], start=False, stop=k == kts - 1)
            done.then_inc(sem(name), L.add(name))

        def transposes(bank, pairs, began=None):
            pe.wait_ge(sem(f"bank{bank}_free"), L.next(f"bank{bank}_free"))
            at_col = 0
            for src in pairs:
                rows, cols = src.shape[0], src.shape[1]
                done = nc.tensor.transpose(psum[0:cols, bank, at_col:at_col + rows], src, ident[0:rows, 0:rows])
                if began and at_col == 0:
                    done.then_inc(sem(began), L.add(began))
                at_col += rows
            done.then_inc(sem(f"bank{bank}_full"), L.add(f"bank{bank}_full"))

        def fold_samples(bank, rows, tiles):
            pe.wait_ge(sem(f"bank{bank}_free"), L.next(f"bank{bank}_free"))
            for n in range(tiles):
                done = mm(psum[:, bank, n * NS:(n + 1) * NS], rows[:, n * P:(n + 1) * P], fold[:], start=True, stop=True)
            done.then_inc(sem(f"bank{bank}_full"), L.add(f"bank{bank}_full"))

        def norm(split=True):
            pe.wait_ge(sem("sample_squares_ready"), L.next("sample_squares_ready"))
            pe.wait_ge(sem("bank5_free"), L.next("bank5_free"))
            mm(psum[:, 5, 0:NS], ones[:], s_tmp[:, 1, 0:NS], start=True, stop=True
            ).then_inc(sem("bank5_full"), L.add("bank5_full"))
            pe.wait_ge(sem("square_free"), L.next("square_free", KT))
            pe.wait_ge(sem("bank3_free"), L.next("bank3_free"))
            for c in range(CH):
                done = mm(psum[:, 3, c:c + 1], sq_sum[:, c * P:(c + 1) * P], ones[:, 0:1], start=True, stop=True)
            done.then_inc(sem("bank3_full"), L.add("bank3_full"))
            pe.wait_ge(sem("rs_wide_ready"), L.next("rs_wide_ready"))
            for h in range(2):
                pe.wait_ge(sem(f"bank{4 - h}_free"), L.next(f"bank{4 - h}_free"))
                mm(psum[:, 4 - h], ones[:], sq[:, 0, halves[h]], start=True, stop=True
                ).then_inc(sem(f"bank{4 - h}_full"), L.add(f"bank{4 - h}_full"))

        pe.wait_ge(sem("ones_set"), L.next("ones_set"))
        pe.wait_ge(sem("constants_landed"), L.next("constants_landed", 16 * len(CONSTS)))
        def dense_quarters(first, last, slots):
            if slots is None:
                return
            for m in range(first, last):
                n, quarter = divmod(m, 4)
                tile, h = divmod(n, 2)
                if quarter == 0:
                    pe.wait_ge(sem("product_free"), L.next("product_free"))
                for k in (2 * quarter, 2 * quarter + 1):
                    slot, kk = slots[k // UW], k % UW
                    whi = w_hi[:, slot, kk, tile * P:(tile + 1) * P]
                    wlo = w_lo[:, slot, kk, tile * P:(tile + 1) * P]
                    mm(psum[:, n % 2], whi, x_hi[:, k, halves[h]], start=k == 0, stop=False)
                    mm(psum[:, n % 2], whi, x_lo[:, k, halves[h]], start=False, stop=False)
                    done = mm(psum[:, n % 2], wlo, x_hi[:, k, halves[h]], start=False, stop=k == KT - 1)
                if quarter == 3:
                    done.then_inc(sem("product_full"), L.add("product_full"))

        def samples_in(slots):
            pe.wait_ge(sem("sample_free"), L.next("sample_free"))
            sample_product(slots, KT, s_lhs, "sample_full", 2)

        pe.wait_ge(sem("w_ab_ready"), L.next("w_ab_ready"))
        pe.wait_ge(sem("x_landed"), L.next("x_landed", 16 * KT))
        for h in range(2):
            pe.wait_ge(sem(f"bank{6 + h}_free"), L.next(f"bank{6 + h}_free"))
            for k in range(KT):
                done = mm(psum[0:2 * HEADS, 6 + h], w_ab[:, k], x[:, k, halves[h]], start=k == 0, stop=k == KT - 1)
            done.then_inc(sem(f"bank{6 + h}_full"), L.add(f"bank{6 + h}_full"))
        norm()
        pe.wait_ge(sem("bank5_free"), L.next("bank5_free"))
        for k in range(KT):
            done = mm(psum[0:2 * HEADS, 5, 0:NS], w_ab[:, k], s_x[:, k], start=k == 0, stop=k == KT - 1)
        done.then_inc(sem("bank5_full"), L.add("bank5_full"))
        pe.wait_ge(sem("x_ready"), L.next("x_ready", KT))
        pe.wait_ge(sem("samples_ready"), L.next("samples_ready"))
        pe.wait_ge(sem("raw_free"), L.next("raw_free", 4))
        dense_quarters(0, 4, (0, 1))
        for bank in (6, 7):
            pe.wait_ge(sem(f"bank{bank}_free"), L.next(f"bank{bank}_free"))
            L.skip(f"bank{bank}_free", -1)
        transposes(5, [ab_feat[:, c * P:(c + 1) * P] for c in range(CH)])
        pe.wait_ge(sem("s_wide_ready"), L.next("s_wide_ready"))
        pe.wait_ge(sem("bank5_free"), L.next("bank5_free"))
        mm(psum[:, 5, 0:P], ones[0:2 * HEADS], s_wide[:].rearrange("p m n -> p (m n)"), start=True, stop=True
        ).then_inc(sem("bank5_full"), L.add("bank5_full"))
        dense_quarters(4, 8, (0, 1))
        pe.wait_ge(sem("g_ready"), L.next("g_ready"))
        pe.wait_ge(sem("bank6_free"), L.next("bank6_free"))
        mm(psum[:, 6, 0:64], tri[:], ab[:, 3, 0:64], start=True, stop=True).then_inc(sem("bank6_full"), L.add("bank6_full"))
        pe.wait_ge(sem("bank7_free"), L.next("bank7_free"))
        mm(psum[:, 7, 0:64], ones[:], ab[:, 3, 0:64], start=True, stop=True).then_inc(sem("bank7_full"), L.add("bank7_full"))

        def gdn(slots):
            pe.wait_ge(sem("sample_free"), L.next("sample_free"))
            L.skip("sample_free", -1)
            fold_samples(3, s_tok, 4)
            if slots:
                pe.wait_ge(sem("raw_free"), L.next("raw_free", 4))
            dense_quarters(0, 8, slots)
            for h in range(2):
                for b, n in ((3, 1), (4, 0), (5, 2)):
                    if h == 0 and n != 0:
                        pe.wait_ge(sem("qkv_ready"), L.next("qkv_ready", 2 if n == 1 else 1))
                    transposes(b, [qkv[:, n, (4 * h + c) * P:(4 * h + c + 1) * P] for c in range(4)])
            pe.wait_ge(sem("decay_terms_ready"), L.next("decay_terms_ready"))
            for h in range(2):
                pe.wait_ge(sem(f"bank{6 + h}_free"), L.next(f"bank{6 + h}_free"))
                mm(psum[:, 6 + h], ones[:], inv[:, hc(h)], start=True, stop=True
                ).then_inc(sem(f"bank{6 + h}_full"), L.add(f"bank{6 + h}_full"))
            for p, b in enumerate((3, 4, 5, 3)):
                if p == 3:
                    dense_quarters(8, 13, slots)
                pe.wait_ge(sem(f"bank{b}_free"), L.next(f"bank{b}_free"))
                for c in (2 * p, 2 * p + 1):
                    lo = (c % 2) * 2 * P
                    toks = slice(c * P, (c + 1) * P)
                    mm(psum[:, b, lo:lo + P], qkv[:, 1, toks], qkv[:, 1, toks], start=True, stop=True)
                    done = mm(psum[:, b, lo + P:lo + 2 * P], qkv[:, 1, toks], qkv[:, 0, toks], start=True, stop=True)
                done.then_inc(sem(f"bank{b}_full"), L.add(f"bank{b}_full"))
            dense_quarters(13, 16, slots)
            pe.wait_ge(sem("blocks_ready"), L.next("blocks_ready"))
            for h in range(2):
                transposes(6 + h, [blk[:, 4 * h + c] for c in range(4)])
            pe.wait_ge(sem("inverse_t_ready"), L.next("inverse_t_ready"))

            def four(bank, h, lhs, rhs):
                pe.wait_ge(sem(f"bank{bank}_free"), L.next(f"bank{bank}_free"))
                for c in range(4):
                    done = mm(psum[:, bank, c * P:(c + 1) * P], lhs[:, 4 * h + c], rhs[:, 4 * h + c], start=True, stop=True)
                done.then_inc(sem(f"bank{bank}_full"), L.add(f"bank{bank}_full"))
            for level in range(1, LEVELS + 1):
                pe.wait_ge(sem("blocks_ready"), L.next("blocks_ready"))
                if level == 1:
                    pe.wait_ge(sem("bank6_free"), L.next("bank6_free")), pe.wait_ge(sem("bank7_free"), L.next("bank7_free"))
                    L.skip("bank6_free", -1), L.skip("bank7_free", -1)
                for h in range(2):
                    if level > 1:
                        pe.wait_ge(sem(f"bank{5 + h}_free"), L.next(f"bank{5 + h}_free"))
                        L.skip(f"bank{5 + h}_free", -1)
                    four(3 + h, h, blk, inv)
                for h in range(2):
                    pe.wait_ge(sem(f"bank{3 + h}_free"), L.next(f"bank{3 + h}_free"))
                    L.skip(f"bank{3 + h}_free", -1)
                    if h == 0:
                        pe.wait_ge(sem("bank7_free"), L.next("bank7_free"))
                        L.skip("bank7_free", -1)
                    if level < LEVELS:
                        four(5 + h, h, inv_t, prod)
                    four((7, 3)[h], h, prod, inv_t)
                dense_quarters(15 + level, 16 + level, slots)
            for c in range(CH):
                toks = slice(c * P, (c + 1) * P)
                if c == 0:
                    pe.wait_ge(sem("state_ready"), L.next("state_ready"))
                else:
                    pe.wait_ge(sem("bank3_free"), L.next("bank3_free"))
                    L.skip("bank3_free", -1)
                for b, lhs, rhs in ((4, qkv[:, 1, toks], state[:]), (6, qkv[:, 0, toks], state[:])):
                    pe.wait_ge(sem(f"bank{b}_free"), L.next(f"bank{b}_free"))
                    mm(psum[:, b, 0:P], lhs, rhs, start=True, stop=True
                    ).then_inc(sem(f"bank{b}_full"), L.add(f"bank{b}_full"))
                if c < 6:
                    dense_quarters(22 + c, 23 + c, slots)
                pe.wait_ge(sem("bank4_free"), L.next("bank4_free"))
                L.skip("bank4_free", -1)
                pe.wait_ge(sem("bank5_free"), L.next("bank5_free"))
                mm(psum[:, 5, 0:P], inv_t[:, c], vz[:, 0], start=True, stop=True
                ).then_inc(sem("bank5_full"), L.add("bank5_full"))
                pe.wait_ge(sem("v_for_state_ready"), L.next("v_for_state_ready"))
                pe.wait_ge(sem("bank3_free"), L.next("bank3_free"))
                mm(psum[:, 3, 0:P], k_tok[:, c], vz[:, 2], start=True, stop=True
                ).then_inc(sem("bank3_full"), L.add("bank3_full"))
                pe.wait_ge(sem("bank5_free"), L.next("bank5_free"))
                L.skip("bank5_free", -1)
                pe.wait_ge(sem("bank7_free"), L.next("bank7_free"))
                mm(psum[:, 7, 0:P], att[:, c], vz[:, 1], start=True, stop=True
                ).then_inc(sem("bank7_full"), L.add("bank7_full"))
            dense_quarters(28, 32, slots)
            pe.wait_ge(sem("o_tok_ready"), L.next("o_tok_ready"))
            for h in range(2):
                transposes(4 + h, [o_tok[:, 4 * h + c] for c in range(4)])
            if slots:
                samples_in(slots)
            pe.wait_ge(sem("s_squares_ready"), L.next("s_squares_ready"))
            pe.wait_ge(sem("bank3_free"), L.next("bank3_free"))
            mm(psum[:, 3, 0:2 * NS], ones[:], s_u[:, 2:4].rearrange("p k n -> p (k n)"), start=True, stop=True
            ).then_inc(sem("bank3_full"), L.add("bank3_full"))
            pe.wait_ge(sem("s_qk_ready"), L.next("s_qk_ready"))
            pe.wait_ge(sem("s_state_landed"), L.next("s_state_landed", 16))
            pe.wait_ge(sem("bank4_free"), L.next("bank4_free"))
            for n in range(NS):
                mm(psum[:, 4, 2 * n:2 * n + 2], s_state[:, n], s_qkv[:, 0:2, n], start=True, stop=True)
            mm(psum[:, 4, 2 * NS:3 * NS], ones[:], s_u[:, 2], start=True, stop=True
            ).then_inc(sem("bank4_full"), L.add("bank4_full"))
            pe.wait_ge(sem("s_v_ready"), L.next("s_v_ready"))
            pe.wait_ge(sem("bank5_free"), L.next("bank5_free"))
            mm(psum[0:NS, 5, 0:P], s_qkv[:, 1], ident[:], start=True, stop=True)
            mm(psum[0:NS, 5, P:2 * P], s_u[:, 5], ident[:], start=True, stop=True
            ).then_inc(sem("bank5_full"), L.add("bank5_full"))
            pe.wait_ge(sem("s_v_wide_ready"), L.next("s_v_wide_ready"))
            for h in range(2):
                pe.wait_ge(sem(f"bank{6 + h}_free"), L.next(f"bank{6 + h}_free"))
                mm(psum[:, 6 + h], s_rows[0:NS, 0], s_v_wide[0:NS, hc(h)], start=True, stop=True
                ).then_inc(sem(f"bank{6 + h}_full"), L.add(f"bank{6 + h}_full"))
            pe.wait_ge(sem("s_out_squares_ready"), L.next("s_out_squares_ready"))
            pe.wait_ge(sem("bank3_free"), L.next("bank3_free"))
            mm(psum[:, 3, 0:NS], ones[:], s_u[:, 7], start=True, stop=True
            ).then_inc(sem("bank3_full"), L.add("bank3_full"))

        dense_quarters(8, 32, (0, 1))
        samples_in((0, 1))
        with L.loop(HEADS // 2 - 1, "pe heads"):
            gdn((2, 3))
            gdn((0, 1))
        gdn((2, 3))
        gdn(None)

        L.skip("product_free", -2)
        for g in range(2):
            slots = ((0, 1), (2, 3))[g]
            pe.wait_ge(sem("raw_free"), L.next("raw_free", 4))
            if g == 0:
                first_products(slots, "o_split")
            for n in range(4 if g == 0 else 0, 8):
                h, tile = divmod(n, 4)
                product(n, slots, tile, h, x_hi, x_lo, KT)
            if g == 0:
                pe.wait_ge(sem("samples_ready"), L.next("samples_ready"))
            pe.wait_ge(sem("sample_free"), L.next("sample_free"))
            sample_product(slots, KT, s_lhs, "sample_full", 2)
            pe.wait_ge(sem("sample_free"), L.next("sample_free"))
            L.skip("sample_free", -1)
            fold_samples(3, s_tok, 4)

        def mlp(name, more):
            def block(first=False):
                pe.wait_ge(sem("raw_free"), L.next("raw_free", 4))
                if first:
                    first_products((0, 1), "x_ready")
                    norm()
                    pe.wait_ge(sem("samples_ready"), L.next("samples_ready"))
                for n in range(4 if first else 0, 8):
                    h, tile = divmod(n, 4)
                    product(n, (0, 1), tile, h, x_hi, x_lo, KT)
                pe.wait_ge(sem("sample_free"), L.next("sample_free"))
                sample_product((0, 1), KT, s_lhs, "sample_full", 2)
                for j in range(2):
                    pe.wait_ge(sem("raw_free"), L.next("raw_free", 2))
                    for n in range(8):
                        h, tile = divmod(n, 4)
                        if j == 0 and n in (0, 4):
                            pe.wait_ge(sem("u_ready"), L.next("u_ready", 4))
                        product(n, (2 + j,), tile, h, u_hi, u_lo, UW)
                        if j == 0 and n == 1:
                            pe.wait_ge(sem("sample_free"), L.next("sample_free")), L.skip("sample_free", -1)
                            fold_samples(3, s_tok, 4)
                    if j == 0:
                        pe.wait_ge(sem("u_samples_ready"), L.next("u_samples_ready"))
                    pe.wait_ge(sem(f"bank{4 + j}_free"), L.next(f"bank{4 + j}_free"))
                    sample_product((2 + j,), UW, u_lhs, f"bank{4 + j}_full", 4 + j)
            block(first=True)
            with L.loop(7 if more else 6, name):
                block()
            if not more:
                block()
            for bank in (4, 5):
                pe.wait_ge(sem(f"bank{bank}_free"), L.next(f"bank{bank}_free")), L.skip(f"bank{bank}_free", -1)
            fold_samples(3, s_acc, KT)

        def attention_layer():
            for gi in range(5):
                tiles = 2 if gi == 1 else 4
                slots = ((0, 1), (2, 3))[gi % 2]
                pe.wait_ge(sem("raw_free"), L.next("raw_free", 4))
                if gi == 0:
                    first_products(slots, "x_ready")
                    norm()
                    pe.wait_ge(sem("samples_ready"), L.next("samples_ready"))
                for n in range(4 if gi == 0 else 0, 2 * tiles):
                    h, tile = divmod(n, tiles)
                    product(n, slots, tile, h, x_hi, x_lo, KT)
                pe.wait_ge(sem("sample_free"), L.next("sample_free"))
                sample_product(slots, KT, s_lhs, "sample_full", 2)
                pe.wait_ge(sem("sample_free"), L.next("sample_free")), L.skip("sample_free", -1)
                fold_samples(3, s_tok, tiles)
            pe.wait_ge(sem("kvq_done"), L.next("kvq_done"))
            for b in range(BRANCH):
                for h in range(2):
                    transposes(3 + h, [v_feat[:, b, (4 * h + c) * P:(4 * h + c + 1) * P] for c in range(4)])
            pe.wait_ge(sem("bank4_free"), L.next("bank4_free"))
            for b in range(BRANCH):
                done = mm(psum[0:NS, 4, b * P:(b + 1) * P], s_kv[:, 2 * b + 1], ident[:], start=True, stop=True)
            done.then_inc(sem("bank4_full"), L.add("bank4_full"))
            pe.wait_ge(sem("s_keys_ready"), L.next("s_keys_ready", 3))
            pe.wait_ge(sem("product_free"), L.next("product_free", 4)), L.skip("product_free", -4)
            for n in range(NS):
                k, lo = n // 2, (n % 2) * 256
                if n % 2 == 0:
                    pe.wait_ge(sem(f"bank{k}_free"), L.next(f"bank{k}_free"))
                for b, first, last in ((0, 0, SA), (1, SA, SA + 65), (2, SA + 65, SA + 82), (0, SA + 82, SK)):
                    done = mm(psum[0:8, k, lo + first:lo + last], s_qz[:, b, n], s_keys[:, n, first:last],
                              start=True, stop=True)
                if n % 2:
                    done.then_inc(sem(f"bank{k}_full"), L.add(f"bank{k}_full"))
            pe.wait_ge(sem("s_probs_ready"), L.next("s_probs_ready"))
            for bank, first, last in ((4, 0, SA), (5, SA, SK)):
                pe.wait_ge(sem("bank5_free" if bank == 5 else "s_vrow_ready"), L.next("bank5_free" if bank == 5 else "s_vrow_ready"))
                for n in range(NS):
                    done = nc.tensor.transpose(psum[0:last - first, bank, 8 * n:8 * n + 8], s_p[:, n, first:last],
                                               ident[0:8, 0:8])
                done.then_inc(sem(f"bank{bank}_full"), L.add(f"bank{bank}_full"))
            pe.wait_ge(sem("s_vown_landed"), L.next("s_vown_landed", 48))
            for bank in (4, 5):
                pe.wait_ge(sem(f"bank{bank}_free"), L.next(f"bank{bank}_free")), L.skip(f"bank{bank}_free", -1)
            pe.wait_ge(sem("bank6_free"), L.next("bank6_free"))
            for n in range(NS):
                mm(psum[:, 6, 8 * n:8 * n + 8], s_va[:, n], s_pt[:, 0, 8 * n:8 * n + 8], start=True, stop=False)
                done = mm(psum[:, 6, 8 * n:8 * n + 8], s_vb[:, n], s_pt[0:SB, 1, 8 * n:8 * n + 8], start=False, stop=True)
            done.then_inc(sem("bank6_full"), L.add("bank6_full"))

            def scores(tile_):
                b, tile, par, nk, _ = tile_
                pe.wait_ge(sem(f"q_tile{par}_landed"), L.next(f"q_tile{par}_landed", 16))
                for j in range(4):
                    pe.wait_ge(sem(f"bank{j}_free"), L.next(f"bank{j}_free"))
                    for g in range(2):
                        done = mm(psum[:, j, g * 256 + (2 - nk) * P:(g + 1) * 256], q_tile[:, par, j],
                                  k_mask[:, b, g, bass.ds((tile + 1 - nk) * P, nk * P)], start=True, stop=True)
                    done.then_inc(sem(f"bank{j}_full"), L.add(f"bank{j}_full"))

            def turn(tile_, hs):
                _, _, par, nk, _ = tile_
                pe.wait_ge(sem("probs_ready"), L.next("probs_ready", 4))
                for kt in range(2 - nk, 2):
                    transposes(4 + kt, [prob[:, par, n, kt * P:(kt + 1) * P] for n in range(4 * hs, 4 * hs + 4)],
                               "q_tile_free" if (hs, kt) == (0, 1) else None)

            def apply(tile_, hs):
                b, tile, par, nk, _ = tile_
                for kt in range(2 - nk, 2):
                    if hs == 1:
                        pe.wait_ge(sem(f"bank{4 + kt}_free"), L.next(f"bank{4 + kt}_free"))
                        L.skip(f"bank{4 + kt}_free", -1)
                free = ("bank6_free", "out_taken")[hs]
                pe.wait_ge(sem(free), L.next(free))
                for n in range(4):
                    for kt in range(2 - nk, 2):
                        done = mm(psum[:, 6 + hs, n * P:(n + 1) * P], prob_t[:, kt, 4 * hs + n],
                                  v_keys[:, b, bass.ds(tile + kt - 1, 1)].rearrange("p u n -> p (u n)"),
                                  start=kt == 2 - nk, stop=kt == 1)
                done.then_inc(sem(f"bank{6 + hs}_full"), L.add(f"bank{6 + hs}_full"))

            def step(cur, nxt):
                if cur:
                    turn(cur, 0)
                if nxt:
                    scores(nxt)
                if cur:
                    turn(cur, 1)
                    apply(cur, 0)
                    apply(cur, 1)
            tiles_of(L, "pe", step)
            with L.loop(CH // 2, "pe merge"):
                for par in range(2):
                    pe.wait_ge(sem("merged_ready"), L.next("merged_ready"))
                    transposes(4 + par, [merged[:, par, j * P:(j + 1) * P] for j in range(4)])
            for bank in (4, 5):
                pe.wait_ge(sem(f"bank{bank}_free"), L.next(f"bank{bank}_free")), L.skip(f"bank{bank}_free", -1)
            pe.wait_ge(sem("u_samples_ready"), L.next("u_samples_ready"))
            pe.wait_ge(sem("raw_free"), L.next("raw_free", 4))
            for free in ("bank0_free", "bank1_free", "bank6_free", "out_taken"):
                pe.wait_ge(sem(free), L.next(free)), L.skip(free, -1)
            for j in range(2):
                for n in range(8):
                    h, tile = divmod(n, 4)
                    product(n, (2 + j,), tile, h, u_hi, u_lo, UW)
                pe.wait_ge(sem(f"bank{4 + j}_free"), L.next(f"bank{4 + j}_free"))
                sample_product((2 + j,), UW, u_lhs, f"bank{4 + j}_full", 4 + j)
            for bank in (4, 5):
                pe.wait_ge(sem(f"bank{bank}_free"), L.next(f"bank{bank}_free")), L.skip(f"bank{bank}_free", -1)
            fold_samples(3, s_acc, KT)

        mlp("pe mlp0", True)
        attention_layer()
        mlp("pe mlp1", False)
        norm()
    ctx.close()


CONSTS = [("ident", "ident"), ("w_ab", "w_ab"), ("g_ab", "g_ab"), ("dtb", "dtb"), ("lvl", "lvl"), ("tri", "tri"),
          ("msk", "msk"), ("cw", "cw"), ("fold", "fold"), ("s_ext", "s_ext"), ("g_fin", "g_fin"), ("s_x", "xs"), ("gains", "gains")]


def pack(i):
    c = np.ascontiguousarray

    def feat(x):
        return c(x.reshape(x.shape[0], -1, P).transpose(2, 1, 0))

    def units(w):
        k, n = w.shape
        w = w.reshape(k // (UW * P), 2, 2, P, n // HALF, HALF).transpose(4, 0, 1, 3, 2, 5)
        return w.reshape(-1, P, 2, HALF)

    w_in = i["w_in_a"][0]
    heads = w_in[:, :4 * D_MODEL].reshape(D_MODEL, 4, HEADS, P).transpose(0, 2, 1, 3).reshape(D_MODEL, -1)
    up, down = i["w_up"], i["w_down"]

    def mlp(l):
        parts = []
        for b in range(D_FF // HALF):
            parts += [units(up[l][:, b * HALF:(b + 1) * HALF]), units(down[l][b * HALF:(b + 1) * HALF])]
        return parts
    q = i["w_q_b"][0].reshape(D_MODEL, BRANCH, 2, 4, HD).transpose(0, 1, 3, 2, 4).reshape(D_MODEL, -1)
    wo = i["w_o_b"][0].reshape(2, 4, HD, D_MODEL).transpose(1, 0, 2, 3).reshape(-1, D_MODEL)
    kv = np.concatenate([i["w_kv"], np.zeros((D_MODEL, 256), np.float32)], axis=1)
    w = np.concatenate([units(heads), units(i["w_out_a"][0]), *mlp(0), units(kv), units(q), units(wo), *mlp(1)])

    def rows(g):
        return g.reshape(-1, P).T
    one = np.ones((P, UW), np.float32)
    mix, nm = i["norm_mix"], i["norm_mlp"]

    def mlp_gain(l):
        return [rows(nm[l]), one, one] * (D_FF // HALF)
    go = np.repeat(i["norm_o_a"][0][:, None], KT, axis=1)
    gains = np.concatenate([rows(mix[0])] * 8 + [go] * 2 + mlp_gain(0) + [rows(i["norm_kv"])] * 2 + [rows(mix[1])] * 3
                           + [one] * 2 + mlp_gain(1), axis=1)
    j, k = np.arange(P)[:, None], np.arange(P)[None, :]
    lvl = np.zeros((P, LEVELS + 1, P), np.float32)
    for n in range(LEVELS + 1):
        b = 1 << n
        lvl[:, n] = (j // (2 * b) == k // (2 * b)) & (k // b % 2 == 1) & (j // b % 2 == 0)
    cw = i["conv_a"][0].reshape(4, 3, HEADS, P).transpose(3, 2, 1, 0)
    se = np.zeros((P, HEADS, 3, 4, NS), np.float32)
    se[:, :, :, 0:3] = i["state_a_conv"][0].reshape(NS, 3, 3, HEADS, P).transpose(4, 3, 2, 1, 0)
    slot_slope = np.array([2.0 ** -(4 * g + jj + 1) for jj in range(4) for g in range(2)], np.float32)
    dist = np.full((P, 3, P), NEG, np.float32)
    dist[:, 0] = np.where(k >= j, -(P + j - k), NEG)
    dist[:, 1] = np.where(k <= j, -(j - k), NEG)
    dist[:, 2] = np.where((k <= j) & (k // HD == j // HD), -(j - k), NEG)
    slopes = np.broadcast_to((np.array(DIL, np.float32)[:, None] * slot_slope).astype(np.float32), (P, BRANCH, 8))
    far = np.concatenate([np.arange(128, 0, -1), np.arange(256, -1, -4), np.arange(256, -1, -16), [0]])
    taken = [i[f"cache_b{b}_kv"][:, ::DIL[b]] for b in range(BRANCH)]

    def keys(kv):
        own = np.zeros((NS, 1, 2, HD), np.float32)
        parts = [x[:, :, kv] for x in taken]
        return np.concatenate([parts[0], parts[1], own, parts[2], own, own], axis=1).reshape(NS, SK, P)
    all_k, all_v = keys(0), keys(1)
    caches = [c(i[f"cache_b{b}_kv"].reshape(NS, -1, 256)) for b in range(BRANCH)]
    return {
        "dist": dist, "slopes": c(slopes), "s_bias": (-slot_slope[:, None] * far).astype(np.float32), "s_keys": c(all_k.transpose(2, 0, 1)),
        "s_va": c(all_v[:, :SA].transpose(1, 0, 2)), "s_vb": c(all_v[:, SA:].transpose(1, 0, 2)),
        "cache0": c(caches[0][:, 1:]), "cache1": caches[1], "cache2": caches[2], "g_fin": c(rows(i["norm_final"])),
        "s_ext": se, "s_rec_in": c(i["state_a_rec"][0].transpose(2, 1, 0, 3)),
        "x": feat(i["x_prompt"][0]), "xs": feat(i["x_sample"][:, 0]), "w": c(w), "gains": c(gains),
        "w_ab": c(w_in[:, 4 * D_MODEL:].reshape(KT, P, 2 * HEADS).transpose(1, 0, 2)), "g_ab": c(rows(mix[0])),
        "dtb": c(np.broadcast_to(np.stack([i["a_log"][0], i["dt_bias"][0]]), (P, 2, HEADS))),
        "cw": c(cw.reshape(P, -1)),
        "fold": np.tile(np.eye(NS, dtype=np.float32), (2, 1)), "ident": np.eye(P, dtype=np.float32), "lvl": lvl, "tri": (j <= k).astype(np.float32),
        "msk": np.where(j <= k, 0, NEG).astype(np.float32),
    }


def declare(nc, arrays):
    t = {n: nc.dram_tensor(f"in_{n}", a.shape, mybir.dt.from_np(a.dtype), kind="ExternalInput").ap() for n, a in arrays.items()}
    t["w"] = t["w"].rearrange("u p k n -> p u k n")
    for n, shape in OUTS.items():
        t[n] = nc.dram_tensor(f"out_{n}", shape, F32, kind="ExternalOutput").ap()
    for n, shape in SCRATCH.items():
        t[n] = nc.dram_tensor(f"scratch_{n}", shape, F32, kind="Internal").ap()
    return t


OUTS = {
    "y": (P, KT, SEQ), "s_y": (P, KT, NS), "p_conv": (P, 3 * HEADS, 3), "p_rec": (P, HEADS, P),
    "s_rec": (P, HEADS, NS, P), "s_conv": (P, 3 * HEADS, 3, NS),
    "p_k": (P, BRANCH, SEQ), "p_v": (P, BRANCH, SEQ), "s_kv_new": (P, 2 * BRANCH, NS),
    "s_kv0_old": (NS, 127, 256), "s_kv1_old": (NS, 256, 256), "s_kv2_old": (NS, 256, 256),
}
SCRATCH = {"q": (P, 4 * BRANCH, SEQ), "att": (SEQ, BRANCH, OW), "s_vnew": (NS, BRANCH, P), "o_heads": (P, HEADS, SEQ)}


def unpack(o):
    def tokens(x):
        return x.transpose(2, 1, 0).reshape(x.shape[2], -1)

    def window(b):
        both = [o[name][:, b].reshape(P, DIL[b], SEQ // DIL[b]).transpose(2, 1, 0).reshape(SEQ, P) for name in ("p_k", "p_v")]
        return np.stack(both, axis=1)[-min(DIL[b] * P, SEQ):].reshape(1, -1, 2, 2, HD)

    def cache(b):
        new = o["s_kv_new"][:, 2 * b:2 * b + 2].transpose(2, 1, 0).reshape(NS, 1, 2 * P)
        return np.concatenate([o[f"s_kv{b}_old"], new], axis=1).reshape(NS, -1, 2, 2, HD)
    return (
        tokens(o["y"])[None], tokens(o["s_y"])[:, None],
        o["p_rec"].transpose(1, 0, 2)[None, None],
        o["p_conv"].reshape(P, HEADS, 3, 3).transpose(3, 2, 1, 0).reshape(1, 1, 3, -1),
        window(0), window(1), window(2),
        o["s_rec"].transpose(2, 1, 0, 3)[None],
        o["s_conv"].reshape(P, HEADS, 3, 3, NS).transpose(4, 3, 2, 1, 0).reshape(1, NS, 3, -1),
        cache(0), cache(1), cache(2),
    )


def kernel(**inputs):
    import concourse.bacc as _bacc
    from concourse.bass_utils import run_bass_kernel_spmd as _run

    arrays = pack({name: np.asarray(a) for name, a in inputs.items()})
    nc = _bacc.Bacc("TRN2", target_bir_lowering=False, num_devices=1, dynamic_dma_scratch_size=1024)
    build(nc, declare(nc, arrays))
    result = _run(nc, [{f"in_{name}": a for name, a in arrays.items()}], core_ids=[0]).results[0]
    return unpack({name: result[f"out_{name}"] for name in OUTS})
```
